# Optimizing a Trainium2 kernel written in Bass

```python
import numpy as np
import jax
import jax.numpy as jnp
from jax import lax

D_MODEL = 2048
BATCH = 1
SEQ = 512
DEPTH = 1

HEAD_DIM = 128
N_MIX_HEADS = D_MODEL // HEAD_DIM
FOX_HEADS = N_MIX_HEADS // 2
NSA_HEADS = N_MIX_HEADS - FOX_HEADS
NSA_KV_HEADS = 2
NSA_GROUP = NSA_HEADS // NSA_KV_HEADS
N_BRANCH = 3
D_FF = 4 * D_MODEL
ROPE_THETA = 10000.0
Q_BLOCK = 128
CMP_LEN = 32
CMP_STRIDE = 16
CMP_HIDDEN = 2 * HEAD_DIM
SEL_BLOCK = 64
SEL_TOPK = 16
WINDOW = 512
NORM_EPS = 1e-6
ATTN_SCALE = HEAD_DIM ** -0.5
FOX_W = FOX_HEADS * HEAD_DIM
NSA_W = NSA_HEADS * HEAD_DIM
KV_W = NSA_KV_HEADS * HEAD_DIM
IN_SIZES = (FOX_W, FOX_W, FOX_W, FOX_HEADS, NSA_W, KV_W, KV_W, KV_W, KV_W, KV_W, KV_W, N_BRANCH * NSA_HEADS)
D_IN = 3 * FOX_W + FOX_HEADS + NSA_W + 6 * KV_W + N_BRANCH * NSA_HEADS

kernel_name = 'hybrid_fox_nsa_block'

def _rms_norm(x, gain):
    xf = x.astype(jnp.float32)
    y = xf * lax.rsqrt(jnp.mean(xf * xf, axis=-1, keepdims=True) + NORM_EPS)
    return (y * gain.astype(jnp.float32)).astype(x.dtype)

def _modulate(h, shift, scale):
    return h * (1.0 + scale[:, None, :]) + shift[:, None, :]

def _heads(a, n):
    return a.reshape(a.shape[0], a.shape[1], n, HEAD_DIM)

def _rope(x, pos):
    half = HEAD_DIM // 2
    inv_freq = ROPE_THETA ** (-jnp.arange(half, dtype=jnp.float32) / half)
    ang = pos.astype(jnp.float32)[:, None] * inv_freq[None, :]
    cos = jnp.cos(ang)[None, :, None, :]
    sin = jnp.sin(ang)[None, :, None, :]
    xf = x.astype(jnp.float32)
    x1, x2 = xf[..., :half], xf[..., half:]
    return jnp.concatenate([x1 * cos - x2 * sin, x2 * cos + x1 * sin], axis=-1).astype(x.dtype)

def _masked_softmax(s, mask):
    s = jnp.where(mask, s, -jnp.inf)
    m = jnp.max(s, axis=-1, keepdims=True)
    m = jnp.where(jnp.isfinite(m), m, 0.0)
    e = jnp.exp(s - m)
    return e / jnp.maximum(jnp.sum(e, axis=-1, keepdims=True), 1e-30)

def _fox_attention(q, k, v, log_f):
    B, T, H, D = q.shape
    nb = T // Q_BLOCK
    cum = jnp.cumsum(log_f, axis=1)
    q_blocks = q.reshape(B, nb, Q_BLOCK, H, D).transpose(1, 0, 3, 2, 4)
    c_blocks = cum.reshape(B, nb, Q_BLOCK, H).transpose(1, 0, 3, 2)
    k_t = k.transpose(0, 2, 1, 3)
    v_t = v.transpose(0, 2, 1, 3)
    c_k = cum.transpose(0, 2, 1)
    k_pos = jnp.arange(T)

    def block(args):
        q_i, c_i, i = args
        q_pos = i * Q_BLOCK + jnp.arange(Q_BLOCK)
        s = jnp.einsum('bhqd,bhkd->bhqk', q_i, k_t).astype(jnp.float32) * ATTN_SCALE
        s = s + (c_i[..., :, None] - c_k[:, :, None, :])
        p = _masked_softmax(s, k_pos[None, :] <= q_pos[:, None])
        return jnp.einsum('bhqk,bhkd->bhqd', p.astype(v_t.dtype), v_t)

    o = lax.map(block, (q_blocks, c_blocks, jnp.arange(nb)))
    return o.transpose(1, 0, 3, 2, 4).reshape(B, T, H * D)

def _compress(x, pe, w1, w2):
    B, T, G, D = x.shape
    n_cmp = (T - CMP_LEN) // CMP_STRIDE + 1
    idx = np.arange(n_cmp)[:, None] * CMP_STRIDE + np.arange(CMP_LEN)[None, :]
    xb = x[:, idx] + pe[None, None, :, None, :]
    xb = xb.transpose(0, 1, 3, 2, 4).reshape(B, n_cmp, G, CMP_LEN * D)
    return jax.nn.silu(xb @ w1) @ w2

def _nsa_attention(q, k_cmp, v_cmp, k_slc, v_slc, k_win, v_win, gates):
    B, T, H, D = q.shape
    G, hg = NSA_KV_HEADS, NSA_GROUP
    nb = T // Q_BLOCK
    t_pos = jnp.arange(T)
    n_cmp = k_cmp.shape[1]

    q_g = q.reshape(B, T, G, hg, D)
    s = jnp.einsum('btghd,bngd->bghtn', q_g, k_cmp).astype(jnp.float32) * ATTN_SCALE
    cmp_end = jnp.arange(n_cmp) * CMP_STRIDE + CMP_LEN - 1
    p_cmp = _masked_softmax(s, cmp_end[None, :] <= t_pos[:, None])
    o_cmp = jnp.einsum('bghtn,bngd->btghd', p_cmp.astype(v_cmp.dtype), v_cmp)

    n_sel = T // SEL_BLOCK
    c0 = np.arange(n_cmp) * CMP_STRIDE
    s0 = np.arange(n_sel) * SEL_BLOCK
    overlap = np.clip(np.minimum(c0[:, None] + CMP_LEN, s0[None, :] + SEL_BLOCK)
                      - np.maximum(c0[:, None], s0[None, :]), 0, None).astype(np.float32) / CMP_LEN
    imp = jnp.einsum('bghtn,nj->bgtj', p_cmp, jnp.asarray(overlap))
    q_blk = t_pos // SEL_BLOCK
    blk = jnp.arange(n_sel)
    causal = blk[None, :] <= q_blk[:, None]
    forced = (blk[None, :] == 0) | (blk[None, :] == q_blk[:, None]) | (blk[None, :] == q_blk[:, None] - 1)
    imp = jnp.where(forced, jnp.inf, jnp.where(causal, imp, -jnp.inf))
    n_top = min(SEL_TOPK, n_sel)
    _, sel_idx = lax.top_k(imp, n_top)

    q_r = _rope(q, t_pos).reshape(B, T, G, hg, D)
    k_s = k_slc.reshape(B, n_sel, SEL_BLOCK, G, D).transpose(0, 3, 1, 2, 4)
    v_s = v_slc.reshape(B, n_sel, SEL_BLOCK, G, D).transpose(0, 3, 1, 2, 4)
    q_blocks = q_r.reshape(B, nb, Q_BLOCK, G, hg, D).transpose(1, 0, 2, 3, 4, 5)
    i_blocks = sel_idx.reshape(B, G, nb, Q_BLOCK, n_top).transpose(2, 0, 1, 3, 4)
    b_ix = jnp.arange(B)[:, None, None, None]
    g_ix = jnp.arange(G)[None, :, None, None]
    m_keys = n_top * SEL_BLOCK

    def sel_block(args):
        q_i, idx_i, i = args
        q_pos = i * Q_BLOCK + jnp.arange(Q_BLOCK)
        k_g = k_s[b_ix, g_ix, idx_i].reshape(B, G, Q_BLOCK, m_keys, D)
        v_g = v_s[b_ix, g_ix, idx_i].reshape(B, G, Q_BLOCK, m_keys, D)
        k_pos = (idx_i[..., None] * SEL_BLOCK + jnp.arange(SEL_BLOCK)).reshape(B, G, Q_BLOCK, m_keys)
        mask = (k_pos <= q_pos[None, None, :, None])[:, :, None]
        s_i = jnp.einsum('bqghd,bgqmd->bghqm', q_i, k_g).astype(jnp.float32) * ATTN_SCALE
        p = _masked_softmax(s_i, mask)
        return jnp.einsum('bghqm,bgqmd->bqghd', p.astype(v_g.dtype), v_g)

    o_slc = lax.map(sel_block, (q_blocks, i_blocks, jnp.arange(nb)))
    o_slc = o_slc.transpose(1, 0, 2, 3, 4, 5).reshape(B, T, G, hg, D)

    k_wp = jnp.pad(k_win, ((0, 0), (WINDOW, 0), (0, 0), (0, 0)))
    v_wp = jnp.pad(v_win, ((0, 0), (WINDOW, 0), (0, 0), (0, 0)))

    def win_block(args):
        q_i, i = args
        start = i * Q_BLOCK
        k_b = lax.dynamic_slice_in_dim(k_wp, start, Q_BLOCK + WINDOW, axis=1)
        v_b = lax.dynamic_slice_in_dim(v_wp, start, Q_BLOCK + WINDOW, axis=1)
        q_pos = start + jnp.arange(Q_BLOCK)
        k_pos = start - WINDOW + jnp.arange(Q_BLOCK + WINDOW)
        diff = q_pos[:, None] - k_pos[None, :]
        mask = (k_pos[None, :] >= 0) & (diff >= 0) & (diff < WINDOW)
        s_i = jnp.einsum('bqghd,bkgd->bghqk', q_i, k_b).astype(jnp.float32) * ATTN_SCALE
        p = _masked_softmax(s_i, mask)
        return jnp.einsum('bghqk,bkgd->bqghd', p.astype(v_b.dtype), v_b)

    o_win = lax.map(win_block, (q_blocks, jnp.arange(nb)))
    o_win = o_win.transpose(1, 0, 2, 3, 4, 5).reshape(B, T, G, hg, D)

    g = gates.reshape(B, T, G, hg, N_BRANCH)
    o = g[..., 0:1] * o_cmp + g[..., 1:2] * o_slc + g[..., 2:3] * o_win
    return o.reshape(B, T, H * D)

def setup_inputs(seed: int = 0) -> dict:
    key = jax.random.key(seed)
    ks = jax.random.split(key, 24)
    L = DEPTH
    f32 = jnp.float32

    def nrm(k, shape, scale):
        return jax.random.normal(k, shape, f32) * scale

    return {
        'x': nrm(ks[0], (BATCH, SEQ, D_MODEL), 1.0),
        'c': nrm(ks[1], (BATCH, D_MODEL), 1.0),
        'w_ada': nrm(ks[2], (L, D_MODEL, 6 * D_MODEL), D_MODEL ** -0.5),
        'b_ada': nrm(ks[3], (L, 6 * D_MODEL), 0.02),
        'norm1_g': 1.0 + nrm(ks[4], (L, D_MODEL), 0.05),
        'w_in': nrm(ks[5], (L, D_MODEL, D_IN), D_MODEL ** -0.5),
        'b_forget': jax.random.uniform(ks[6], (L, FOX_HEADS), f32, 1.0, 4.0),
        'fox_q_norm': 1.0 + nrm(ks[7], (L, HEAD_DIM), 0.05),
        'fox_k_norm': 1.0 + nrm(ks[8], (L, HEAD_DIM), 0.05),
        'nsa_q_norm': 1.0 + nrm(ks[9], (L, HEAD_DIM), 0.05),
        'cmp_k_norm': 1.0 + nrm(ks[10], (L, HEAD_DIM), 0.05),
        'slc_k_norm': 1.0 + nrm(ks[11], (L, HEAD_DIM), 0.05),
        'win_k_norm': 1.0 + nrm(ks[12], (L, HEAD_DIM), 0.05),
        'cmp_pe_k': nrm(ks[13], (L, CMP_LEN, HEAD_DIM), 0.2),
        'cmp_w1_k': nrm(ks[14], (L, CMP_LEN * HEAD_DIM, CMP_HIDDEN), (CMP_LEN * HEAD_DIM) ** -0.5),
        'cmp_w2_k': nrm(ks[15], (L, CMP_HIDDEN, HEAD_DIM), CMP_HIDDEN ** -0.5),
        'cmp_pe_v': nrm(ks[16], (L, CMP_LEN, HEAD_DIM), 0.2),
        'cmp_w1_v': nrm(ks[17], (L, CMP_LEN * HEAD_DIM, CMP_HIDDEN), (CMP_LEN * HEAD_DIM) ** -0.5),
        'cmp_w2_v': nrm(ks[18], (L, CMP_HIDDEN, HEAD_DIM), CMP_HIDDEN ** -0.5),
        'w_out': nrm(ks[19], (L, D_MODEL, D_MODEL), D_MODEL ** -0.5),
        'norm2_g': 1.0 + nrm(ks[20], (L, D_MODEL), 0.05),
        'w_up': nrm(ks[21], (L, D_MODEL, D_FF), D_MODEL ** -0.5),
        'w_down': nrm(ks[22], (L, D_FF, D_MODEL), D_FF ** -0.5),
    }

def reference(x, c, w_ada, b_ada, norm1_g, w_in, b_forget, fox_q_norm, fox_k_norm, nsa_q_norm,
              cmp_k_norm, slc_k_norm, win_k_norm, cmp_pe_k, cmp_w1_k, cmp_w2_k, cmp_pe_v, cmp_w1_v,
              cmp_w2_v, w_out, norm2_g, w_up, w_down):
    B, T, _ = x.shape
    t_pos = jnp.arange(T)
    split_at = np.cumsum(IN_SIZES)[:-1].tolist()
    c_act = jax.nn.silu(c)
    for l in range(DEPTH):
        mod = c_act @ w_ada[l] + b_ada[l]
        shift1, scale1, gate1, shift2, scale2, gate2 = jnp.split(mod, 6, axis=-1)

        h = _modulate(_rms_norm(x, norm1_g[l]), shift1, scale1)
        proj = h @ w_in[l]
        fq, fk, fv, fz, nq, kc, vc, ksl, vsl, kw, vw, gz = jnp.split(proj, split_at, axis=-1)

        fq = _rms_norm(_heads(fq, FOX_HEADS), fox_q_norm[l])
        fk = _rms_norm(_heads(fk, FOX_HEADS), fox_k_norm[l])
        log_f = jax.nn.log_sigmoid(fz.astype(jnp.float32) + b_forget[l].astype(jnp.float32))
        o_fox = _fox_attention(fq, fk, _heads(fv, FOX_HEADS), log_f)

        nq = _rms_norm(_heads(nq, NSA_HEADS), nsa_q_norm[l])
        k_cmp = _rms_norm(_compress(_heads(kc, NSA_KV_HEADS), cmp_pe_k[l], cmp_w1_k[l], cmp_w2_k[l]), cmp_k_norm[l])
        v_cmp = _compress(_heads(vc, NSA_KV_HEADS), cmp_pe_v[l], cmp_w1_v[l], cmp_w2_v[l])
        k_slc = _rope(_rms_norm(_heads(ksl, NSA_KV_HEADS), slc_k_norm[l]), t_pos)
        k_win = _rope(_rms_norm(_heads(kw, NSA_KV_HEADS), win_k_norm[l]), t_pos)
        gates = jax.nn.sigmoid(gz).reshape(B, T, NSA_HEADS, N_BRANCH)
        o_nsa = _nsa_attention(nq, k_cmp, v_cmp, k_slc, _heads(vsl, NSA_KV_HEADS),
                               k_win, _heads(vw, NSA_KV_HEADS), gates)

        mix = jnp.concatenate([o_fox, o_nsa], axis=-1) @ w_out[l]
        x = x + gate1[:, None, :] * mix

        h = _modulate(_rms_norm(x, norm2_g[l]), shift2, scale2)
        x = x + gate2[:, None, :] * (jnp.square(jax.nn.relu(h @ w_up[l])) @ w_down[l])
    return x


_drawn_inputs = setup_inputs


def setup_inputs(seed=0):
    import zlib

    import numpy as np

    out = dict(_drawn_inputs(seed))
    spreads = {}
    factors = {'norm1_g': 4.072,
     'fox_q_norm': 8.0,
     'fox_k_norm': 8.0,
     'nsa_q_norm': 8.0,
     'cmp_k_norm': 8.0,
     'slc_k_norm': 8.0,
     'win_k_norm': 8.0,
     'cmp_pe_k': 8.0,
     'cmp_pe_v': 4.72,
     'norm2_g': 2.743}
    for name, (base, spread) in spreads.items():
        noise = np.random.default_rng([zlib.crc32(name.encode()), seed]).standard_normal(out[name].shape)
        drawn = base * np.exp(spread * noise) if base else spread * noise
        out[name] = jnp.asarray(drawn.astype(out[name].dtype))
    for name, factor in factors.items():
        out[name] = (out[name] * factor).astype(out[name].dtype)
    return out
```

```python
from collections import namedtuple
from contextlib import ExitStack

import numpy as np

import concourse.bass as bass
from concourse import mybir

F32 = mybir.dt.float32
F32R = mybir.dt.float32r
ALU = mybir.AluOpType
ACT = mybir.ActivationFunctionType
AX = mybir.AxisListType
ds = bass.ds


class Names:
    pass

P = 128
T = 512
TM = T // P
D = 2048
KT = D // P
HD = 128
FOX = 8
NSA = 8
NG = 2
FF = 4 * D
CMP_LEN, CMP_STRIDE = 32, 16
NCMP = (T - CMP_LEN) // CMP_STRIDE + 1
CW = 32
CMP_HID = 2 * HD
NB_IN = 11
FOX_COLS = 3 * FOX * HD
FZ = FOX_COLS
GZ = FZ + FOX + 5 * 512
NZ = 40
EPS = 1e-6
SCALE = HD ** -0.5
NEG = -1e30

C_ID, C_CAUSAL, C_FLAG, C_NFLAG, C_M1, C_M2, C_N1, C_N2, C_END = 0, 128, 256, 300, 344, 352, 360, 361, 362
N_MASK, N_COS, N_SIN, N_END = 0, 512, 1024, 1536

PAIR_IN = 0
PAIR_CMP = 2 * NB_IN
PAIR_OUT = PAIR_CMP + 4
PAIR_FF = PAIR_OUT + 8
CHUNKS = 8
PAIR_END = PAIR_FF + 8 * CHUNKS
ROUND_IN = KT // 4
ROUND_OUT = ROUND_IN + NB_IN
ROUND_NORM2 = ROUND_OUT + 4
ROUND_FF = ROUND_NORM2 + KT // 4


def host_constants():
    p = np.arange(P)[:, None]
    base = np.zeros((P, C_END), np.float32)
    base[:, C_ID:C_ID + P] = np.eye(P)
    base[:, C_CAUSAL:C_CAUSAL + P] = np.where(np.arange(P)[None, :] <= p, 0.0, NEG)
    flag = np.zeros((NB_IN, 4), np.float32)
    flag[[0, 1, 2, 3, 6, 7]] = 1.0
    flag[9:11, 0:2] = 1.0
    base[:, C_FLAG:C_FLAG + 44] = flag.reshape(1, 44)
    base[:, C_NFLAG:C_NFLAG + 44] = 1.0 - flag.reshape(1, 44)
    h = np.arange(FOX)[None, :]
    base[:, C_M1:C_M1 + FOX] = p == h
    base[:, C_M2:C_M2 + FOX] = -1.0 * (p == 32 + h)
    base[:, C_N1] = p[:, 0] >= 32
    base[:, C_N2] = p[:, 0] < FOX

    nsa = np.zeros((P, N_END), np.float32)
    m = np.arange(TM)[None, :, None]
    n = np.arange(NG * CW)[None, None, :]
    t = m * P + p[:, :, None]
    for g in range(NG):
        see = (n // CW == g) & (n % CW < NCMP) & ((n % CW) * CMP_STRIDE + CMP_LEN - 1 <= t)
        nsa[:, N_MASK + g * 256:N_MASK + (g + 1) * 256] = see.reshape(P, 256)
    half = HD // 2
    inv = np.float32(10000.0) ** (-np.arange(half, dtype=np.float32) / np.float32(half))
    ang = (np.arange(T, dtype=np.float32)[:, None] * inv[None, :]).astype(np.float32)
    cos, sin = np.cos(ang), np.sin(ang)
    cos2 = np.concatenate([cos, cos], 1).reshape(TM, P, HD).transpose(1, 0, 2)
    sin2 = np.concatenate([-sin, sin], 1).reshape(TM, P, HD).transpose(1, 0, 2)
    nsa[:, N_COS:N_COS + 512] = cos2.reshape(P, 512)
    nsa[:, N_SIN:N_SIN + 512] = sin2.reshape(P, 512)
    return base, nsa



def load_unit(sp, s, pair, slot, src, first=False):
    if not first:
        sp.wait_ge(s.w_lo_ready, 2 * pair + slot - 1)
    sp.dma_start(s.w_raw[:, slot], src).then_inc(s.w_landed[slot], 16)


def split_hi(nc, act, s, pair, slot, first=False):
    act.wait_ge(s.w_landed[slot], 16 * (pair + 1))
    if not first:
        act.wait_ge(s.unit_used, 2 * pair + slot - 1)
    nc.scalar.activation(s.w_hi[:, slot], s.w_raw[:, slot], ACT.Copy).then_inc(s.w_hi_ready, 1)


def split_lo(nc, dve, s, pair, slot):
    dve.wait_ge(s.w_hi_ready, 2 * pair + slot + 1)
    nc.vector.tensor_tensor(s.w_lo[:, slot], s.w_raw[:, slot], s.w_hi[:, slot].bitcast(F32),
                            ALU.subtract).then_inc(s.w_lo_ready, 1)


def await_bank(eng, s, product_round, m, last_unit):
    if m < 3:
        eng.wait_ge(s.bank_done, 3 * product_round + m + 1)
    else:
        eng.wait_ge(s.unit_used, last_unit + 1)


def three_products(nc, out, a_hi, a_lo, b_hi, b_lo, start, stop):
    nc.tensor.matmul(out, a_hi, b_hi, start=start, stop=False)
    nc.tensor.matmul(out, a_hi, b_lo, start=False, stop=False)
    return nc.tensor.matmul(out, a_lo, b_hi, start=False, stop=stop)


def rows_unit(nc, pe, s, pair, slot, lhs_hi, lhs_lo, k0, first, last, round_):
    pe.wait_ge(s.w_lo_ready, 2 * pair + slot + 1)
    for m in range(TM):
        if first:
            pe.wait_ge(s.bank_free, 4 * round_ + m - 3)
        for kk in range(4):
            tok = slice(m * P, (m + 1) * P)
            mm = three_products(nc, s.gb[m][:, :], lhs_hi[:, k0 + kk, tok], lhs_lo[:, k0 + kk, tok],
                                s.w_hi[:, slot, kk, :], s.w_lo[:, slot, kk, :],
                                first and kk == 0, last and kk == 3)
        if last and m < 3:
            mm.then_inc(s.bank_done, 1)
    mm.then_inc(s.unit_used, 1)


def cols_unit(nc, pe, s, pair, slot, k0, first, last, round_):
    pe.wait_ge(s.w_lo_ready, 2 * pair + slot + 1)
    for m in range(4):
        if first:
            pe.wait_ge(s.bank_free, 4 * round_ + m - 3)
        for kk in range(4):
            col = slice(m * P, (m + 1) * P)
            mm = three_products(nc, s.gb[m][:, :], s.w_hi[:, slot, kk, col], s.w_lo[:, slot, kk, col],
                                s.act_hi[:, k0 + kk, :], s.act_lo[:, k0 + kk, :],
                                first and kk == 0, last and kk == 3)
        if last and m < 3:
            mm.then_inc(s.bank_done, 1)
    mm.then_inc(s.unit_used, 1)



def modulated_tensor(nc, pe, s, xn, round0, turned):
    for k in range(KT):
        turn = 4 * round0 + k
        if turn >= 4:
            pe.wait_ge(s.bank_free, turn - 3)
        for m in range(TM):
            mm = nc.tensor.transpose(s.gb[k % 4][:, m * P:(m + 1) * P], xn[:, m, k * P:(k + 1) * P], s.ident)
        mm.then_inc(turned, 1)


def modulated_vector(nc, dve, s, tmp, a, b, round0, turned, h_hi, h_lo):
    with dve.Fori(0, KT // 4) as i:
        for c in range(0, 4, 2):
            for e in (c, c + 1):
                dve.wait_ge(turned, 4 * i + e + 1)
                nc.vector.tensor_scalar(tmp[:, e, :], s.gb[e][:, :], a[:, ds(4 * i + e, 1)],
                                        b[:, ds(4 * i + e, 1)], ALU.mult, ALU.add).then_inc(s.bank_free, 1)
            for e in (c, c + 1):
                dve.wait_ge(h_hi, 4 * i + e + 1)
                nc.vector.tensor_tensor(s.act_lo[:, ds(4 * i + e, 1), :].rearrange("p o t -> p (o t)"),
                                        tmp[:, e, :],
                                        s.act_hi[:, ds(4 * i + e, 1), :].rearrange("p o t -> p (o t)").bitcast(F32),
                                        ALU.subtract).then_inc(h_lo, 1)


def modulated_scalar(nc, act, s, tmp, round0, h_hi):
    with act.Fori(0, KT // 4) as i:
        for e in range(4):
            act.wait_ge(s.bank_free, 4 * (round0 + i) + e + 1)
            nc.scalar.activation(s.act_hi[:, ds(4 * i + e, 1), :].rearrange("p o t -> p (o t)"), tmp[:, e, :],
                                 ACT.Copy).then_inc(h_hi, 1)


def w_in_unit(A, block, u):
    w = A.w_in.rearrange("l (k p) n -> p (l k) n", p=P)
    return w[:, 4 * u:4 * u + 4, ds(block, 512)]


def w_cmp_unit(w1, u):
    return w1.rearrange("l (k p) n -> p (l k) n", p=P)[:, 8 * u:8 * u + 8, :].rearrange(
        "p (a b) n -> p a b n", b=2)


def w_out_unit(A, n, u):
    return A.w_out.rearrange("l (k p) n -> p (l k) n", p=P)[:, 4 * u:4 * u + 4, ds(n * 512, 512)]


def w_up_unit(A, block, u):
    return A.w_up.rearrange("l (k p) n -> p (l k) n", p=P)[:, 4 * u:4 * u + 4, ds(block * 512, 512)]


def w_down_unit(A, chunk, n, u):
    w = A.w_down.rearrange("l (k p) n -> p (l k) n", p=P)
    return w[:, ds(chunk * 8 + 4 * u, 4), ds(n * 512, 512)]



def phase_norm1(nc, A, s):
    with ExitStack() as ctx:
        sb = lambda name, shape, dt=F32: ctx.enter_context(nc.sbuf_tensor(name, shape, dt))
        sem = s.sem
        xn = sb("xn", [P, TM, D])
        ada_raw = sb("ada1_raw", [P, 3, D])
        acc = sb("ada1_acc", [P, 2, D])
        junk = sb("square_out", [P, D])
        tmp = junk[:, :].rearrange("p (e t) -> p e t", e=4)
        rows = sb("vector_rows", [P, 2, P])
        ssq = sb("ssq1", [P, 4 * TM])

        consts_in, rows_in = sem("consts_in"), sem("rows_in")
        gains_in = sem("gains_in")
        x_in = [sem(f"x_in{m}") for m in range(TM)]
        ada_in = [sem(f"ada1_in{i}") for i in range(3)]
        ada_used, acc_zero, rows_zero = sem("ada1_used"), sem("acc1_zero"), sem("rows_zero")
        cols_done, cols_read, c_exp, c_ready = sem("cols_done"), sem("cols_read"), sem("c_exp"), sem("c_ready")
        sq_done, ms_ready, rms_ready, rstd_ready = sem("sq1"), sem("ms1"), sem("rms1"), sem("rstd1")
        xn_ready, mod_sums, mod_ready = sem("xn1_ready"), sem("mod1_sums"), sem("mod1_ready")
        ones_set, scaled = sem("ones_set"), sem("gain_scaled")
        h_turned, h_hi, h_lo = sem("h1_turned"), sem("h1_hi"), sem("h1_lo")
        NADA = 2 * KT
        ada = A.w_ada.rearrange("l (k p) n -> p (l k) n", p=P)

        block = ctx.enter_context(nc.Block())

        @block.sync
        def _(sp):
            sp.dma_start(s.base[:, :], A.base).then_inc(consts_in, 16)
            sp.dma_start(rows[0:96, 0, :], A.b_ada.rearrange("l (r c) -> (l r) c", c=P)).then_inc(rows_in, 16)
            sp.dma_start(rows[96:112, 0, :], A.norm1_g.rearrange("l (r c) -> (l r) c", c=P)).then_inc(rows_in, 16)
            sp.dma_start(rows[112:128, 0, :], A.norm2_g.rearrange("l (r c) -> (l r) c", c=P)).then_inc(rows_in, 16)
            sp.wait_ge(rows_zero, 1)
            sp.dma_start(rows[0:16, 1, :], A.c.rearrange("l (r c) -> (l r) c", c=P)).then_inc(rows_in, 16)
            for r, v in enumerate((A.fox_q_norm, A.fox_k_norm, A.nsa_q_norm, A.cmp_k_norm)):
                sp.dma_start(rows[16 + r:17 + r, 1, :], v).then_inc(rows_in, 16)
            sp.dma_start(rows[22:54, 1, :], A.cmp_pe_k.rearrange("l r c -> (l r) c")).then_inc(rows_in, 16)
            sp.dma_start(rows[54:86, 1, :], A.cmp_pe_v.rearrange("l r c -> (l r) c")).then_inc(rows_in, 16)
            for m in range(TM):
                sp.dma_start(xn[:, m, :], A.x[0, m * P:(m + 1) * P, :]).then_inc(x_in[m], 16)
            for j in range(3):
                sp.dma_start(ada_raw[:, j, :], ada[:, j // 2, (j % 2) * D:(j % 2 + 1) * D]).then_inc(ada_in[j], 16)
            for r, v in enumerate((A.nsa_q_norm, A.slc_k_norm, A.win_k_norm)):
                sp.dma_start(s.gain_bc[:, r, :], v[0, :].partition_broadcast(P)).then_inc(gains_in, 16)
            with sp.Fori(1, NADA // 3) as i:
                for e in range(3):
                    j = 3 * i + e
                    sp.wait_ge(ada_used, j - 2)
                    sp.dma_start(ada_raw[:, e, :], ada[:, ds(j // 2, 1), ds((j % 2) * D, D)].rearrange(
                        "p o n -> p (o n)")).then_inc(ada_in[e], 16)
            for j in range(NADA // 3 * 3, NADA):
                sp.wait_ge(ada_used, j - 2)
                sp.dma_start(ada_raw[:, j % 3, :], ada[:, j // 2, (j % 2) * D:(j % 2 + 1) * D]).then_inc(ada_in[j % 3], 16)
            for u in range(4):
                load_unit(sp, s, u // 2, u % 2, w_in_unit(A, 0, u), first=u < 2)

        @block.gpsimd
        def _(pool):
            nc.gpsimd.memset(rows[:, 1, :], 0.0).then_inc(rows_zero, 1)
            nc.gpsimd.memset(acc[:, :, :], 0.0).then_inc(acc_zero, 1)
            nc.gpsimd.memset(s.ones[:, :], 1.0).then_inc(ones_set, 1)

        @block.scalar
        def _(act):
            act.wait_ge(cols_done, 1)
            nc.scalar.activation(s.cols1[:, :], s.mb[0][:, 0:P], ACT.Copy).then_inc(cols_read, 1)
            nc.scalar.activation(s.cols2[:, :], s.mb[0][:, P:2 * P], ACT.Copy).then_inc(cols_read, 1)
            act.wait_ge(cols_read, 2)
            nc.scalar.activation(s.c_col[:, 0, :], s.cols2[:, 0:KT], ACT.Exp, scale=-1.0).then_inc(c_exp, 1)
            for m in range(TM):
                act.wait_ge(x_in[m], 16)
                nc.scalar.activation(junk[:, :], xn[:, m, :], ACT.Square,
                                     accum_out=ssq[:, m:m + 1]).then_inc(sq_done, 1)
                act.wait_ge(sq_done, m + 1)
            act.wait_ge(ms_ready, 1)
            nc.scalar.activation(ssq[:, 8:12], ssq[:, 4:8], ACT.Sqrt).then_inc(rms_ready, 1)
            modulated_scalar(nc, act, s, tmp, 0, h_hi)
            for u in range(2):
                split_hi(nc, act, s, 0, u, first=True)

        @block.tensor
        def _(pe):
            pe.wait_ge(consts_in, 16)
            pe.wait_ge(rows_in, 16 * 10)
            nc.tensor.transpose(s.mb[0][:, 0:P], rows[:, 0, :], s.ident)
            nc.tensor.transpose(s.mb[0][:, P:2 * P], rows[:, 1, :], s.ident).then_inc(cols_done, 1)
            pe.wait_ge(ada_used, NADA)
            pe.wait_ge(ones_set, 1)
            for sct in range(2):
                for k in range(KT):
                    mm = nc.tensor.matmul(s.mb[1][:, sct * KT + k:sct * KT + k + 1], acc[:, sct, k * P:(k + 1) * P],
                                          s.ones[:, 0:1], start=True, stop=True)
            mm.then_inc(mod_sums, 1)
            pe.wait_ge(xn_ready, TM)
            pe.wait_ge(mod_ready, 1)
            modulated_tensor(nc, pe, s, xn, 0, h_turned)

        @block.vector
        def _(dve):
            dve.wait_ge(c_exp, 1)
            nc.vector.tensor_scalar(s.c_col[:, 1, :], s.c_col[:, 0, :], 1.0, None, ALU.add).then_inc(c_ready, 1)
            dve.wait_ge(c_ready, 1)
            nc.vector.reciprocal(s.c_col[:, 2, :], s.c_col[:, 1, :]).then_inc(c_ready, 1)
            dve.wait_ge(c_ready, 2)
            nc.vector.tensor_tensor(s.c_col[:, 3, :], s.c_col[:, 2, :], s.cols2[:, 0:KT], ALU.mult).then_inc(c_ready, 1)
            nc.vector.tensor_copy(s.ident_bf[:, :], s.ident).then_inc(scaled, 1)
            nc.vector.tensor_copy(s.causal_bf[:, :], s.base[:, C_CAUSAL:C_CAUSAL + P]).then_inc(scaled, 1)
            nc.vector.tensor_scalar(s.fq_gain[:, :], s.cols2[:, 16:17], SCALE, None, ALU.mult).then_inc(scaled, 1)
            dve.wait_ge(gains_in, 48)
            nc.vector.tensor_scalar(s.gain_bc[:, 0, :], s.gain_bc[:, 0, :], SCALE, None, ALU.mult).then_inc(scaled, 1)
            dve.wait_ge(acc_zero, 1)
            dve.wait_ge(c_ready, 3)

            def step(j, slot, uses):
                dve.wait_ge(ada_in[slot], 16 * uses)
                if not isinstance(j, int) or j >= 2:
                    dve.wait_ge(ada_used, j - 1)
                sct = acc[:, ds(j % 2, 1), :].rearrange("p o n -> p (o n)")
                nc.vector.scalar_tensor_tensor(out=sct, in0=ada_raw[:, slot, :], scalar=s.c_col[:, 3, ds(j // 2, 1)],
                                               in1=sct, op0=ALU.mult, op1=ALU.add).then_inc(ada_used, 1)

            for j in range(3):
                step(j, j, 1)
            dve.wait_ge(sq_done, TM)
            nc.vector.tensor_scalar(ssq[:, 4:8], ssq[:, 0:4], 1.0 / D, EPS, ALU.mult, ALU.add).then_inc(ms_ready, 1)
            dve.wait_ge(rms_ready, 1)
            nc.vector.reciprocal(ssq[:, 12:16], ssq[:, 8:12]).then_inc(rstd_ready, 1)
            dve.wait_ge(rstd_ready, 1)
            for m in range(TM):
                nc.vector.tensor_scalar(xn[:, m, :], xn[:, m, :], ssq[:, 12 + m:13 + m], None,
                                        ALU.mult).then_inc(xn_ready, 1)
            with dve.Fori(1, NADA // 3) as i:
                for e in range(3):
                    step(3 * i + e, e, i + 1)
            for j in range(NADA // 3 * 3, NADA):
                step(j, j % 3, j // 3 + 1)
            dve.wait_ge(mod_sums, 1)
            nc.vector.tensor_tensor(s.mod[:, 1, :], s.mb[1][:, 0:KT], s.cols1[:, 0:KT], ALU.add).then_inc(scaled, 1)
            nc.vector.tensor_tensor(s.mod[:, 4, :], s.mb[1][:, KT:2 * KT], s.cols1[:, KT:2 * KT],
                                    ALU.add).then_inc(mod_ready, 1)
            dve.wait_ge(mod_ready, 1)
            nc.vector.scalar_tensor_tensor(out=s.mod[:, 0, :], in0=s.mod[:, 4, :], scalar=1.0,
                                           in1=s.cols1[:, 96:112], op0=ALU.add, op1=ALU.mult).then_inc(mod_ready, 1)
            dve.wait_ge(mod_ready, 2)
            dve.wait_ge(scaled, 5)
            modulated_vector(nc, dve, s, tmp, s.mod[:, 0, :], s.mod[:, 1, :], 0, h_turned, h_hi, h_lo)
            for u in range(2):
                split_lo(nc, dve, s, 0, u)



def phase_project(nc, A, s):
    with ExitStack() as ctx:
        sb = lambda name, shape, dt=F32: ctx.enter_context(nc.sbuf_tensor(name, shape, dt))
        sem = s.sem
        ada_raw = sb("ada2_raw", [P, 3, D])
        acc = sb("ada2_acc", [P, 4, D])
        stage = sb("proj_stage", [P, TM, 512])
        sq = sb("proj_sq", [P, 2, 512])
        st = sb("proj_stats", [P, 4, 16])

        ada_in = [sem(f"ada2_in{i}") for i in range(3)]
        ada_used, acc_zero, bias_in = sem("ada2_used"), sem("acc2_zero"), sem("gate_bias_in")
        squared, summed = sem("proj_squared"), sem("proj_summed")
        ms, rms, rstd, normed = sem("proj_ms"), sem("proj_rms"), sem("proj_rstd"), sem("proj_normed")
        stored = s.proj_stored
        gate_sums, gate_ready, col_sums, col_ready = sem("gate_sums"), sem("gate_ready"), sem("col_sums"), sem("col_ready")
        PER = 6
        NADA = 4 * KT
        ada = A.w_ada.rearrange("l (k p) n -> p (l k) n", p=P)

        block = ctx.enter_context(nc.Block())

        @block.sync
        def _(sp):
            for g, sct in enumerate((2, 5)):
                sp.dma_start(s.gate_bc[g][:, :], A.b_ada[0, sct * D:(sct + 1) * D].partition_broadcast(P)).then_inc(bias_in, 16)

            def loads(i, units, steps, skip=0):
                for u in range(4):
                    for e in (range(2 * u, 2 * u + 2) if u < 3 else ()):
                        if e >= steps:
                            continue
                        j = PER * i + e
                        if e >= 3 or skip == 0:
                            sp.wait_ge(ada_used, j - 2)
                        sp.dma_start(ada_raw[:, e % 3, :], ada[:, ds(j % KT, 1), ds((2 + j // KT) * D, D)].rearrange(
                            "p o n -> p (o n)")).then_inc(ada_in[e % 3], 16)
                    load_unit(sp, s, 2 * i + 2 + u // 2, u % 2, units(u))

            loads(0, lambda u: w_in_unit(A, 512, u), PER, skip=1)
            with sp.Fori(1, 5) as i:
                loads(i, lambda u: w_in_unit(A, (i + 1) * 512, u), PER)
            with sp.Fori(5, NB_IN - 1) as i:
                loads(i, lambda u: w_in_unit(A, (i + 1) * 512 + FOX, u), PER)
            loads(NB_IN - 1, lambda u: w_cmp_unit(A.cmp_w1_k, u), NADA - PER * (NB_IN - 1))

        @block.scalar
        def _(act):
            def body(i, first=False):
                for u in range(3):
                    split_hi(nc, act, s, 2 * i + u // 2 + 1, u % 2)
                for m in range(TM):
                    await_bank(act, s, i, m, 4 * i + 3)
                    if not first:
                        act.wait_ge(stored[m], 16 * i)
                    nc.scalar.activation(stage[:, m, :], s.gb[m][:, :], ACT.Copy).then_inc(s.bank_free, 1)
                    act.wait_ge(s.bank_free, 4 * (ROUND_IN + i) + m + 1)
                    if not first or m >= 2:
                        act.wait_ge(summed, 4 * i + m - 1)
                    nc.scalar.activation(sq[:, m % 2, :], stage[:, m, :], ACT.Square).then_inc(squared, 1)
                split_hi(nc, act, s, 2 * i + 2, 1)
                act.wait_ge(ms, i + 1)
                nc.scalar.activation(st[:, 2, :], st[:, 1, :], ACT.Sqrt).then_inc(rms, 1)

            body(0, True)
            with act.Fori(1, NB_IN) as i:
                body(i)

        @block.tensor
        def _(pe):
            with pe.Fori(0, NB_IN) as i:
                for u in range(4):
                    rows_unit(nc, pe, s, 2 * i + u // 2, u % 2, s.act_hi, s.act_lo, 4 * u, u == 0, u == 3, ROUND_IN + i)
            pe.wait_ge(ada_used, NADA)
            for g, sct in enumerate((0, 3)):
                for n in range(4):
                    if g:
                        pe.wait_ge(gate_ready, n + 1)
                    nc.tensor.matmul(s.mb[n][:, :], s.ones[:, :], acc[:, sct, n * 512:(n + 1) * 512],
                                     start=True, stop=True).then_inc(gate_sums, 1)
            pe.wait_ge(gate_ready, 5)
            for sct in (1, 2):
                for k in range(KT):
                    mm = nc.tensor.matmul(s.mb[0][:, (sct - 1) * KT + k:(sct - 1) * KT + k + 1],
                                          acc[:, sct, k * P:(k + 1) * P], s.ones[:, 0:1], start=True, stop=True)
            mm.then_inc(col_sums, 1)

        @block.vector
        def _(dve):
            def step(j, slot, uses, first):
                dve.wait_ge(ada_in[slot], 16 * uses)
                if not first:
                    dve.wait_ge(ada_used, j)
                sct = acc[:, ds(j // KT, 1), :].rearrange("p o n -> p (o n)")
                nc.vector.scalar_tensor_tensor(out=sct, in0=ada_raw[:, slot, :], scalar=s.c_col[:, 3, ds(j % KT, 1)],
                                               in1=sct, op0=ALU.mult, op1=ALU.add).then_inc(ada_used, 1)

            def body(i, steps, first=False):
                for u in range(4):
                    if u == 3:
                        for m in range(TM):
                            dve.wait_ge(squared, 4 * i + m + 1)
                            nc.vector.tensor_reduce(st[:, 0, 4 * m:4 * m + 4],
                                                    sq[:, m % 2, :].rearrange("p (h d) -> p h d", h=4),
                                                    AX.X, ALU.add).then_inc(summed, 1)
                    split_lo(nc, dve, s, 2 * i + u // 2 + 1, u % 2)
                    if u < 3:
                        for e in (2 * u, 2 * u + 1):
                            if e < steps:
                                step(PER * i + e, e % 3, 2 * i + e // 3 + 1, first and e == 0)
                dve.wait_ge(summed, 4 * i + 4)
                nc.vector.tensor_scalar(st[:, 1, :], st[:, 0, :], 1.0 / HD, EPS, ALU.mult, ALU.add).then_inc(ms, 1)
                dve.wait_ge(rms, i + 1)
                nc.vector.reciprocal(st[:, 3, :], st[:, 2, :]).then_inc(rstd, 1)
                dve.wait_ge(rstd, 3 * i + 1)
                r = st[:, 3, :].rearrange("p (m h) -> p m h", m=TM)
                flag = s.base[:, ds(C_FLAG + 4 * i, 4)].unsqueeze(1).broadcast_to([P, TM, 4])
                nflag = s.base[:, ds(C_NFLAG + 4 * i, 4)].unsqueeze(1).broadcast_to([P, TM, 4])
                nc.vector.tensor_tensor(r, r, flag, ALU.mult).then_inc(rstd, 1)
                dve.wait_ge(rstd, 3 * i + 2)
                nc.vector.tensor_tensor(r, r, nflag, ALU.add).then_inc(rstd, 1)
                dve.wait_ge(rstd, 3 * i + 3)
                for m in range(TM):
                    v = stage[:, m, :].rearrange("p (h d) -> p h d", h=4)
                    nc.vector.tensor_tensor(v, v, st[:, 3, 4 * m:4 * m + 4].unsqueeze(2).broadcast_to([P, 4, HD]),
                                            ALU.mult).then_inc(normed, 1)

            dve.wait_ge(acc_zero, 1)
            body(0, PER, True)
            with dve.Fori(1, NB_IN - 1) as i:
                body(i, PER)
            body(NB_IN - 1, NADA - PER * (NB_IN - 1))
            dve.wait_ge(bias_in, 32)
            for g in range(2):
                for n in range(4):
                    dve.wait_ge(gate_sums, 4 * g + n + 1)
                    part = s.gate_bc[g][:, n * 512:(n + 1) * 512]
                    nc.vector.tensor_tensor(part, s.mb[n][:, :], part, ALU.add).then_inc(gate_ready, 1)
            dve.wait_ge(col_sums, 1)
            nc.vector.tensor_tensor(s.mod[:, 3, :], s.mb[0][:, 0:KT], s.cols1[:, 3 * KT:4 * KT], ALU.add).then_inc(col_ready, 1)
            nc.vector.tensor_tensor(s.mod[:, 5, :], s.mb[0][:, KT:2 * KT], s.cols1[:, 4 * KT:5 * KT], ALU.add).then_inc(col_ready, 1)
            dve.wait_ge(col_ready, 2)
            nc.vector.scalar_tensor_tensor(out=s.mod[:, 2, :], in0=s.mod[:, 5, :], scalar=1.0,
                                           in1=s.cols1[:, 112:128], op0=ALU.add, op1=ALU.mult).then_inc(col_ready, 1)

        @block.gpsimd
        def _(pool):
            nc.gpsimd.memset(acc[:, :, :], 0.0).then_inc(acc_zero, 1)
            with pool.Fori(0, NB_IN) as i:
                for m in range(TM):
                    pool.wait_ge(normed, 4 * i + m + 1)
                    pool.dma_start(s.proj[ds(i, 1), m].rearrange("o p n -> (o p) n"), stage[:, m, :]).then_inc(stored[m], 16)
            for m in range(TM):
                pool.wait_ge(stored[m], 16 * NB_IN)



def phase_compress(nc, A, s):
    with ExitStack() as ctx:
        sb = lambda name, shape, dt=F32: ctx.enter_context(nc.sbuf_tensor(name, shape, dt))
        sem = s.sem
        ZW = KT * NZ + P
        wz = sb("wz", [P, ZW])
        wz_hi, wz_lo = sb("wz_hi", [P, ZW], F32R), sb("wz_lo", [P, ZW], F32R)
        zb = sb("z_bias", [NZ, 1])
        z = sb("z", [NZ, 5, T])
        kcv = sb("kcv", [P, TM, 512])
        kcvT = sb("kcvT", [P, 4, T])
        XW = CMP_LEN * 64 + 64
        xb = sb("xb", [P, XW])
        xb_hi, xb_lo = sb("xb_hi", [P, XW], F32R), sb("xb_lo", [P, XW], F32R)
        w2 = sb("w2", [P, 2, 2, HD])
        hid = sb("hid", [64, 5, CMP_HID])
        hidT = sb("hidT", [P, 2, 64])
        kn = sb("cmp_kn", [64, 2, HD])
        kst = sb("cmp_kst", [64, 4])

        wz_in, zb_in, kc_in, w2_in = sem("wz_in"), sem("zb_in"), sem("kc_in"), sem("w2_in")
        zeroed = sem("wz_zero")
        wzh, wzl, z_sums = sem("wz_hi_ready"), sem("wz_lo_ready"), sem("z_sums")
        zs, za, gtr, g_ready = sem("z_vector"), sem("z_scalar"), sem("gates_turned"), s.gates_ready
        ktr, ktr_read, x_ready, xh, xl = sem("kcv_turned"), sem("kcv_read"), sem("xb_ready"), sem("xb_hi_ready"), sem("xb_lo_ready")
        h_exp, h_vec, h_tr, h_trr = sem("hid_exp"), sem("hid_vec"), sem("hid_turned"), sem("hid_turned_read")
        k2, k2s, k2v, k2t, k2r = sem("cmp_out"), sem("cmp_out_sq"), sem("cmp_out_vec"), sem("cmp_out_turned"), s.cmp_ready
        hfree = sem("hid_free")

        block = ctx.enter_context(nc.Block())

        @block.sync
        def _(sp):
            sp.wait_ge(zeroed, 4)
            wv = wz[:, 0:KT * NZ].rearrange("p (k n) -> p k n", n=NZ)
            src = A.w_in.rearrange("l (k p) n -> p (l k) n", p=P)
            sp.dma_start(wv[:, :, 0:FOX], src[:, :, FZ:FZ + FOX]).then_inc(wz_in, 16)
            sp.dma_start(wv[:, :, FOX:32], src[:, :, GZ:GZ + 24]).then_inc(wz_in, 16)
            sp.dma_start(wv[:, :, 32:NZ], src[:, :, FZ:FZ + FOX]).then_inc(wz_in, 16)
            sp.dma_start(zb[0:FOX, :], A.b_forget.rearrange("l h -> h l")).then_inc(zb_in, 16)
            sp.dma_start(zb[32:NZ, :], A.b_forget.rearrange("l h -> h l")).then_inc(zb_in, 16)
            sp.dma_start(kcv[:, :, :], s.proj[8].rearrange("m p n -> p m n")).then_inc(kc_in, 16)
            for kv, w in enumerate((A.cmp_w2_k, A.cmp_w2_v)):
                sp.dma_start(w2[:, kv], w.rearrange("l (k p) n -> p (l k) n", p=P)).then_inc(w2_in, 16)
            for u in range(4):
                load_unit(sp, s, PAIR_CMP + 2 + u // 2, u % 2, w_cmp_unit(A.cmp_w1_v, u))
            for u in range(4):
                load_unit(sp, s, PAIR_OUT + u // 2, u % 2, w_out_unit(A, 0, u))

        @block.gpsimd
        def _(pool):
            nc.gpsimd.memset(wz[:, :], 0.0).then_inc(zeroed, 1)
            nc.gpsimd.memset(zb[:, :], 0.0).then_inc(zeroed, 1)
            nc.gpsimd.memset(xb[:, :], 0.0).then_inc(zeroed, 1)
            nc.gpsimd.memset(kst[:, :], 0.0).then_inc(zeroed, 1)

        @block.tensor
        def _(pe):
            pe.wait_ge(wzl, 1)
            for k in range(KT):
                c = slice(k * NZ, k * NZ + P)
                mm = three_products(nc, s.mb[0][:, :], wz_hi[:, c], wz_lo[:, c], s.act_hi[:, k, :], s.act_lo[:, k, :],
                                    k == 0, k == KT - 1)
            mm.then_inc(z_sums, 1)
            pe.wait_ge(kc_in, 16)
            for e in range(4):
                if e >= 2:
                    pe.wait_ge(ktr_read, e - 1)
                for m in range(TM):
                    mm = nc.tensor.transpose(s.mb[1 + e % 2][:, m * P:(m + 1) * P], kcv[:, m, e * HD:(e + 1) * HD], s.ident)
                mm.then_inc(ktr, 1)
            for kv in range(2):
                pe.wait_ge(xl, kv + 1)
                for u in range(4):
                    pair, slot = PAIR_CMP + 2 * kv + u // 2, u % 2
                    pe.wait_ge(s.w_lo_ready, 2 * pair + slot + 1)
                    wh = s.w_hi[:, slot].rearrange("p a (b n) -> p (a b) n", b=2)
                    wl = s.w_lo[:, slot].rearrange("p a (b n) -> p (a b) n", b=2)
                    for e in range(8):
                        l = 8 * u + e
                        c = slice(l * 64, l * 64 + P)
                        mm = three_products(nc, s.mb[3][:, kv * 256:(kv + 1) * 256], xb_hi[:, c], xb_lo[:, c],
                                            wh[:, e, :], wl[:, e, :], l == 0, l == CMP_LEN - 1)
                    mm.then_inc(s.unit_used, 1)
                pe.wait_ge(h_vec, 3 * kv + 3)
                for c in range(2):
                    mm = nc.tensor.transpose(s.mb[1][:, c * 64:(c + 1) * 64], hid[:, 3, c * P:(c + 1) * P], s.ident[0:64, 0:64])
                mm.then_inc(h_tr, 1)
                pe.wait_ge(h_trr, kv + 1)
                pe.wait_ge(w2_in, 32)
                for c in range(2):
                    mm = nc.tensor.matmul(s.mb[2][0:64, 0:HD], hidT[:, c, :], w2[:, kv, c, :], start=c == 0, stop=c == 1)
                mm.then_inc(k2, 1)
                if kv == 0:
                    pe.wait_ge(k2v, 3)
                    nc.tensor.transpose(s.mb[1][:, 0:64], kn[:, 1, :], s.ident[0:64, 0:64]).then_inc(k2t, 1)
                    pe.wait_ge(k2r, 1)
            pe.wait_ge(zs, 5)
            for m in range(TM):
                mm = nc.tensor.transpose(s.mb[0][:, m * NZ:(m + 1) * NZ], z[:, 3, m * P:(m + 1) * P], s.ident[0:NZ, 0:NZ])
            mm.then_inc(gtr, 1)

        @block.scalar
        def _(act):
            act.wait_ge(wz_in, 48)
            nc.scalar.activation(wz_hi[:, :], wz[:, :], ACT.Copy).then_inc(wzh, 1)
            for e in range(4):
                act.wait_ge(ktr, e + 1)
                nc.scalar.activation(kcvT[:, e, :], s.mb[1 + e % 2][:, :], ACT.Copy).then_inc(ktr_read, 1)
            act.wait_ge(x_ready, 4)
            nc.scalar.activation(xb_hi[:, :], xb[:, :], ACT.Copy).then_inc(xh, 1)
            for u in range(4):
                split_hi(nc, act, s, PAIR_CMP + u // 2 + 1, u % 2)
            act.wait_ge(zs, 1)
            nc.scalar.activation(z[:, 1, :], z[:, 0, :], ACT.Abs).then_inc(za, 1)
            act.wait_ge(za, 1)
            nc.scalar.activation(z[:, 2, :], z[:, 1, :], ACT.Exp, scale=-1.0).then_inc(za, 1)
            nc.scalar.activation(z[:, 3, :], z[:, 0, :], ACT.Exp, scale=-1.0).then_inc(za, 1)
            act.wait_ge(zs, 2)
            nc.scalar.activation(z[:, 1, :], z[:, 2, :], ACT.Ln).then_inc(za, 1)
            for kv in range(2):
                act.wait_ge(s.unit_used, 2 * PAIR_CMP + 4 * kv + 4)
                nc.scalar.activation(hid[:, 0, :], s.mb[3][0:64, kv * 256:(kv + 1) * 256], ACT.Copy).then_inc(h_exp, 1)
                act.wait_ge(h_exp, 2 * kv + 1)
                nc.scalar.activation(hid[:, 1, :], hid[:, 0, :], ACT.Exp, scale=-1.0).then_inc(h_exp, 1)
                if kv == 0:
                    act.wait_ge(x_ready, 8)
                    act.wait_ge(s.unit_used, 2 * PAIR_CMP + 4)
                    nc.scalar.activation(xb_hi[:, :], xb[:, :], ACT.Copy).then_inc(xh, 1)
                act.wait_ge(h_tr, kv + 1)
                nc.scalar.activation(hidT[:, :, :], s.mb[1][:, 0:P].rearrange("p (c n) -> p c n", c=2), ACT.Copy).then_inc(h_trr, 1)
                act.wait_ge(k2, kv + 1)
                if kv == 0:
                    nc.scalar.activation(kn[:, 0, :], s.mb[2][0:64, 0:HD], ACT.Copy).then_inc(k2s, 1)
                    act.wait_ge(k2s, 1)
                    nc.scalar.activation(hid[:, 4, 0:HD], kn[:, 0, :], ACT.Square, accum_out=kst[:, 0:1]).then_inc(k2s, 1)
                    act.wait_ge(k2v, 1)
                    nc.scalar.activation(kst[:, 2:3], kst[:, 1:2], ACT.Sqrt).then_inc(k2s, 1)
                    act.wait_ge(k2t, 1)
                    nc.scalar.activation(s.kcT[:, :], s.mb[1][:, 0:64], ACT.Copy, scale=s.cols2[:, 19:20]).then_inc(k2r, 1)
                    for u in range(4):
                        split_hi(nc, act, s, PAIR_CMP + 2 + u // 2 + 1, u % 2)
                else:
                    nc.scalar.activation(s.vc[:, :], s.mb[2][0:64, 0:HD], ACT.Copy).then_inc(k2r, 1)

        @block.vector
        def _(dve):
            dve.wait_ge(wzh, 1)
            nc.vector.tensor_tensor(wz_lo[:, :], wz[:, :], wz_hi[:, :].bitcast(F32), ALU.subtract).then_inc(wzl, 1)

            def windows(kv):
                xv = xb[:, 0:CMP_LEN * 64].rearrange("p (l g n) -> p l g n", g=NG, n=CW)
                for g in range(NG):
                    src = kcvT[:, 2 * kv + g, :].rearrange("p (n b) -> p b n", b=CMP_STRIDE)
                    for a in range(2):
                        pe_l = s.cols2[:, 22 + 32 * kv + 16 * a:22 + 32 * kv + 16 * a + 16]
                        nc.vector.tensor_tensor(xv[:, 16 * a:16 * a + 16, g, 0:NCMP], src[:, :, a:a + NCMP],
                                                pe_l.unsqueeze(2).broadcast_to([P, 16, NCMP]), ALU.add).then_inc(x_ready, 1)

            dve.wait_ge(ktr_read, 2)
            dve.wait_ge(zeroed, 4)
            windows(0)
            dve.wait_ge(xh, 1)
            nc.vector.tensor_tensor(xb_lo[:, :], xb[:, :], xb_hi[:, :].bitcast(F32), ALU.subtract).then_inc(xl, 1)
            dve.wait_ge(z_sums, 1)
            dve.wait_ge(zb_in, 32)
            nc.vector.tensor_scalar(z[:, 0, :], s.mb[0][0:NZ, :], zb[:, :], None, ALU.add).then_inc(zs, 1)
            dve.wait_ge(ktr_read, 4)
            dve.wait_ge(xl, 1)
            windows(1)
            for u in range(4):
                split_lo(nc, dve, s, PAIR_CMP + u // 2 + 1, u % 2)
            dve.wait_ge(za, 3)
            nc.vector.tensor_scalar(z[:, 2, :], z[:, 2, :], 1.0, None, ALU.add).then_inc(zs, 1)
            nc.vector.tensor_scalar(z[:, 3, :], z[:, 3, :], 1.0, None, ALU.add).then_inc(zs, 1)
            dve.wait_ge(zs, 3)
            nc.vector.tensor_scalar(z[:, 4, :], z[:, 0, :], 0.0, None, ALU.min).then_inc(zs, 1)
            nc.vector.reciprocal(z[:, 3, :], z[:, 3, :]).then_inc(zs, 1)
            dve.wait_ge(za, 4)
            dve.wait_ge(zs, 5)
            nc.vector.tensor_tensor(z[:, 4, :], z[:, 4, :], z[:, 1, :], ALU.subtract).then_inc(zs, 1)
            nc.vector.memset(z[:, 2, :], 1.0).then_inc(zs, 1)
            dve.wait_ge(zs, 7)
            nc.vector.tensor_tensor_scan(s.cum[:, :], z[:, 2, :], z[:, 4, :], 0.0, ALU.mult, ALU.add).then_inc(zs, 1)
            dve.wait_ge(zs, 8)
            nc.vector.tensor_scalar(s.auxR[:, :], s.cum[:, :], s.base[0:NZ, C_N1:C_N1 + 1], s.base[0:NZ, C_N2:C_N2 + 1],
                                    ALU.mult, ALU.add).then_inc(zs, 1)
            for kv in range(2):
                dve.wait_ge(h_exp, 2 * kv + 2)
                nc.vector.tensor_scalar(hid[:, 2, :], hid[:, 1, :], 1.0, None, ALU.add).then_inc(h_vec, 1)
                dve.wait_ge(h_vec, 3 * kv + 1)
                nc.vector.reciprocal(hid[:, 4, :], hid[:, 2, :]).then_inc(h_vec, 1)
                dve.wait_ge(h_vec, 3 * kv + 2)
                nc.vector.tensor_tensor(hid[:, 3, :], hid[:, 0, :], hid[:, 4, :], ALU.mult).then_inc(h_vec, 1)
                if kv == 0:
                    dve.wait_ge(xh, 2)
                    nc.vector.tensor_tensor(xb_lo[:, :], xb[:, :], xb_hi[:, :].bitcast(F32), ALU.subtract).then_inc(xl, 1)
                    dve.wait_ge(k2s, 2)
                    nc.vector.tensor_scalar(kst[:, 1:2], kst[:, 0:1], 1.0 / HD, EPS, ALU.mult, ALU.add).then_inc(k2v, 1)
                    dve.wait_ge(k2s, 3)
                    nc.vector.reciprocal(kst[:, 3:4], kst[:, 2:3]).then_inc(k2v, 1)
                    dve.wait_ge(k2v, 2)
                    nc.vector.tensor_scalar(kn[:, 1, :], kn[:, 0, :], kst[:, 3:4], None, ALU.mult).then_inc(k2v, 1)
                    for u in range(4):
                        split_lo(nc, dve, s, PAIR_CMP + 2 + u // 2 + 1, u % 2)
            dve.wait_ge(gtr, 1)
            nc.vector.tensor_copy(s.gates[:, :, :], s.mb[0][:, 0:TM * NZ].rearrange("p (m n) -> p m n", m=TM)).then_inc(g_ready, 1)
            dve.wait_ge(g_ready, 1)



def item_scores(nc, pe, s, a, I, n, qT, kT, aux, early):
    w = (n + 1) * P
    if not early:
        pe.wait_ge(a.p_ready, I - 1)
    bank = s.gb[n % 2]
    nc.tensor.matmul(bank[:, n * P:w], s.ident_bf[:, :], s.causal_bf[:, :], start=True, stop=False, skip_group_check=True)
    if aux is not None:
        nc.tensor.matmul(bank[:, 0:w], aux[:, n * P:(n + 1) * P], s.auxR[:, 0:w], start=False, stop=False,
                         skip_group_check=True)
    nc.tensor.matmul(bank[:, 0:w], qT[:, n * P:(n + 1) * P], kT(w), start=False, stop=True,
                     skip_group_check=True).then_inc(a.s_done, 1)


def item_max(nc, dve, s, a, I, n):
    dve.wait_ge(a.s_done, I + 1)
    nc.vector.tensor_reduce(a.nmax[:, n:n + 1], s.gb[n % 2][:, 0:(n + 1) * P], AX.X, ALU.max,
                            negate=True).then_inc(a.max_ready, 1)


def item_exp(nc, act, s, a, I, n, early):
    act.wait_ge(a.max_ready, I + 1)
    if not early:
        act.wait_ge(a.pt_done, I - 3)
    nc.scalar.activation(a.p[:, n, 0:(n + 1) * P], s.gb[n % 2][:, 0:(n + 1) * P], ACT.Exp,
                         bias=a.nmax[:, n:n + 1], accum_out=a.rsum[:, n:n + 1]).then_inc(a.p_ready, 1)


def item_reciprocal(nc, dve, s, a, I, n):
    dve.wait_ge(a.p_ready, I + 1)
    nc.vector.tensor_scalar(a.rinv[:, 0, n:n + 1], a.rsum[:, n:n + 1], 1e-30, None, ALU.max).then_inc(a.r_ready, 1)
    dve.wait_ge(a.r_ready, 2 * I + 1)
    nc.vector.reciprocal(a.rinv[:, 1, n:n + 1], a.rinv[:, 0, n:n + 1]).then_inc(a.r_ready, 1)


def item_normalise(nc, dve, s, a, I, n, gate):
    dve.wait_ge(a.r_ready, 2 * I + 2)
    part = a.p[:, n, 0:(n + 1) * P]
    if gate is None:
        nc.vector.tensor_scalar(part, part, a.rinv[:, 1, n:n + 1], None, ALU.mult).then_inc(a.pn_ready, 1)
    else:
        nc.vector.tensor_scalar(part, part, a.rinv[:, 1, n:n + 1], gate, ALU.mult, ALU.mult).then_inc(a.pn_ready, 1)


def item_turn(nc, pe, s, a, I, n, early):
    pe.wait_ge(a.pn_ready, I + 1)
    if not early:
        pe.wait_ge(a.pt_ready, I - 1)
    for b in range(n + 1):
        mm = nc.tensor.transpose(s.gb[2 + n % 2][:, b * P:(b + 1) * P], a.p[:, n, b * P:(b + 1) * P], s.ident)
    mm.then_inc(a.pt_done, 1)


def item_copy(nc, act, s, a, I, n, early):
    act.wait_ge(a.pt_done, I + 1)
    if not early:
        act.wait_ge(a.pv_done, I - 1)
    nc.scalar.activation(a.pT[:, n % 2, 0:(n + 1) * P], s.gb[2 + n % 2][:, 0:(n + 1) * P], ACT.Copy).then_inc(a.pt_ready, 1)


def item_values(nc, pe, s, a, I, n, v, bank, start):
    pe.wait_ge(a.pt_ready, I + 1)
    for b in range(n + 1):
        mm = nc.tensor.matmul(bank[:, n * P:(n + 1) * P], v[:, b, :], a.pT[:, n % 2, b * P:(b + 1) * P],
                              start=start and b == 0, stop=b == n, skip_group_check=True)
    mm.then_inc(a.pv_done, 1)


def attention_state(nc, s, sb, sem, tag):
    a = Names()
    a.p, a.pT = sb(tag + "p", [P, 4, T]), sb(tag + "pT", [P, 2, T])
    a.nmax, a.rsum, a.rinv = sb(tag + "nmax", [P, TM]), sb(tag + "rsum", [P, TM]), sb(tag + "rinv", [P, 3, TM])
    a.s_done, a.max_ready, a.p_ready = sem(tag + "scores_done"), sem(tag + "max_ready"), sem(tag + "p_ready")
    a.r_ready, a.pn_ready = sem(tag + "r_ready"), sem(tag + "pn_ready")
    a.pt_done, a.pt_ready, a.pv_done = sem(tag + "pT_done"), sem(tag + "pT_ready"), sem(tag + "pv_done")
    a.o_hi, a.o_lo = sem(tag + "o_hi"), sem(tag + "o_lo")
    return a


def phase_fox(nc, A, s):
    with ExitStack() as ctx:
        sb = lambda name, shape, dt=F32: ctx.enter_context(nc.sbuf_tensor(name, shape, dt))
        sem = s.sem
        raw = sb("fox_raw", [P, 2, 3, TM, HD])
        qkT = sb("fox_qkT", [P, 2, 2, T])
        aux = sb("fox_aux", [NZ, 2, T])
        a = attention_state(nc, s, sb, sem, "fox_")
        landed, v_landed = [sem(f"fox_qk_landed{i}") for i in range(2)], [sem(f"fox_v_landed{i}") for i in range(2)]
        turned, turned_read, aux_ready = sem("fox_qk_turned"), sem("fox_qk_read"), sem("fox_aux_ready")
        PAIRS = FOX // 2

        block = ctx.enter_context(nc.Block())

        @block.sync
        def _(sp):
            def load(j, e, first=False):
                for x in range(3):
                    if not first and x == 0:
                        sp.wait_ge(turned, 2 * (2 * j + e) - 2)
                    if not first and x == 2:
                        sp.wait_ge(a.pv_done, 4 * (2 * j + e) - 4)
                    src = s.proj[ds(2 * x + j // 2, 1), :, :, ds((j % 2) * 256 + e * HD, HD)]
                    sp.dma_start(raw[:, e, x], src.rearrange("o m p d -> p (o m) d")).then_inc(
                        (v_landed if x == 2 else landed)[e], 16)
            for e in range(2):
                load(0, e, True)
            with sp.Fori(1, PAIRS) as j:
                for e in range(2):
                    load(j, e)

        def turn_qk(pe, j, e):
            h = 2 * j + e
            pe.wait_ge(landed[e], 32 * (j + 1))
            if not (isinstance(h, int) and h == 0):
                pe.wait_ge(turned_read, 2 * h)
            for x in range(2):
                for m in range(TM):
                    mm = nc.tensor.transpose(s.mb[2 + x][:, m * P:(m + 1) * P], raw[:, e, x, m, :], s.ident)
                mm.then_inc(turned, 1)

        @block.tensor
        def _(pe):
            def pair(j, first, last):
                for e in range(2):
                    h = 2 * j + e
                    start = first and e == 0
                    for n in range(TM):
                        I = 4 * h + n
                        if n == 0:
                            pe.wait_ge(turned_read, 2 * h + 2)
                            pe.wait_ge(aux_ready, h + 1)
                        item_scores(nc, pe, s, a, I, n, qkT[:, e, 0], lambda w: qkT[:, e, 1, 0:w], aux[:, e], start and n < 2)
                        if n >= 2 or not start:
                            item_turn(nc, pe, s, a, I - 2, (n - 2) % 4, start and n < 4)
                        if n == 3:
                            if not first:
                                pe.wait_ge(a.o_lo, h - 1)
                            pe.wait_ge(v_landed[e], 16 * (j + 1))
                            item_values(nc, pe, s, a, I - 3, 0, raw[:, e, 2], s.mb[e], True)
                        elif not start:
                            item_values(nc, pe, s, a, I - 3, n + 1, raw[:, 1 - e, 2], s.mb[1 - e], False)
                        if n == 1 and not (last and e == 1):
                            turn_qk(pe, j + e, 1 - e)
            turn_qk(pe, 0, 0)
            pair(0, True, False)
            with pe.Fori(1, PAIRS - 1) as j:
                pair(j, False, False)
            pair(PAIRS - 1, False, True)
            END = 4 * FOX
            item_turn(nc, pe, s, a, END - 2, 2, False)
            item_values(nc, pe, s, a, END - 3, 1, raw[:, 1, 2], s.mb[1], False)
            item_turn(nc, pe, s, a, END - 1, 3, False)
            for n in (2, 3):
                item_values(nc, pe, s, a, END - 4 + n, n, raw[:, 1, 2], s.mb[1], False)

        @block.scalar
        def _(act):
            def read_qk(h, e):
                for x in range(2):
                    act.wait_ge(turned, 2 * h + x + 1)
                    if not isinstance(h, int) or h >= 2:
                        act.wait_ge(a.s_done, 4 * h - 4)
                    nc.scalar.activation(qkT[:, e, x], s.mb[2 + x][:, :], ACT.Copy,
                                         scale=s.fq_gain[:, :] if x == 0 else s.cols2[:, 17:18]).then_inc(turned_read, 1)

            def o_hi(h, e):
                act.wait_ge(a.pv_done, 4 * h + 4)
                nc.scalar.activation(s.act_hi[:, ds(h, 1), :].rearrange("p o t -> p (o t)"), s.mb[e][:, :],
                                     ACT.Copy).then_inc(a.o_hi, 1)

            def pair(j, first, last):
                for e in range(2):
                    h = 2 * j + e
                    start = first and e == 0
                    for n in range(TM):
                        item_exp(nc, act, s, a, 4 * h + n, n, start)
                        if n >= 2 or not start:
                            item_copy(nc, act, s, a, 4 * h + n - 2, (n - 2) % 4, start)
                        if n == 2 and not (last and e == 1):
                            read_qk(h + 1, 1 - e)
                        if n == 3 and not start:
                            o_hi(h - 1, 1 - e)
            read_qk(0, 0)
            pair(0, True, False)
            with act.Fori(1, PAIRS - 1) as j:
                pair(j, False, False)
            pair(PAIRS - 1, False, True)
            for n in (2, 3):
                item_copy(nc, act, s, a, 4 * FOX - 4 + n, n, False)
            o_hi(FOX - 1, 1)

        @block.vector
        def _(dve):
            def make_aux(h, e):
                if not isinstance(h, int) or h >= 2:
                    dve.wait_ge(a.s_done, 4 * h - 4)
                nc.vector.tensor_scalar(aux[:, e, :], s.cum[:, :], s.base[0:NZ, ds(C_M1 + h, 1)],
                                        s.base[0:NZ, ds(C_M2 + h, 1)], ALU.mult, ALU.add).then_inc(aux_ready, 1)

            def o_lo(h, e):
                dve.wait_ge(a.o_hi, h + 1)
                nc.vector.tensor_tensor(s.act_lo[:, ds(h, 1), :].rearrange("p o t -> p (o t)"), s.mb[e][:, :],
                                        s.act_hi[:, ds(h, 1), :].rearrange("p o t -> p (o t)").bitcast(F32),
                                        ALU.subtract).then_inc(a.o_lo, 1)

            def pair(j, first, last):
                for e in range(2):
                    h = 2 * j + e
                    start = first and e == 0
                    for n in range(TM):
                        I = 4 * h + n
                        item_max(nc, dve, s, a, I, n)
                        if n >= 1 or not start:
                            item_reciprocal(nc, dve, s, a, I - 1, (n - 1) % 4)
                            item_normalise(nc, dve, s, a, I - 1, (n - 1) % 4, None)
                        if n == 0 and not (first and e < 2) and not (isinstance(h, int) and h < 2):
                            o_lo(h - 2, e)
                        if n == 2:
                            if not (last and e == 1):
                                make_aux(h + 1, 1 - e)
            make_aux(0, 0)
            pair(0, True, False)
            with dve.Fori(1, PAIRS - 1) as j:
                pair(j, False, False)
            pair(PAIRS - 1, False, True)
            item_reciprocal(nc, dve, s, a, 4 * FOX - 1, 3)
            item_normalise(nc, dve, s, a, 4 * FOX - 1, 3, None)
            for e in range(2):
                o_lo(FOX - 2 + e, e)


def phase_nsa(nc, A, s):
    with ExitStack() as ctx:
        sb = lambda name, shape, dt=F32: ctx.enter_context(nc.sbuf_tensor(name, shape, dt))
        sem = s.sem
        tabs = sb("nsa_tabs", [P, N_END])
        cos = tabs[:, N_COS:N_COS + 512].rearrange("p (m d) -> p m d", m=TM)
        sin = tabs[:, N_SIN:N_SIN + 512].rearrange("p (m d) -> p m d", m=TM)
        nq = sb("nsa_q", [P, 2, TM, HD])
        vv = sb("nsa_v", [P, 2, 2, TM, HD])
        qn = sb("nsa_qn", [P, 2, TM, HD])
        ra = sb("rope_a", [P, TM, HD])
        rb = sb("rope_b", [P, TM, HD])
        qr = sb("nsa_qr", [P, 2, TM, HD])
        qT = sb("nsa_qT", [P, 2, T])
        qrT = sb("nsa_qrT", [P, 2, T])
        kT = sb("nsa_kT", [P, 2, NG, T])
        pcw = sb("cmp_p", [P, 2, (TM + 1) * 64])
        pc = pcw[:, :, 0:TM * 64].rearrange("p e (m n) -> p e m n", m=TM)
        cst = sb("cmp_stats", [P, 4, TM])
        pcT = sb("cmp_pT", [64, 2, T])
        a = attention_state(nc, s, sb, sem, "nsa_")

        tabs_in, q_in = sem("nsa_tabs_in"), [sem(f"nsa_q_in{i}") for i in range(2)]
        v_in = [sem(f"nsa_v_in{i}") for i in range(2)]
        gained, roped, r_a, r_b = sem("nsa_gained"), sem("nsa_roped"), sem("rope_a_done"), sem("rope_b_done")
        turned, turned_read = sem("nsa_turned"), sem("nsa_turned_read")
        c_s, c_v, c_e, c_t, c_tr, c_pv = (sem("cmp_scores"), sem("cmp_vec"), sem("cmp_exp"), sem("cmp_turned"),
                                          sem("cmp_turned_read"), sem("cmp_pv"))
        NK = 2 * NG
        pad_zero = sem("cmp_pad_zero")
        PAIRS = NSA // 2

        block = ctx.enter_context(nc.Block())

        @block.sync
        def _(sp):
            sp.dma_start(tabs[:, :], A.nsa_tabs).then_inc(tabs_in, 16)

            def load_turn(t, e, src, first):
                if not first:
                    sp.wait_ge(gained, t - 1)
                sp.dma_start(nq[:, e], src).then_inc(q_in[e], 16)
            for t in range(NK):
                br, g = t // NG, t % NG
                load_turn(t, t % 2, s.proj[9 + br, :, :, g * HD:(g + 1) * HD].rearrange("m p d -> p m d"), t < 2)

            def load_head(j, e, first=False):
                h = 2 * j + e
                load_turn(h + NK, e, s.proj[ds(6 + j // 2, 1), :, :, ds((j % 2) * 256 + e * HD, HD)].rearrange(
                    "o m p d -> p (o m) d"), False)
                if not first:
                    sp.wait_ge(a.pv_done, 8 * h - 8)
                for br in range(2):
                    sp.dma_start(vv[:, e, br], s.proj[9 + br, :, :, ds((j // 2) * HD + 256, HD)].rearrange(
                        "m p d -> p m d")).then_inc(v_in[e], 16)
            for e in range(2):
                load_head(0, e, True)
            with sp.Fori(1, PAIRS) as j:
                for e in range(2):
                    load_head(j, e)

        @block.gpsimd
        def _(pool):
            def rope(t, e):
                pool.wait_ge(gained, t + 1)
                if not isinstance(t, int) or t >= 1:
                    pool.wait_ge(roped, t)
                nc.gpsimd.tensor_tensor(ra[:, :, :], qn[:, e], cos, ALU.mult).then_inc(r_a, 1)
                nc.gpsimd.tensor_tensor(rb[:, :, 0:64], qn[:, e, :, 64:HD], sin[:, :, 0:64], ALU.mult).then_inc(r_b, 1)
                nc.gpsimd.tensor_tensor(rb[:, :, 64:HD], qn[:, e, :, 0:64], sin[:, :, 64:HD], ALU.mult).then_inc(r_b, 1)
                pool.wait_ge(r_a, t + 1)
                pool.wait_ge(r_b, 2 * t + 2)
                if not isinstance(t, int) or t >= 2:
                    pool.wait_ge(turned, 2 * t - 2)
                nc.gpsimd.tensor_tensor(qr[:, e], ra[:, :, :], rb[:, :, :], ALU.add).then_inc(roped, 1)
            nc.gpsimd.memset(pcw[:, :, TM * 64:], 0.0).then_inc(pad_zero, 1)
            pool.wait_ge(tabs_in, 16)
            for t in range(NK):
                rope(t, t % 2)
            with pool.Fori(0, PAIRS) as j:
                for e in range(2):
                    rope(2 * j + e + NK, e)

        def turn(pe, t, e):
            early = isinstance(t, int) and t < 1
            pe.wait_ge(gained, t + 1)
            if not early:
                pe.wait_ge(turned_read, 2 * t)
            for m in range(TM):
                mm = nc.tensor.transpose(s.mb[2][:, m * P:(m + 1) * P], qn[:, e, m, :], s.ident)
            mm.then_inc(turned, 1)
            pe.wait_ge(roped, t + 1)
            for m in range(TM):
                mm = nc.tensor.transpose(s.mb[3][:, m * P:(m + 1) * P], qr[:, e, m, :], s.ident)
            mm.then_inc(turned, 1)

        @block.tensor
        def _(pe):
            def cmp_scores(h, e):
                pe.wait_ge(turned_read, 2 * (h + NK) + 1)
                for m in range(TM):
                    mm = nc.tensor.matmul(s.mb[2][:, m * 64:(m + 1) * 64], qT[:, e, m * P:(m + 1) * P], s.kcT[:, :],
                                          start=True, stop=True)
                mm.then_inc(c_s, 1)

            def cmp_turn(h, e):
                pe.wait_ge(c_v, 7 * h + 7)
                pe.wait_ge(turned_read, 2 * (h + NK) + 2)
                for m in range(TM):
                    mm = nc.tensor.transpose(s.mb[3][:, m * P:(m + 1) * P], pcw[:, e, m * 64:m * 64 + P], s.ident)
                mm.then_inc(c_t, 1)

            def cmp_values(h, e, early):
                pe.wait_ge(c_tr, h + 1)
                if not early:
                    pe.wait_ge(a.o_lo, h - 1)
                nc.tensor.matmul(s.mb[e][:, :], s.vc[:, :], pcT[:, e, :], start=True, stop=False,
                                 skip_group_check=True).then_inc(c_pv, 1)

            def pair(j, first, last):
                for e in range(2):
                    h = 2 * j + e
                    start = first and e == 0
                    more = not (last and e == 1)
                    for i in range(8):
                        br, n = i // 4, i % 4
                        I = 8 * h + i
                        if i == 0:
                            pe.wait_ge(turned_read, 2 * (h + NK) + 2)
                        item_scores(nc, pe, s, a, I, n, qrT[:, e], lambda w: kT[:, br, ds(j // 2, 1), 0:w].rearrange(
                            "p o t -> p (o t)"), None, start and i < 2)
                        if i >= 2 or not start:
                            item_turn(nc, pe, s, a, I - 2, (n - 2) % 4, start and i < 4)
                        if i == 2:
                            cmp_values(h, e, first)
                        if i >= 3:
                            if i == 3:
                                pe.wait_ge(v_in[e], 32 * (j + 1))
                            item_values(nc, pe, s, a, I - 3, (n - 3) % 4, vv[:, e, (i - 3) // 4], s.mb[e], False)
                        elif not start:
                            item_values(nc, pe, s, a, I - 3, n + 1, vv[:, 1 - e, 1], s.mb[1 - e], False)
                        if more:
                            if i == 2:
                                turn(pe, h + 1 + NK, 1 - e)
                            if i == 4:
                                cmp_scores(h + 1, 1 - e)
                            if i == 7:
                                cmp_turn(h + 1, 1 - e)
            for t in range(NK):
                turn(pe, t, t % 2)
            pe.wait_ge(pad_zero, 1)
            turn(pe, NK, 0)
            cmp_scores(0, 0)
            cmp_turn(0, 0)
            pair(0, True, False)
            with pe.Fori(1, PAIRS - 1) as j:
                pair(j, False, False)
            pair(PAIRS - 1, False, True)
            END = 8 * NSA
            item_turn(nc, pe, s, a, END - 2, 2, False)
            item_values(nc, pe, s, a, END - 3, 1, vv[:, 1, 1], s.mb[1], False)
            item_turn(nc, pe, s, a, END - 1, 3, False)
            for n in (2, 3):
                item_values(nc, pe, s, a, END - 4 + n, n, vv[:, 1, 1], s.mb[1], False)

        @block.scalar
        def _(act):
            def read_turn(t, plain, roped_):
                act.wait_ge(turned, 2 * t + 1)
                nc.scalar.activation(plain, s.mb[2][:, :], ACT.Copy).then_inc(turned_read, 1)
                act.wait_ge(turned, 2 * t + 2)
                nc.scalar.activation(roped_, s.mb[3][:, :], ACT.Copy).then_inc(turned_read, 1)

            def cmp_exp(h, e):
                act.wait_ge(c_v, 7 * h + 3)
                nc.scalar.activation(pc[:, e], pc[:, e], ACT.Exp).then_inc(c_e, 1)

            def cmp_read(h, e, early=False):
                act.wait_ge(c_t, h + 1)
                if not early:
                    act.wait_ge(c_pv, h - 1)
                nc.scalar.activation(pcT[:, e, :], s.mb[3][0:64, :], ACT.Copy).then_inc(c_tr, 1)

            def o_hi(h, e):
                act.wait_ge(a.pv_done, 8 * h + 8)
                nc.scalar.activation(s.act_hi[:, ds(FOX + h, 1), :].rearrange("p o t -> p (o t)"), s.mb[e][:, :],
                                     ACT.Copy).then_inc(a.o_hi, 1)

            def pair(j, first, last):
                for e in range(2):
                    h = 2 * j + e
                    start = first and e == 0
                    more = not (last and e == 1)
                    for i in range(8):
                        item_exp(nc, act, s, a, 8 * h + i, i % 4, start and i < 4)
                        if i >= 2 or not start:
                            item_copy(nc, act, s, a, 8 * h + i - 2, (i - 2) % 4, start and i < 4)
                        if i == 3:
                            if not start:
                                o_hi(h - 1, 1 - e)
                        if more:
                            if i == 3:
                                read_turn(h + 1 + NK, qT[:, 1 - e], qrT[:, 1 - e])
                            if i == 5:
                                cmp_exp(h + 1, 1 - e)
                            if i == 7:
                                cmp_read(h + 1, 1 - e, start)
            for t in range(NK):
                read_turn(t, qT[:, 0], kT[:, t // NG, t % NG])
                act.wait_ge(turned_read, 2 * t + 2)
            read_turn(NK, qT[:, 0], qrT[:, 0])
            cmp_exp(0, 0)
            cmp_read(0, 0, True)
            pair(0, True, False)
            with act.Fori(1, PAIRS - 1) as j:
                pair(j, False, False)
            pair(PAIRS - 1, False, True)
            for n in (2, 3):
                item_copy(nc, act, s, a, 8 * NSA - 4 + n, n, False)
            o_hi(NSA - 1, 1)

        @block.vector
        def _(dve):
            def gain(t, e, uses, row):
                dve.wait_ge(q_in[e], 16 * uses)
                if not isinstance(t, int) or t >= 2:
                    dve.wait_ge(turned, 2 * t - 2)
                nc.vector.tensor_tensor(qn[:, e], nq[:, e], s.gain_bc[:, row:row + 1, :].broadcast_to([P, TM, HD]),
                                        ALU.mult).then_inc(gained, 1)

            def cmp_first(h, e, j):
                mask = tabs[:, ds(N_MASK + 256 * (j // 2), 256)].rearrange("p (m n) -> p m n", m=TM)
                dve.wait_ge(c_s, h + 1)
                nc.vector.tensor_scalar(pc[:, e], mask, -NEG, NEG, ALU.mult, ALU.add).then_inc(c_v, 1)
                dve.wait_ge(c_v, 7 * h + 1)
                nc.vector.tensor_tensor(pc[:, e], s.mb[2][:, 0:256].rearrange("p (m n) -> p m n", m=TM), pc[:, e],
                                        ALU.add).then_inc(c_v, 1)
                dve.wait_ge(c_v, 7 * h + 2)
                nc.vector.tensor_reduce(cst[:, 0, :], pc[:, e], AX.X, ALU.max).then_inc(c_m, 1)
                dve.wait_ge(c_m, h + 1)
                nc.vector.tensor_tensor(pc[:, e], pc[:, e], cst[:, 0, :].unsqueeze(2).broadcast_to([P, TM, 64]),
                                        ALU.subtract).then_inc(c_v, 1)

            def cmp_second(h, e, j):
                mask = tabs[:, ds(N_MASK + 256 * (j // 2), 256)].rearrange("p (m n) -> p m n", m=TM)
                dve.wait_ge(c_e, h + 1)
                nc.vector.tensor_tensor(pc[:, e], pc[:, e], mask, ALU.mult).then_inc(c_v, 1)
                dve.wait_ge(c_v, 7 * h + 4)
                nc.vector.tensor_reduce(cst[:, 1, :], pc[:, e], AX.X, ALU.add).then_inc(c_v, 1)
                dve.wait_ge(c_v, 7 * h + 5)
                nc.vector.tensor_scalar(cst[:, 1, :], cst[:, 1, :], 1e-30, None, ALU.max).then_inc(c_r, 1)
                dve.wait_ge(c_r, 2 * h + 1)
                nc.vector.reciprocal(cst[:, 2, :], cst[:, 1, :]).then_inc(c_r, 1)
                dve.wait_ge(c_r, 2 * h + 2)
                nc.vector.tensor_tensor(cst[:, 3, :], cst[:, 2, :], s.gates[:, :, ds(FOX + 3 * h, 1)].rearrange(
                    "p m o -> p (m o)"), ALU.mult).then_inc(c_v, 1)
                dve.wait_ge(c_v, 7 * h + 6)
                nc.vector.tensor_tensor(pc[:, e], pc[:, e], cst[:, 3, :].unsqueeze(2).broadcast_to([P, TM, 64]),
                                        ALU.mult).then_inc(c_v, 1)

            c_m, c_r = sem("cmp_max"), sem("cmp_r")

            def o_lo(h, e):
                dve.wait_ge(a.o_hi, h + 1)
                nc.vector.tensor_tensor(s.act_lo[:, ds(FOX + h, 1), :].rearrange("p o t -> p (o t)"), s.mb[e][:, :],
                                        s.act_hi[:, ds(FOX + h, 1), :].rearrange("p o t -> p (o t)").bitcast(F32),
                                        ALU.subtract).then_inc(a.o_lo, 1)

            def gate(h, br, n):
                return s.gates[:, n, ds(FOX + 3 * h + 1 + br, 1)]

            def pair(j, first, last):
                for e in range(2):
                    h = 2 * j + e
                    start = first and e == 0
                    more = not (last and e == 1)
                    for i in range(8):
                        br, n = i // 4, i % 4
                        I = 8 * h + i
                        item_max(nc, dve, s, a, I, n)
                        if i >= 1 or not start:
                            item_reciprocal(nc, dve, s, a, I - 1, (n - 1) % 4)
                            item_normalise(nc, dve, s, a, I - 1, (n - 1) % 4,
                                           gate(h, (i - 1) // 4, (n - 1) % 4) if i else gate(h - 1, 1, 3))
                        if i == 4 and not start:
                            o_lo(h - 1, 1 - e)
                        if more:
                            if i == 0:
                                gain(h + 1 + NK, 1 - e, NK // 2 + j + e + 1, 0)
                            if i == 5:
                                cmp_first(h + 1, 1 - e, j + e)
                            if i == 6:
                                cmp_second(h + 1, 1 - e, j + e)
            for t in range(NK):
                gain(t, t % 2, t // 2 + 1, 1 + t // NG)
            gain(NK, 0, NK // 2 + 1, 0)
            dve.wait_ge(tabs_in, 16)
            cmp_first(0, 0, 0)
            cmp_second(0, 0, 0)
            pair(0, True, False)
            with dve.Fori(1, PAIRS - 1) as j:
                pair(j, False, False)
            pair(PAIRS - 1, False, True)
            item_reciprocal(nc, dve, s, a, 8 * NSA - 1, 3)
            item_normalise(nc, dve, s, a, 8 * NSA - 1, 3, gate(NSA - 1, 1, 3))
            o_lo(NSA - 1, 1)



def phase_out(nc, A, s):
    with ExitStack() as ctx:
        gated = ctx.enter_context(nc.sbuf_tensor("out_gated", [P, 2, 512], F32))
        sem = s.sem
        x_in, gated_ready, added = sem("x2_in"), sem("out_gated_ready"), sem("out_added")

        block = ctx.enter_context(nc.Block())

        @block.sync
        def _(sp):
            for m in range(TM):
                sp.dma_start(s.x2[:, m, :], A.x[0, m * P:(m + 1) * P, :]).then_inc(x_in, 16)
            with sp.Fori(0, 3) as n:
                for u in range(4):
                    load_unit(sp, s, PAIR_OUT + 2 * n + 2 + u // 2, u % 2, w_out_unit(A, n + 1, u))
            for u in range(4):
                load_unit(sp, s, PAIR_FF + u // 2, u % 2, w_up_unit(A, 0, u))

        @block.tensor
        def _(pe):
            with pe.Fori(0, 4) as n:
                for u in range(4):
                    rows_unit(nc, pe, s, PAIR_OUT + 2 * n + u // 2, u % 2, s.act_hi, s.act_lo, 4 * u, u == 0, u == 3,
                              ROUND_OUT + n)

        @block.scalar
        def _(act):
            with act.Fori(0, 4) as n:
                for u in range(4):
                    split_hi(nc, act, s, PAIR_OUT + 2 * n + u // 2 + 1, u % 2)

        @block.vector
        def _(dve):
            def body(n, first):
                for u in range(3):
                    split_lo(nc, dve, s, PAIR_OUT + 2 * n + u // 2 + 1, u % 2)
                for m in range(TM):
                    await_bank(dve, s, NB_IN + n, m, 2 * PAIR_OUT + 4 * n + 3)
                    if not first or m >= 2:
                        dve.wait_ge(added, 4 * n + m - 1)
                    nc.vector.tensor_tensor(gated[:, m % 2, :], s.gb[m][:, :], s.gate_bc[0][:, ds(n * 512, 512)],
                                            ALU.mult).then_inc(s.bank_free, 1)
                split_lo(nc, dve, s, PAIR_OUT + 2 * n + 2, 1)
            body(0, True)
            with dve.Fori(1, 4) as n:
                body(n, False)

        @block.gpsimd
        def _(pool):
            pool.wait_ge(x_in, 64)
            with pool.Fori(0, 4) as n:
                for m in range(TM):
                    pool.wait_ge(s.bank_free, 4 * (ROUND_OUT + n) + m + 1)
                    part = s.x2[:, m, ds(n * 512, 512)]
                    nc.gpsimd.tensor_tensor(part, part, gated[:, m % 2, :], ALU.add).then_inc(added, 1)



def phase_norm2(nc, A, s):
    with ExitStack() as ctx:
        sb = lambda name, shape, dt=F32: ctx.enter_context(nc.sbuf_tensor(name, shape, dt))
        sem = s.sem
        xn = sb("xn2", [P, TM, D])
        tmp = s.gate_bc[0][:, :].rearrange("p (e t) -> p e t", e=4)
        ssq = sb("ssq2", [P, 16])
        sq_done, ms_ready, rms_ready, rstd_ready, xn_ready = (sem("sq2"), sem("ms2"), sem("rms2"), sem("rstd2"),
                                                              sem("xn2_ready"))
        h_turned, h_hi, h_lo = sem("h2_turned"), sem("h2_hi"), sem("h2_lo")

        block = ctx.enter_context(nc.Block())

        @block.scalar
        def _(act):
            for m in range(TM):
                nc.scalar.activation(xn[:, m, :], s.x2[:, m, :], ACT.Square, accum_out=ssq[:, m:m + 1]).then_inc(sq_done, 1)
            act.wait_ge(ms_ready, 1)
            nc.scalar.activation(ssq[:, 8:12], ssq[:, 4:8], ACT.Sqrt).then_inc(rms_ready, 1)
            modulated_scalar(nc, act, s, tmp, ROUND_NORM2, h_hi)

        @block.tensor
        def _(pe):
            pe.wait_ge(xn_ready, TM)
            modulated_tensor(nc, pe, s, xn, ROUND_NORM2, h_turned)

        @block.vector
        def _(dve):
            dve.wait_ge(sq_done, TM)
            nc.vector.tensor_scalar(ssq[:, 4:8], ssq[:, 0:4], 1.0 / D, EPS, ALU.mult, ALU.add).then_inc(ms_ready, 1)
            dve.wait_ge(rms_ready, 1)
            nc.vector.reciprocal(ssq[:, 12:16], ssq[:, 8:12]).then_inc(rstd_ready, 1)
            dve.wait_ge(rstd_ready, 1)
            for m in range(TM):
                nc.vector.tensor_scalar(xn[:, m, :], s.x2[:, m, :], ssq[:, 12 + m:13 + m], None,
                                        ALU.mult).then_inc(xn_ready, 1)
            modulated_vector(nc, dve, s, tmp, s.mod[:, 2, :], s.mod[:, 3, :], ROUND_NORM2, h_turned, h_hi, h_lo)



def phase_mlp(nc, A, s):
    with ExitStack() as ctx:
        sb = lambda name, shape, dt=F32: ctx.enter_context(nc.sbuf_tensor(name, shape, dt))
        sem = s.sem
        u_hi, u_lo = sb("u_hi", [P, 8, T], F32R), sb("u_lo", [P, 8, T], F32R)
        spare = s.gate_bc[0][:, :].rearrange("p (a e t) -> p a e t", a=2, e=2)
        relu, squ = spare[:, 0], spare[:, 1]
        gated = sb("mlp_gated", [P, 2, 512])
        sq_n, hi_n, lo_n, added = sem("relu_sq_n"), sem("u_hi_n"), sem("u_lo_n"), sem("mlp_added")
        out_stored = sem("out_stored")

        block = ctx.enter_context(nc.Block())

        @block.sync
        def _(sp):
            def down_loads(c, n):
                for u in range(2):
                    load_unit(sp, s, PAIR_FF + 8 * c + 4 + n, u, w_down_unit(A, c, n, u))

            def up_loads(c, b):
                for u in range(4):
                    load_unit(sp, s, PAIR_FF + 8 * c + 2 * b + u // 2, u % 2, w_up_unit(A, 2 * c + b, u))
            up_loads(0, 1)
            with sp.Fori(0, CHUNKS - 1) as c:
                with sp.Fori(0, 4) as n:
                    down_loads(c, n)
                with sp.Fori(0, 2) as b:
                    up_loads(c + 1, b)
            with sp.Fori(0, 4) as n:
                down_loads(CHUNKS - 1, n)
            for m in range(TM):
                sp.wait_ge(added, 16 * CHUNKS - 3 + m)
                sp.dma_start(A.out[0, m * P:(m + 1) * P, :], s.x2[:, m, :]).then_inc(out_stored, 16)
            sp.wait_ge(out_stored, 64)

        @block.tensor
        def _(pe):
            with pe.Fori(0, CHUNKS) as c:
                with pe.Fori(0, 2) as b:
                    for u in range(4):
                        cols_unit(nc, pe, s, PAIR_FF + 8 * c + 2 * b + u // 2, u % 2, 4 * u, u == 0, u == 3,
                                  ROUND_FF + 6 * c + b)
                with pe.Fori(0, 4) as n:
                    for u in range(2):
                        pe.wait_ge(lo_n, 8 * c + 4 * u + 4)
                        rows_unit(nc, pe, s, PAIR_FF + 8 * c + 4 + n, u, u_hi, u_lo, 4 * u, u == 0, u == 1,
                                  ROUND_FF + 6 * c + 2 + n)

        @block.scalar
        def _(act):
            def up(c, b, first):
                for u in range(3):
                    split_hi(nc, act, s, PAIR_FF + 8 * c + 2 * b + u // 2 + 1, u % 2)
                for m in range(4):
                    t = 8 * c + 4 * b + m
                    await_bank(act, s, NB_IN + 4 + 6 * c + b, m, 2 * PAIR_FF + 16 * c + 4 * b + 3)
                    if not first or m >= 2:
                        act.wait_ge(sq_n, t - 1)
                    nc.scalar.activation(relu[:, m % 2, :], s.gb[m][:, :], ACT.Relu).then_inc(s.bank_free, 1)
                    if m >= 1:
                        hi(t - 1, b, m - 1)
                hi(8 * c + 4 * b + 3, b, 3)
                split_hi(nc, act, s, PAIR_FF + 8 * c + 2 * b + 2, 1)

            def hi(t, b, m):
                act.wait_ge(sq_n, t + 1)
                nc.scalar.activation(u_hi[:, ds(4 * b + m, 1), :].rearrange("p o t -> p (o t)"), squ[:, m % 2, :],
                                     ACT.Copy).then_inc(hi_n, 1)

            def down(c, n, slots=(0, 1)):
                for u in slots:
                    split_hi(nc, act, s, PAIR_FF + 8 * c + 4 + n + 1, u)

            def chunk(c, first):
                if first:
                    up(c, 0, True)
                    up(c, 1, False)
                else:
                    with act.Fori(0, 2) as b:
                        up(c, b, False)
            chunk(0, True)
            with act.Fori(0, 4) as n:
                down(0, n)
            with act.Fori(1, CHUNKS - 1) as c:
                chunk(c, False)
                with act.Fori(0, 4) as n:
                    down(c, n)
            chunk(CHUNKS - 1, False)
            with act.Fori(0, 3) as n:
                down(CHUNKS - 1, n)

        @block.vector
        def _(dve):
            def up(c, b, first):
                for u in range(3):
                    split_lo(nc, dve, s, PAIR_FF + 8 * c + 2 * b + u // 2 + 1, u % 2)
                for m in range(4):
                    t = 8 * c + 4 * b + m
                    dve.wait_ge(s.bank_free, 4 * (ROUND_FF + 6 * c + b) + m + 1)
                    if not first or m >= 2:
                        dve.wait_ge(lo_n, t - 1)
                    nc.vector.tensor_tensor(squ[:, m % 2, :], relu[:, m % 2, :], relu[:, m % 2, :], ALU.mult).then_inc(sq_n, 1)
                    if m >= 1:
                        lo(t - 1, b, m - 1)
                lo(8 * c + 4 * b + 3, b, 3)
                split_lo(nc, dve, s, PAIR_FF + 8 * c + 2 * b + 2, 1)

            def lo(t, b, m):
                dve.wait_ge(hi_n, t + 1)
                nc.vector.tensor_tensor(u_lo[:, ds(4 * b + m, 1), :].rearrange("p o t -> p (o t)"), squ[:, m % 2, :],
                                        u_hi[:, ds(4 * b + m, 1), :].rearrange("p o t -> p (o t)").bitcast(F32),
                                        ALU.subtract).then_inc(lo_n, 1)

            def down(c, n, first, last=False):
                if not last:
                    split_lo(nc, dve, s, PAIR_FF + 8 * c + 4 + n + 1, 0)
                for m in range(TM):
                    e = 16 * c + 4 * n + m
                    await_bank(dve, s, NB_IN + 4 + 6 * c + 2 + n, m, 2 * PAIR_FF + 16 * c + 8 + 2 * n + 1)
                    if not first or m >= 2:
                        dve.wait_ge(added, e - 1)
                    nc.vector.tensor_tensor(gated[:, m % 2, :], s.gb[m][:, :], s.gate_bc[1][:, ds(n * 512, 512)],
                                            ALU.mult).then_inc(s.bank_free, 1)
                if not last:
                    split_lo(nc, dve, s, PAIR_FF + 8 * c + 4 + n + 1, 1)
            up(0, 0, True)
            up(0, 1, False)
            down(0, 0, True)
            with dve.Fori(1, 4) as n:
                down(0, n, False)
            with dve.Fori(1, CHUNKS - 1) as c:
                with dve.Fori(0, 2) as b:
                    up(c, b, False)
                with dve.Fori(0, 4) as n:
                    down(c, n, False)
            with dve.Fori(0, 2) as b:
                up(CHUNKS - 1, b, False)
            with dve.Fori(0, 3) as n:
                down(CHUNKS - 1, n, False)
            down(CHUNKS - 1, 3, False, last=True)

        @block.gpsimd
        def _(pool):
            with pool.Fori(0, CHUNKS) as c:
                with pool.Fori(0, 4) as n:
                    for m in range(TM):
                        pool.wait_ge(s.bank_free, 4 * (ROUND_FF + 6 * c + 2 + n) + m + 1)
                        part = s.x2[:, m, ds(n * 512, 512)]
                        nc.gpsimd.tensor_tensor(part, part, gated[:, m % 2, :], ALU.add).then_inc(added, 1)


def build(nc, A):
    with ExitStack() as ctx:
        sb = lambda name, shape, dt=F32: ctx.enter_context(nc.sbuf_tensor(name, shape, dt))
        sem = lambda name: ctx.enter_context(nc.semaphore(name))
        s = Names()
        s.sem = sem
        s.act_hi, s.act_lo = sb("act_hi", [P, KT, T], F32R), sb("act_lo", [P, KT, T], F32R)
        s.w_raw = sb("w_raw", [P, 2, 4, 512])
        s.w_hi, s.w_lo = sb("w_hi", [P, 2, 4, 512], F32R), sb("w_lo", [P, 2, 4, 512], F32R)
        s.base = sb("base_consts", [P, C_END])
        s.ident = s.base[:, C_ID:C_ID + P]
        s.ones = sb("ones", [P, P])
        s.ident_bf, s.causal_bf = sb("ident_bf", [P, P], mybir.dt.bfloat16), sb("causal_bf", [P, P], mybir.dt.bfloat16)
        s.cols1, s.cols2 = sb("cols1", [P, P]), sb("cols2", [P, P])
        s.c_col = sb("c_col", [P, 4, KT])
        s.mod = sb("mod", [P, 6, KT])
        s.fq_gain = sb("fq_gain", [P, 1])
        s.gain_bc = sb("gain_bc", [P, 3, HD])
        s.cum, s.auxR = sb("cum", [NZ, T]), sb("auxR", [NZ, T])
        s.gates = sb("gates", [P, TM, NZ])
        s.kcT, s.vc = sb("kcT", [P, 64]), sb("vc", [64, HD])
        s.gb = [ctx.enter_context(nc.psum_tensor(f"gemm_bank{m}", [P, 512], F32)) for m in range(4)]
        s.mb = [ctx.enter_context(nc.psum_tensor(f"misc_bank{m}", [P, 512], F32)) for m in range(4)]
        s.w_landed = [sem(f"w_landed{i}") for i in range(2)]
        s.w_hi_ready, s.w_lo_ready, s.unit_used = sem("w_hi_ready"), sem("w_lo_ready"), sem("unit_used")
        s.bank_done, s.bank_free = sem("bank_done"), sem("bank_free")
        s.proj_stored = [sem(f"proj_stored{m}") for m in range(TM)]
        s.gates_ready, s.cmp_ready = sem("gates_ready"), sem("cmp_ready")
        s.proj = nc.dram_tensor("proj", [NB_IN, TM, P, 512], F32).ap()

        phase_norm1(nc, A, s)
        with nc.sbuf_tensor("gate2_bc", [P, D], F32) as gate2:
            with nc.sbuf_tensor("gate1_bc", [P, D], F32) as gate1:
                s.gate_bc = [gate1, gate2]
                phase_project(nc, A, s)
                phase_compress(nc, A, s)
                phase_fox(nc, A, s)
                phase_nsa(nc, A, s)
                with nc.sbuf_tensor("x2", [P, TM, D], F32) as x2:
                    s.x2 = x2
                    phase_out(nc, A, s)
                    phase_norm2(nc, A, s)
                    phase_mlp(nc, A, s)


INPUTS = ["x", "c", "w_ada", "b_ada", "norm1_g", "w_in", "b_forget", "fox_q_norm", "fox_k_norm", "nsa_q_norm",
          "cmp_k_norm", "slc_k_norm", "win_k_norm", "cmp_pe_k", "cmp_w1_k", "cmp_w2_k", "cmp_pe_v", "cmp_w1_v",
          "cmp_w2_v", "w_out", "norm2_g", "w_up", "w_down"]


def kernel(**inputs):
    import concourse.bacc as _bacc
    from concourse.bass_utils import run_bass_kernel_spmd as _run

    nc = _bacc.Bacc("TRN2", target_bir_lowering=False, num_devices=1)
    base, nsa_tabs = host_constants()
    arrays = {name: np.ascontiguousarray(inputs[name]) for name in INPUTS}
    arrays["base"], arrays["nsa_tabs"] = base, nsa_tabs
    fields = {name: nc.dram_tensor("in_" + name, a.shape, mybir.dt.from_np(a.dtype), kind="ExternalInput").ap()
              for name, a in arrays.items()}
    fields["out"] = nc.dram_tensor("out", (1, T, D), F32, kind="ExternalOutput").ap()
    A = namedtuple("Arrays", fields)(**fields)
    build(nc, A)
    r = _run(nc, [{"in_" + name: a for name, a in arrays.items()}], core_ids=[0])
    return r.results[0]["out"]
```

```python
from collections import namedtuple
from contextlib import ExitStack

import numpy as np

import concourse.bass as bass
from concourse import mybir

F32 = mybir.dt.float32
F32R = mybir.dt.float32r
ALU = mybir.AluOpType
ACT = mybir.ActivationFunctionType
AX = mybir.AxisListType
ds = bass.ds


class Names:
    pass

P = 128
T = 512
TM = T // P
D = 2048
KT = D // P
HD = 128
FOX = 8
NSA = 8
NG = 2
FF = 4 * D
CMP_LEN, CMP_STRIDE = 32, 16
NCMP = (T - CMP_LEN) // CMP_STRIDE + 1
CW = 32
CMP_HID = 2 * HD
NB_IN = 11
FOX_COLS = 3 * FOX * HD
FZ = FOX_COLS
GZ = FZ + FOX + 5 * 512
NZ = 40
EPS = 1e-6
SCALE = HD ** -0.5
NEG = -1e30

C_ID, C_CAUSAL, C_FLAG, C_NFLAG, C_M1, C_M2, C_N1, C_N2, C_END = 0, 128, 256, 300, 344, 352, 360, 361, 362
N_MASK, N_NEG, N_COS, N_SIN, N_END = 0, 512, 1024, 1536, 2048

PAIR_CMP = 2 * NB_IN
PAIR_OUT = PAIR_CMP + 4
PAIR_FF = PAIR_OUT + 8
CHUNKS = 8
PAIR_END = PAIR_FF + 8 * CHUNKS
ROUND_OUT = NB_IN
ROUND_FF = ROUND_OUT + 4


def host_constants():
    p = np.arange(P)[:, None]
    base = np.zeros((P, C_END), np.float32)
    base[:, C_ID:C_ID + P] = np.eye(P)
    base[:, C_CAUSAL:C_CAUSAL + P] = np.where(np.arange(P)[None, :] <= p, 0.0, NEG)
    flag = np.zeros((NB_IN, 4), np.float32)
    flag[[0, 1, 2, 3, 6, 7]] = 1.0
    flag[9:11, 0:2] = 1.0
    base[:, C_FLAG:C_FLAG + 44] = flag.reshape(1, 44)
    base[:, C_NFLAG:C_NFLAG + 44] = 1.0 - flag.reshape(1, 44)
    h = np.arange(FOX)[None, :]
    base[:, C_M1:C_M1 + FOX] = p == h
    base[:, C_M2:C_M2 + FOX] = -1.0 * (p == 32 + h)
    base[:, C_N1] = p[:, 0] >= 32
    base[:, C_N2] = p[:, 0] < FOX

    nsa = np.zeros((P, N_END), np.float32)
    m = np.arange(TM)[None, :, None]
    n = np.arange(NG * CW)[None, None, :]
    t = m * P + p[:, :, None]
    for g in range(NG):
        see = (n // CW == g) & (n % CW < NCMP) & ((n % CW) * CMP_STRIDE + CMP_LEN - 1 <= t)
        nsa[:, N_MASK + g * 256:N_MASK + (g + 1) * 256] = see.reshape(P, 256)
        nsa[:, N_NEG + g * 256:N_NEG + (g + 1) * 256] = np.where(see, 0.0, NEG).reshape(P, 256)
    half = HD // 2
    inv = np.float32(10000.0) ** (-np.arange(half, dtype=np.float32) / np.float32(half))
    ang = (np.arange(T, dtype=np.float32)[:, None] * inv[None, :]).astype(np.float32)
    cos, sin = np.cos(ang), np.sin(ang)
    cos2 = np.concatenate([cos, cos], 1).reshape(TM, P, HD).transpose(1, 0, 2)
    sin2 = np.concatenate([-sin, sin], 1).reshape(TM, P, HD).transpose(1, 0, 2)
    nsa[:, N_COS:N_COS + 512] = cos2.reshape(P, 512)
    nsa[:, N_SIN:N_SIN + 512] = sin2.reshape(P, 512)
    return base, nsa



def load_unit(sp, s, pair, slot, src, first=False):
    if not first:
        sp.wait_ge(s.w_lo_ready, 2 * pair + slot - 1)
    sp.dma_start(s.w_raw[:, slot], src).then_inc(s.w_landed[slot], 16)


def split_hi(nc, act, s, pair, slot, first=False):
    act.wait_ge(s.w_landed[slot], 16 * (pair + 1))
    if not first:
        act.wait_ge(s.unit_used, 2 * pair + slot - 1)
    nc.scalar.activation(s.w_hi[:, slot], s.w_raw[:, slot], ACT.Copy).then_inc(s.w_hi_ready, 1)


def split_lo(nc, dve, s, pair, slot):
    dve.wait_ge(s.w_hi_ready, 2 * pair + slot + 1)
    nc.vector.tensor_tensor(s.w_lo[:, slot], s.w_raw[:, slot], s.w_hi[:, slot].bitcast(F32),
                            ALU.subtract).then_inc(s.w_lo_ready, 1)


def await_bank(eng, s, product_round, m, last_unit):
    if m < 3:
        eng.wait_ge(s.bank_done, 3 * product_round + m + 1)
    else:
        eng.wait_ge(s.unit_used, last_unit + 1)


def three_products(nc, out, a_hi, a_lo, b_hi, b_lo, start, stop):
    nc.tensor.matmul(out, a_hi, b_hi, start=start, stop=False)
    nc.tensor.matmul(out, a_hi, b_lo, start=False, stop=False)
    return nc.tensor.matmul(out, a_lo, b_hi, start=False, stop=stop)


def rows_unit(nc, pe, s, pair, slot, lhs_hi, lhs_lo, k0, first, last, round_):
    pe.wait_ge(s.w_lo_ready, 2 * pair + slot + 1)
    for m in range(TM):
        if first and not (isinstance(round_, int) and round_ == 0):
            pe.wait_ge(s.bank_free, 4 * round_ + m - 3)
        for kk in range(4):
            tok = slice(m * P, (m + 1) * P)
            mm = three_products(nc, s.gb[m][:, :], lhs_hi[:, k0 + kk, tok], lhs_lo[:, k0 + kk, tok],
                                s.w_hi[:, slot, kk, :], s.w_lo[:, slot, kk, :],
                                first and kk == 0, last and kk == 3)
        if last and m < 3:
            mm.then_inc(s.bank_done, 1)
    mm.then_inc(s.unit_used, 1)


def cols_unit(nc, pe, s, pair, slot, k0, first, last, round_):
    pe.wait_ge(s.w_lo_ready, 2 * pair + slot + 1)
    for m in range(4):
        if first and not (isinstance(round_, int) and round_ == 0):
            pe.wait_ge(s.bank_free, 4 * round_ + m - 3)
        for kk in range(4):
            col = slice(m * P, (m + 1) * P)
            mm = three_products(nc, s.gb[m][:, :], s.w_hi[:, slot, kk, col], s.w_lo[:, slot, kk, col],
                                s.act_hi[:, k0 + kk, :], s.act_lo[:, k0 + kk, :],
                                first and kk == 0, last and kk == 3)
        if last and m < 3:
            mm.then_inc(s.bank_done, 1)
    mm.then_inc(s.unit_used, 1)



def modulate_tensor(nc, pe, s, xn, g, q):
    for k in range(4 * g, 4 * g + 4):
        if k >= len(q.banks):
            pe.wait_ge((q.a_done, q.b_done)[k % 2], (k - len(q.banks)) // 2 + 1)
        for m in range(TM):
            mm = nc.tensor.transpose(q.banks[k % len(q.banks)][:, m * P:(m + 1) * P], xn[:, m, k * P:(k + 1) * P], s.ident)
        mm.then_inc(q.turned, 1)


def tile(t, k):
    return t[:, ds(k, 1), :].rearrange("p o t -> p (o t)")


def modulate_scalar(nc, act, s, g, q):
    for e in range(0, 4, 2):
        act.wait_ge(q.turned, 4 * g + e + 1)
        if e == 0 and q.mod_ready is not None:
            act.wait_ge(q.mod_ready, g + 1)
        if not isinstance(g, int) or g > 0:
            act.wait_ge(q.lo, 4 * g + e - 3)
        nc.scalar.activation(q.tmp[:, e, :], q.banks[e % len(q.banks)][:, :], ACT.Identity, scale=q.a[:, ds(4 * g + e, 1)],
                             bias=q.b[:, ds(4 * g + e, 1)]).then_inc(q.a_done, 1)
        act.wait_ge(q.a_done, 2 * g + e // 2 + 1)
        nc.scalar.activation(tile(s.act_hi, 4 * g + e), q.tmp[:, e, :], ACT.Copy).then_inc(q.hi, 1)
        act.wait_ge(q.b_done, 2 * g + e // 2 + 1)
        nc.scalar.activation(tile(s.act_hi, 4 * g + e + 1), q.tmp[:, e + 1, :], ACT.Copy).then_inc(q.hi, 1)


def modulate_vector(nc, dve, s, g, q):
    for e in range(0, 4, 2):
        dve.wait_ge(q.turned, 4 * g + e + 2)
        nc.vector.tensor_scalar(q.tmp[:, e + 1, :], q.banks[(e + 1) % len(q.banks)][:, :], q.a[:, ds(4 * g + e + 1, 1)],
                                q.b[:, ds(4 * g + e + 1, 1)], ALU.mult, ALU.add).then_inc(q.b_done, 1)
        for o in (e, e + 1):
            dve.wait_ge(q.hi, 4 * g + o + 1)
            nc.vector.tensor_tensor(tile(s.act_lo, 4 * g + o), q.tmp[:, o, :], tile(s.act_hi, 4 * g + o).bitcast(F32),
                                    ALU.subtract).then_inc(q.lo, 1)


def modulate_state(sem, tag, banks, tmp, a, b):
    q = Names()
    q.banks, q.tmp, q.a, q.b = banks, tmp, a, b
    q.turned, q.a_done, q.b_done = sem(tag + "turned"), sem(tag + "even_done"), sem(tag + "odd_done")
    q.hi, q.lo, q.mod_ready = sem(tag + "hi"), sem(tag + "lo"), None
    return q


def w_in_unit(A, block, u):
    w = A.w_in.rearrange("l (k p) n -> p (l k) n", p=P)
    return w[:, 4 * u:4 * u + 4, ds(block, 512)]


def w_cmp_unit(w1, u):
    return w1.rearrange("l (k p) n -> p (l k) n", p=P)[:, 8 * u:8 * u + 8, :].rearrange(
        "p (a b) n -> p a b n", b=2)


def w_out_unit(A, n, u):
    return A.w_out.rearrange("l (k p) n -> p (l k) n", p=P)[:, 4 * u:4 * u + 4, ds(n * 512, 512)]


def w_up_unit(A, block, u):
    return A.w_up.rearrange("l (k p) n -> p (l k) n", p=P)[:, 4 * u:4 * u + 4, ds(block * 512, 512)]


def w_down_unit(A, chunk, n, u):
    w = A.w_down.rearrange("l (k p) n -> p (l k) n", p=P)
    return w[:, ds(chunk * 8 + 4 * u, 4), ds(n * 512, 512)]



def phase_start(nc, A, s):
    with ExitStack() as ctx:
        sb = lambda name, shape, dt=F32: ctx.enter_context(nc.sbuf_tensor(name, shape, dt))
        sem = s.sem
        SLOTS, STEPS = 4, 8
        xn = sb("xn", [P, TM, D])
        ada_raw = sb("ada1_raw", [P, SLOTS, 2, 2, 512])
        acc = sb("ada1_acc", [P, 2, 2, 512])
        tmp = sb("mod1_tmp", [P, 4, T])
        rows = s.wz[:, 0:2 * P].rearrange("p (e c) -> p e c", e=2)
        ssq = sb("ssq1", [P, 16])

        consts_in, rows_in = sem("consts_in"), sem("rows_in")
        gains_in = sem("gains_in")
        x_in = [sem(f"x_in{m}") for m in range(TM)]
        ada_in = [sem(f"ada1_in{i}") for i in range(SLOTS)]
        ada_used, rows_zero = sem("ada1_used"), sem("rows_zero")
        cols_done, cols_read, c_exp, c_ready = sem("cols_done"), sem("cols_read"), sem("c_exp"), sem("c_ready")
        sq_done, ms_ready, rms_ready, rstd_ready = sem("sq1"), sem("ms1"), sem("rms1"), sem("rstd1")
        xn_ready, mod_sums, mod_part = sem("xn1_ready"), sem("mod1_sums"), sem("mod1_part")
        ones_set, scaled = sem("ones_set"), sem("gain_scaled")
        q = modulate_state(sem, "h1_", s.mb[0:2], tmp, s.mod[:, 0, :], s.mod[:, 1, :])
        q.mod_ready = sem("h1_mod_ready")
        ada = A.w_ada.rearrange("l (k p) (s n) -> p (l k) s n", p=P, n=D)

        block = ctx.enter_context(nc.Block())

        @block.sync
        def _(sp):
            sp.dma_start(s.base[:, :], A.base).then_inc(consts_in, 16)
            sp.dma_start(rows[0:96, 0, :], A.b_ada.rearrange("l (r c) -> (l r) c", c=P)).then_inc(rows_in, 16)
            sp.dma_start(rows[96:112, 0, :], A.norm1_g.rearrange("l (r c) -> (l r) c", c=P)).then_inc(rows_in, 16)
            sp.dma_start(rows[112:128, 0, :], A.norm2_g.rearrange("l (r c) -> (l r) c", c=P)).then_inc(rows_in, 16)
            sp.wait_ge(rows_zero, 1)
            sp.dma_start(rows[0:16, 1, :], A.c.rearrange("l (r c) -> (l r) c", c=P)).then_inc(rows_in, 16)
            for r, v in enumerate((A.fox_q_norm, A.fox_k_norm, A.nsa_q_norm, A.cmp_k_norm)):
                sp.dma_start(rows[16 + r:17 + r, 1, :], v).then_inc(rows_in, 16)
            sp.dma_start(rows[22:54, 1, :], A.cmp_pe_k.rearrange("l r c -> (l r) c")).then_inc(rows_in, 16)
            sp.dma_start(rows[54:86, 1, :], A.cmp_pe_v.rearrange("l r c -> (l r) c")).then_inc(rows_in, 16)

            def load_ada(g, k, used):
                if used is not None:
                    sp.wait_ge(ada_used, used)
                for r in range(2):
                    sp.dma_start(ada_raw[:, k % SLOTS, r], ada[:, 2 * k + r, 0:2, ds(g * 512, 512)]).then_inc(
                        ada_in[k % SLOTS], 16)

            for k in range(SLOTS):
                load_ada(0, k, None)
            for m in range(TM):
                sp.dma_start(xn[:, m, :], A.x[0, m * P:(m + 1) * P, :]).then_inc(x_in[m], 16)
            for r, v in enumerate((A.nsa_q_norm, A.slc_k_norm, A.win_k_norm)):
                sp.dma_start(s.gain_bc[:, r, :], v[0, :].partition_broadcast(P)).then_inc(gains_in, 16)
            for k in range(SLOTS, STEPS):
                load_ada(0, k, 2 * (k - SLOTS + 1))
            for u in range(2):
                load_unit(sp, s, 0, u, w_in_unit(A, 0, u), first=True)
            for g in range(1, 4):
                for k in range(STEPS):
                    load_ada(g, k, 2 * (STEPS * g + k - SLOTS + 1))
                    if k == 6:
                        load_unit(sp, s, (g + 1) // 2, (g + 1) % 2, w_in_unit(A, 0, g + 1) if g < 3 else w_in_unit(A, 512, 0))
            for u in (1, 2):
                load_unit(sp, s, 2 + u // 2, u % 2, w_in_unit(A, 512, u))

        @block.gpsimd
        def _(pool):
            nc.gpsimd.memset(rows[:, 1, :], 0.0).then_inc(rows_zero, 1)
            nc.gpsimd.memset(s.ones[:, :], 1.0).then_inc(ones_set, 1)
            nc.gpsimd.memset(s.wz[:, KT * NZ:KT * NZ + P], 0.0).then_inc(ones_set, 1)

        @block.scalar
        def _(act):
            act.wait_ge(cols_done, 1)
            nc.scalar.activation(s.cols1[:, :], s.mb[0][:, 0:P], ACT.Copy).then_inc(cols_read, 1)
            nc.scalar.activation(s.cols2[:, :], s.mb[0][:, P:2 * P], ACT.Copy).then_inc(cols_read, 1)
            act.wait_ge(cols_read, 2)
            nc.scalar.activation(s.c_col[:, 0, :], s.cols2[:, 0:KT], ACT.Exp, scale=-1.0).then_inc(c_exp, 1)
            junk = tmp[:, :, :].rearrange("p e t -> p (e t)")
            for m in range(TM):
                act.wait_ge(x_in[m], 16)
                nc.scalar.activation(junk, xn[:, m, :], ACT.Square, accum_out=ssq[:, m:m + 1]).then_inc(sq_done, 1)
                act.wait_ge(sq_done, m + 1)
            act.wait_ge(ms_ready, 1)
            nc.scalar.activation(ssq[:, 8:12], ssq[:, 4:8], ACT.Sqrt).then_inc(rms_ready, 1)
            split_hi(nc, act, s, 0, 0, first=True)
            for g in range(4):
                if g:
                    split_hi(nc, act, s, g // 2, g % 2, first=g == 1)
                modulate_scalar(nc, act, s, g, q)
            split_hi(nc, act, s, 2, 0)

        @block.tensor
        def _(pe):
            pe.wait_ge(consts_in, 16)
            pe.wait_ge(rows_in, 16 * 10)
            nc.tensor.transpose(s.mb[0][:, 0:P], rows[:, 0, :], s.ident)
            nc.tensor.transpose(s.mb[0][:, P:2 * P], rows[:, 1, :], s.ident).then_inc(cols_done, 1)
            pe.wait_ge(xn_ready, TM)
            pe.wait_ge(ones_set, 2)
            for g in range(4):
                pe.wait_ge(ada_used, 2 * STEPS * (g + 1))
                if g:
                    pe.wait_ge(q.mod_ready, g)
                for sct in range(2):
                    for k in range(4):
                        mm = nc.tensor.matmul(s.mb[2][:, sct * 4 + k:sct * 4 + k + 1],
                                              acc[:, g % 2, sct, k * P:(k + 1) * P], s.ones[:, 0:1], start=True, stop=True)
                mm.then_inc(mod_sums, 1)
                modulate_tensor(nc, pe, s, xn, g, q)
                pe.wait_ge(q.lo, 4 * g + 4)
                rows_unit(nc, pe, s, g // 2, g % 2, s.act_hi, s.act_lo, 4 * g, g == 0, g == 3, 0)

        @block.vector
        def _(dve):
            dve.wait_ge(c_exp, 1)
            nc.vector.tensor_scalar(s.c_col[:, 1, :], s.c_col[:, 0, :], 1.0, None, ALU.add).then_inc(c_ready, 1)
            dve.wait_ge(c_ready, 1)
            nc.vector.reciprocal(s.c_col[:, 2, :], s.c_col[:, 1, :]).then_inc(c_ready, 1)
            dve.wait_ge(c_ready, 2)
            nc.vector.tensor_tensor(s.c_col[:, 3, :], s.c_col[:, 2, :], s.cols2[:, 0:KT], ALU.mult).then_inc(c_ready, 1)
            nc.vector.tensor_copy(s.ident_bf[:, :], s.ident).then_inc(scaled, 1)
            nc.vector.tensor_copy(s.causal_bf[:, :], s.base[:, C_CAUSAL:C_CAUSAL + P]).then_inc(scaled, 1)
            nc.vector.tensor_scalar(s.fq_gain[:, :], s.cols2[:, 16:17], SCALE, None, ALU.mult).then_inc(scaled, 1)
            dve.wait_ge(c_ready, 3)

            def steps(g, ks):
                for k in ks:
                    dve.wait_ge(ada_in[k % SLOTS], 32 * (2 * g + k // SLOTS + 1))
                    for r in range(2):
                        part, c = acc[:, g % 2], s.c_col[:, 3, 2 * k + r:2 * k + r + 1]
                        if k + r == 0:
                            nc.vector.tensor_scalar(part, ada_raw[:, 0, 0], c, None, ALU.mult).then_inc(ada_used, 1)
                        else:
                            dve.wait_ge(ada_used, 2 * (STEPS * g + k) + r)
                            nc.vector.scalar_tensor_tensor(out=part, in0=ada_raw[:, k % SLOTS, r], scalar=c, in1=part,
                                                           op0=ALU.mult, op1=ALU.add).then_inc(ada_used, 1)

            steps(0, range(3))
            dve.wait_ge(sq_done, TM)
            nc.vector.tensor_scalar(ssq[:, 4:8], ssq[:, 0:4], 1.0 / D, EPS, ALU.mult, ALU.add).then_inc(ms_ready, 1)
            dve.wait_ge(rms_ready, 1)
            nc.vector.reciprocal(ssq[:, 12:16], ssq[:, 8:12]).then_inc(rstd_ready, 1)
            dve.wait_ge(rstd_ready, 1)
            for m in range(TM):
                nc.vector.tensor_scalar(xn[:, m, :], xn[:, m, :], ssq[:, 12 + m:13 + m], None,
                                        ALU.mult).then_inc(xn_ready, 1)
            dve.wait_ge(gains_in, 48)
            nc.vector.tensor_scalar(s.gain_bc[:, 0, :], s.gain_bc[:, 0, :], SCALE, None, ALU.mult).then_inc(scaled, 1)
            steps(0, range(3, STEPS))
            split_lo(nc, dve, s, 0, 0)
            for g in range(4):
                if g < 3:
                    steps(g + 1, range(2))
                dve.wait_ge(mod_sums, g + 1)
                c = slice(4 * g, 4 * g + 4)
                nc.vector.tensor_tensor(s.mod[:, 1, c], s.mb[2][:, 0:4], s.cols1[:, c], ALU.add).then_inc(mod_part, 1)
                nc.vector.tensor_tensor(s.mod[:, 4, c], s.mb[2][:, 4:8], s.cols1[:, KT + 4 * g:KT + 4 * g + 4],
                                        ALU.add).then_inc(mod_part, 1)
                dve.wait_ge(mod_part, 2 * g + 2)
                nc.vector.scalar_tensor_tensor(out=s.mod[:, 0, c], in0=s.mod[:, 4, c], scalar=1.0,
                                               in1=s.cols1[:, 96 + 4 * g:100 + 4 * g], op0=ALU.add,
                                               op1=ALU.mult).then_inc(q.mod_ready, 1)
                if g < 3:
                    steps(g + 1, range(2, 3))
                dve.wait_ge(q.mod_ready, g + 1)
                modulate_vector(nc, dve, s, g, q)
                if g < 3:
                    steps(g + 1, range(3, 5))
                    split_lo(nc, dve, s, (g + 1) // 2, (g + 1) % 2)
                    steps(g + 1, range(5, STEPS))
            split_lo(nc, dve, s, 2, 0)
            dve.wait_ge(scaled, 4)



def phase_project(nc, A, s):
    with ExitStack() as ctx:
        sb = lambda name, shape, dt=F32: ctx.enter_context(nc.sbuf_tensor(name, shape, dt))
        sem = s.sem
        ada_raw = sb("ada2_raw", [P, 2, D])
        acc = sb("ada2_acc", [P, 4, D])
        stage = sb("proj_stage", [P, TM, 512])
        sq = sb("proj_sq", [P, 2, 512])
        st = sb("proj_stats", [P, 4, 16])

        ada_in = [sem(f"ada2_in{i}") for i in range(2)]
        ada_used, acc_zero, bias_in = sem("ada2_used"), sem("acc2_zero"), sem("gate_bias_in")
        squared, summed = sem("proj_squared"), sem("proj_summed")
        ms, rms, rstd, normed = sem("proj_ms"), sem("proj_rms"), sem("proj_rstd"), sem("proj_normed")
        stored = s.proj_stored
        sum_ready, sum_read, col_done = sem("section_sum"), sem("section_sum_read"), sem("section_columns")
        PER = 8
        ADA_BLOCKS = 4 * KT // PER
        NADA = 4 * KT
        SUMS_BLOCK = ADA_BLOCKS + 1
        SUMS_ORDER = (0, 3, 1, 2)
        ada = A.w_ada.rearrange("l (k p) n -> p (l k) n", p=P)

        block = ctx.enter_context(nc.Block())

        @block.sync
        def _(sp):
            for g, sct in enumerate((2, 5)):
                sp.dma_start(s.gate_bc[g][:, :], A.b_ada[0, sct * D:(sct + 1) * D].partition_broadcast(P)).then_inc(bias_in, 16)

            wz = s.wz[:, 0:KT * NZ].rearrange("p (k n) -> p k n", n=NZ)
            src = A.w_in.rearrange("l (k p) n -> p (l k) n", p=P)

            def loads(i, steps=False, first=False, last=None):
                for u in range(4):
                    for e in ((2 * u, 2 * u + 1) if steps else ()):
                        j = PER * (i - 1) + e
                        if e >= 2 or not first:
                            sp.wait_ge(ada_used, j - 1)
                        sp.dma_start(ada_raw[:, e % 2, :], ada[:, ds(j % KT, 1), ds((2 + j // KT) * D, D)].rearrange(
                            "p o n -> p (o n)")).then_inc(ada_in[e % 2], 16)
                    if u == 0:
                        load_unit(sp, s, 2 * i + 1, 1, w_in_unit(A, column(i), 3))
                    elif last is None:
                        load_unit(sp, s, 2 * i + 2 + (u - 1) // 2, (u - 1) % 2, w_in_unit(A, column(i + 1), u - 1))
                    else:
                        load_unit(sp, s, 2 * i + 2 + (u - 1) // 2, (u - 1) % 2, last(u - 1))

            def column(i):
                return i * 512 + (i // 6) * FOX

            loads(1, True, first=True)
            sp.dma_start(wz[:, :, 0:FOX], src[:, :, FZ:FZ + FOX]).then_inc(s.wz_in, 16)
            sp.dma_start(wz[:, :, FOX:32], src[:, :, GZ:GZ + 24]).then_inc(s.wz_in, 16)
            sp.dma_start(wz[:, :, 32:NZ], src[:, :, FZ:FZ + FOX]).then_inc(s.wz_in, 16)
            with sp.Fori(2, ADA_BLOCKS + 1) as i:
                loads(i, True)
            loads(NB_IN - 2)
            loads(NB_IN - 1, last=lambda u: w_cmp_unit(A.cmp_w1_k, u))

        @block.scalar
        def _(act):
            def evacuate(i, first=False):
                for m in range(TM):
                    await_bank(act, s, i, m, 4 * i + 3)
                    if not first:
                        act.wait_ge(stored[m], 16 * i)
                    nc.scalar.activation(stage[:, m, :], s.gb[m][:, :], ACT.Copy).then_inc(s.bank_free, 1)
                    act.wait_ge(s.bank_free, 4 * (i) + m + 1)
                    if not first or m >= 2:
                        act.wait_ge(summed, 4 * i + m - 1)
                    nc.scalar.activation(sq[:, m % 2, :], stage[:, m, :], ACT.Square).then_inc(squared, 1)
                act.wait_ge(ms, i + 1)
                nc.scalar.activation(st[:, 2, :], st[:, 1, :], ACT.Sqrt).then_inc(rms, 1)

            evacuate(0, True)
            with act.Fori(1, NB_IN) as i:
                for u in range(1, 5):
                    split_hi(nc, act, s, 2 * i + u // 2, u % 2)
                evacuate(i)

        @block.tensor
        def _(pe):
            def units(i, us):
                for u in us:
                    rows_unit(nc, pe, s, 2 * i + u // 2, u % 2, s.act_hi, s.act_lo, 4 * u, u == 0, u == 3, i)

            with pe.Fori(1, SUMS_BLOCK) as i:
                units(i, range(4))
            units(SUMS_BLOCK, range(2))
            pe.wait_ge(ada_used, NADA)
            for e, sct in enumerate(SUMS_ORDER):
                for n in range(4):
                    if e:
                        pe.wait_ge(sum_read, 4 * e + n - 3)
                    nc.tensor.matmul(s.mb[n][:, :], s.ones[:, :], acc[:, sct, n * 512:(n + 1) * 512],
                                     start=True, stop=True).then_inc(sum_ready, 1)
            units(SUMS_BLOCK, range(2, 4))
            units(SUMS_BLOCK + 1, range(4))

        @block.vector
        def _(dve):
            def step(j, slot, uses, first):
                dve.wait_ge(ada_in[slot], 16 * uses)
                if not first:
                    dve.wait_ge(ada_used, j)
                sct = acc[:, ds(j // KT, 1), :].rearrange("p o n -> p (o n)")
                nc.vector.scalar_tensor_tensor(out=sct, in0=ada_raw[:, slot, :], scalar=s.c_col[:, 3, ds(j % KT, 1)],
                                               in1=sct, op0=ALU.mult, op1=ALU.add).then_inc(ada_used, 1)

            def work(i, steps, first=False, units=range(1, 5)):
                for u in units:
                    split_lo(nc, dve, s, 2 * i + u // 2, u % 2)
                    for e in ((2 * u - 2, 2 * u - 1) if steps else ()):
                        step(PER * (i - 1) + e, e % 2, (PER * (i - 1) + e) // 2 + 1, first and e == 0)

            def statistics(i):
                for m in range(TM):
                    dve.wait_ge(squared, 4 * i + m + 1)
                    nc.vector.tensor_reduce(st[:, 0, 4 * m:4 * m + 4],
                                            sq[:, m % 2, :].rearrange("p (h d) -> p h d", h=4),
                                            AX.X, ALU.add).then_inc(summed, 1)
                dve.wait_ge(summed, 4 * i + 4)
                nc.vector.tensor_scalar(st[:, 1, :], st[:, 0, :], 1.0 / HD, EPS, ALU.mult, ALU.add).then_inc(ms, 1)
                dve.wait_ge(rms, i + 1)
                nc.vector.reciprocal(st[:, 3, :], st[:, 2, :]).then_inc(rstd, 1)
                dve.wait_ge(rstd, 3 * i + 1)
                r = st[:, 3, :].rearrange("p (m h) -> p m h", m=TM)
                flag = s.base[:, ds(C_FLAG + 4 * i, 4)].unsqueeze(1).broadcast_to([P, TM, 4])
                nflag = s.base[:, ds(C_NFLAG + 4 * i, 4)].unsqueeze(1).broadcast_to([P, TM, 4])
                nc.vector.tensor_tensor(r, r, flag, ALU.mult).then_inc(rstd, 1)
                dve.wait_ge(rstd, 3 * i + 2)
                nc.vector.tensor_tensor(r, r, nflag, ALU.add).then_inc(rstd, 1)
                dve.wait_ge(rstd, 3 * i + 3)
                for m in range(TM):
                    v = stage[:, m, :].rearrange("p (h d) -> p h d", h=4)
                    nc.vector.tensor_tensor(v, v, st[:, 3, 4 * m:4 * m + 4].unsqueeze(2).broadcast_to([P, 4, HD]),
                                            ALU.mult).then_inc(normed, 1)

            dve.wait_ge(acc_zero, 1)
            statistics(0)
            work(1, True, True)
            statistics(1)
            with dve.Fori(2, ADA_BLOCKS + 1) as i:
                work(i, True)
                statistics(i)
            work(SUMS_BLOCK, False, units=(1, 2))
            dve.wait_ge(bias_in, 32)
            for e, sct in enumerate(SUMS_ORDER):
                for n in range(4):
                    dve.wait_ge(sum_ready, 4 * e + n + 1)
                    part = slice(n * 512, (n + 1) * 512)
                    if e < 2:
                        nc.vector.tensor_tensor(s.gate_bc[e][:, part], s.mb[n][:, :], s.gate_bc[e][:, part],
                                                ALU.add).then_inc(sum_read, 1)
                    else:
                        nc.vector.tensor_tensor(ada_raw[:, e % 2, part].rearrange("p (k c) -> p k c", k=4),
                                                s.mb[n][:, :].rearrange("p (k c) -> p k c", k=4),
                                                s.ident.unsqueeze(1).broadcast_to([P, 4, P]), ALU.mult).then_inc(sum_read, 1)
            work(SUMS_BLOCK, False, units=(3, 4))
            dve.wait_ge(sum_read, 16)
            for e in range(2):
                nc.vector.tensor_reduce(s.mod[:, 4 + e, :], ada_raw[:, e, :].rearrange("p (k c) -> p k c", k=KT), AX.X,
                                        ALU.add).then_inc(col_done, 1)
            statistics(SUMS_BLOCK)
            work(SUMS_BLOCK + 1, False)
            dve.wait_ge(col_done, 2)
            nc.vector.tensor_tensor(s.mod[:, 3, :], s.mod[:, 4, :], s.cols1[:, 3 * KT:4 * KT], ALU.add).then_inc(col_done, 1)
            nc.vector.tensor_tensor(s.mod[:, 5, :], s.mod[:, 5, :], s.cols1[:, 4 * KT:5 * KT], ALU.add).then_inc(col_done, 1)
            dve.wait_ge(col_done, 4)
            nc.vector.scalar_tensor_tensor(out=s.mod[:, 2, :], in0=s.mod[:, 5, :], scalar=1.0,
                                           in1=s.cols1[:, 112:128], op0=ALU.add, op1=ALU.mult).then_inc(col_done, 1)
            statistics(SUMS_BLOCK + 1)

        @block.gpsimd
        def _(pool):
            nc.gpsimd.memset(acc[:, :, :], 0.0).then_inc(acc_zero, 1)
            with pool.Fori(0, NB_IN) as i:
                for m in range(TM):
                    pool.wait_ge(normed, 4 * i + m + 1)
                    pool.dma_start(s.proj[ds(i, 1), m].rearrange("o p n -> (o p) n"), stage[:, m, :]).then_inc(stored[m], 16)
            for m in range(TM):
                pool.wait_ge(stored[m], 16 * NB_IN)



def phase_compress(nc, A, s):
    with ExitStack() as ctx:
        sb = lambda name, shape, dt=F32: ctx.enter_context(nc.sbuf_tensor(name, shape, dt))
        sem = s.sem
        ZW = KT * NZ + P
        wz = s.wz[:, 0:ZW]
        wz_hi, wz_lo = sb("wz_hi", [P, ZW], F32R), sb("wz_lo", [P, ZW], F32R)
        zb = sb("z_bias", [NZ, 1])
        z = sb("z", [NZ, 5, T])
        kcv = sb("kcv", [P, TM, 512])
        kcvT = sb("kcvT", [P, 4, T])
        XW = CMP_LEN * 64 + 64
        xb = sb("xb", [P, XW])
        xb_hi, xb_lo = sb("xb_hi", [P, XW], F32R), sb("xb_lo", [P, XW], F32R)
        w2 = sb("w2", [P, 2, 2, HD])
        hid = sb("hid", [64, 5, CMP_HID])
        hidT = sb("hidT", [P, 2, 64])
        kn = kcv[0:64, 0, 0:2 * HD].rearrange("p (e d) -> p e d", e=2)
        kst = sb("cmp_kst", [64, 4])

        zb_in, kc_in, w2_in = sem("zb_in"), sem("kc_in"), sem("w2_in")
        zeroed = sem("wz_zero")
        wzh, wzl, z_sums = sem("wz_hi_ready"), sem("wz_lo_ready"), sem("z_sums")
        zs, za, gtr, g_ready = sem("z_vector"), sem("z_scalar"), sem("gates_turned"), s.gates_ready
        ktr, ktr_read, x_ready, xh, xl = sem("kcv_turned"), sem("kcv_read"), sem("xb_ready"), sem("xb_hi_ready"), sem("xb_lo_ready")
        h_exp, h_vec, h_tr, h_trr = sem("hid_exp"), sem("hid_vec"), sem("hid_turned"), sem("hid_turned_read")
        k2, k2s, k2v, k2t, k2r = sem("cmp_out"), sem("cmp_out_sq"), sem("cmp_out_vec"), sem("cmp_out_turned"), s.cmp_ready
        hfree = sem("hid_free")

        block = ctx.enter_context(nc.Block())

        @block.sync
        def _(sp):
            sp.dma_start(kcv[:, :, :], s.proj[8].rearrange("m p n -> p m n")).then_inc(kc_in, 16)
            sp.wait_ge(zeroed, 3)
            sp.dma_start(zb[0:FOX, :], A.b_forget.rearrange("l h -> h l")).then_inc(zb_in, 16)
            sp.dma_start(zb[32:NZ, :], A.b_forget.rearrange("l h -> h l")).then_inc(zb_in, 16)
            for kv, w in enumerate((A.cmp_w2_k, A.cmp_w2_v)):
                sp.dma_start(w2[:, kv], w.rearrange("l (k p) n -> p (l k) n", p=P)).then_inc(w2_in, 16)
            load_unit(sp, s, PAIR_CMP + 1, 1, w_cmp_unit(A.cmp_w1_k, 3))
            for u in range(4):
                load_unit(sp, s, PAIR_CMP + 2 + u // 2, u % 2, w_cmp_unit(A.cmp_w1_v, u))
            load_unit(sp, s, PAIR_OUT, 0, w_out_unit(A, 0, 0))

        @block.gpsimd
        def _(pool):
            nc.gpsimd.memset(zb[:, :], 0.0).then_inc(zeroed, 1)
            nc.gpsimd.memset(xb[:, :], 0.0).then_inc(zeroed, 1)
            nc.gpsimd.memset(kst[:, :], 0.0).then_inc(zeroed, 1)

        @block.tensor
        def _(pe):
            pe.wait_ge(kc_in, 16)
            for e in range(4):
                if e >= 2:
                    pe.wait_ge(ktr_read, e - 1)
                for m in range(TM):
                    mm = nc.tensor.transpose(s.mb[1 + e % 2][:, m * P:(m + 1) * P], kcv[:, m, e * HD:(e + 1) * HD], s.ident)
                mm.then_inc(ktr, 1)
            pe.wait_ge(wzl, 1)
            for k in range(KT):
                c = slice(k * NZ, k * NZ + P)
                mm = three_products(nc, s.mb[0][:, :], wz_hi[:, c], wz_lo[:, c], s.act_hi[:, k, :], s.act_lo[:, k, :],
                                    k == 0, k == KT - 1)
            mm.then_inc(z_sums, 1)
            pe.wait_ge(ktr_read, 4)

            def hidden_unit(kv, u):
                pair, slot = PAIR_CMP + 2 * kv + u // 2, u % 2
                pe.wait_ge(s.w_lo_ready, 2 * pair + slot + 1)
                wh = s.w_hi[:, slot].rearrange("p a (b n) -> p (a b) n", b=2)
                wl = s.w_lo[:, slot].rearrange("p a (b n) -> p (a b) n", b=2)
                for e in range(8):
                    l = 8 * u + e
                    c = slice(l * 64, l * 64 + P)
                    mm = three_products(nc, s.mb[2 + kv][:, 0:256], xb_hi[:, c], xb_lo[:, c],
                                        wh[:, e, :], wl[:, e, :], l == 0, l == CMP_LEN - 1)
                mm.then_inc(s.unit_used, 1)

            def turn_hidden(kv):
                pe.wait_ge(h_vec, 3 * kv + 3)
                for c in range(2):
                    mm = nc.tensor.transpose(s.mb[1][:, c * 64:(c + 1) * 64], hid[:, 3, c * P:(c + 1) * P], s.ident[0:64, 0:64])
                mm.then_inc(h_tr, 1)

            def second_layer(kv):
                pe.wait_ge(h_trr, kv + 1)
                pe.wait_ge(w2_in, 32)
                for c in range(2):
                    mm = nc.tensor.matmul(s.gb[kv][0:64, 0:HD], hidT[:, c, :], w2[:, kv, c, :], start=c == 0, stop=c == 1)
                mm.then_inc(k2, 1)

            pe.wait_ge(xl, 1)
            for u in range(4):
                hidden_unit(0, u)
            pe.wait_ge(xl, 2)
            hidden_unit(1, 0)
            hidden_unit(1, 1)
            turn_hidden(0)
            hidden_unit(1, 2)
            second_layer(0)
            hidden_unit(1, 3)
            pe.wait_ge(k2v, 3)
            nc.tensor.transpose(s.gb[2][:, 0:64], kn[:, 1, :], s.ident[0:64, 0:64]).then_inc(k2t, 1)
            pe.wait_ge(zs, 5)
            for m in range(TM):
                mm = nc.tensor.transpose(s.mb[0][:, m * NZ:(m + 1) * NZ], z[:, 3, m * P:(m + 1) * P], s.ident[0:NZ, 0:NZ])
            mm.then_inc(gtr, 1)
            turn_hidden(1)
            second_layer(1)

        @block.scalar
        def _(act):
            act.wait_ge(s.wz_in, 48)
            nc.scalar.activation(wz_hi[:, :], wz, ACT.Copy).then_inc(wzh, 1)
            for e in range(4):
                act.wait_ge(ktr, e + 1)
                nc.scalar.activation(kcvT[:, e, :], s.mb[1 + e % 2][:, :], ACT.Copy).then_inc(ktr_read, 1)
            act.wait_ge(x_ready, 4)
            nc.scalar.activation(xb_hi[:, :], xb[:, :], ACT.Copy).then_inc(xh, 1)
            split_hi(nc, act, s, PAIR_CMP, 1)
            act.wait_ge(zs, 1)
            nc.scalar.activation(z[:, 1, :], z[:, 0, :], ACT.Abs).then_inc(za, 1)
            act.wait_ge(za, 1)
            nc.scalar.activation(z[:, 2, :], z[:, 1, :], ACT.Exp, scale=-1.0).then_inc(za, 1)
            nc.scalar.activation(z[:, 3, :], z[:, 0, :], ACT.Exp, scale=-1.0).then_inc(za, 1)
            for u in range(2, 5):
                split_hi(nc, act, s, PAIR_CMP + u // 2, u % 2)

            def hidden(kv):
                act.wait_ge(s.unit_used, 2 * PAIR_CMP + 4 * kv + 4)
                nc.scalar.activation(hid[:, 0, :], s.mb[2 + kv][0:64, 0:256], ACT.Copy).then_inc(h_exp, 1)
                act.wait_ge(h_exp, 2 * kv + 1)
                nc.scalar.activation(hid[:, 1, :], hid[:, 0, :], ACT.Exp, scale=-1.0).then_inc(h_exp, 1)

            def read_hidden(kv):
                act.wait_ge(h_tr, kv + 1)
                nc.scalar.activation(hidT[:, :, :], s.mb[1][:, 0:P].rearrange("p (c n) -> p c n", c=2), ACT.Copy).then_inc(h_trr, 1)

            act.wait_ge(x_ready, 8)
            act.wait_ge(s.unit_used, 2 * PAIR_CMP + 4)
            nc.scalar.activation(xb_hi[:, :], xb[:, :], ACT.Copy).then_inc(xh, 1)
            hidden(0)
            act.wait_ge(zs, 2)
            nc.scalar.activation(z[:, 1, :], z[:, 2, :], ACT.Ln).then_inc(za, 1)
            for u in (1, 2):
                split_hi(nc, act, s, PAIR_CMP + 2 + u // 2, u % 2)
            read_hidden(0)
            split_hi(nc, act, s, PAIR_CMP + 3, 1)
            act.wait_ge(k2, 1)
            nc.scalar.activation(kn[:, 0, :], s.gb[0][0:64, 0:HD], ACT.Copy).then_inc(k2s, 1)
            act.wait_ge(k2s, 1)
            nc.scalar.activation(hid[:, 1, 0:HD], kn[:, 0, :], ACT.Square, accum_out=kst[:, 0:1]).then_inc(k2s, 1)
            act.wait_ge(k2v, 1)
            nc.scalar.activation(kst[:, 2:3], kst[:, 1:2], ACT.Sqrt).then_inc(k2s, 1)
            split_hi(nc, act, s, PAIR_OUT, 0)
            hidden(1)
            act.wait_ge(k2t, 1)
            nc.scalar.activation(s.kcT[:, :], s.gb[2][:, 0:64], ACT.Copy, scale=s.cols2[:, 19:20]).then_inc(k2r, 1)
            read_hidden(1)
            act.wait_ge(k2, 2)
            nc.scalar.activation(s.vc[:, :], s.gb[1][0:64, 0:HD], ACT.Copy).then_inc(k2r, 1)

        @block.vector
        def _(dve):
            dve.wait_ge(wzh, 1)
            nc.vector.tensor_tensor(wz_lo[:, :], wz, wz_hi[:, :].bitcast(F32), ALU.subtract).then_inc(wzl, 1)

            def windows(kv):
                xv = xb[:, 0:CMP_LEN * 64].rearrange("p (l g n) -> p l g n", g=NG, n=CW)
                for g in range(NG):
                    src = kcvT[:, 2 * kv + g, :].rearrange("p (n b) -> p b n", b=CMP_STRIDE)
                    for a in range(2):
                        pe_l = s.cols2[:, 22 + 32 * kv + 16 * a:22 + 32 * kv + 16 * a + 16]
                        nc.vector.tensor_tensor(xv[:, 16 * a:16 * a + 16, g, 0:NCMP], src[:, :, a:a + NCMP],
                                                pe_l.unsqueeze(2).broadcast_to([P, 16, NCMP]), ALU.add).then_inc(x_ready, 1)

            dve.wait_ge(ktr_read, 2)
            dve.wait_ge(zeroed, 3)
            windows(0)
            dve.wait_ge(xh, 1)
            nc.vector.tensor_tensor(xb_lo[:, :], xb[:, :], xb_hi[:, :].bitcast(F32), ALU.subtract).then_inc(xl, 1)
            split_lo(nc, dve, s, PAIR_CMP, 1)
            dve.wait_ge(ktr_read, 4)
            dve.wait_ge(xl, 1)
            windows(1)
            dve.wait_ge(z_sums, 1)
            dve.wait_ge(zb_in, 32)
            nc.vector.tensor_scalar(z[:, 0, :], s.mb[0][0:NZ, :], zb[:, :], None, ALU.add).then_inc(zs, 1)
            for u in range(2, 4):
                split_lo(nc, dve, s, PAIR_CMP + u // 2, u % 2)
            dve.wait_ge(za, 3)
            nc.vector.tensor_scalar(z[:, 2, :], z[:, 2, :], 1.0, None, ALU.add).then_inc(zs, 1)
            nc.vector.tensor_scalar(z[:, 3, :], z[:, 3, :], 1.0, None, ALU.add).then_inc(zs, 1)
            dve.wait_ge(zs, 3)
            nc.vector.tensor_scalar(z[:, 4, :], z[:, 0, :], 0.0, None, ALU.min).then_inc(zs, 1)
            split_lo(nc, dve, s, PAIR_CMP + 2, 0)
            dve.wait_ge(xh, 2)
            nc.vector.tensor_tensor(xb_lo[:, :], xb[:, :], xb_hi[:, :].bitcast(F32), ALU.subtract).then_inc(xl, 1)

            def silu(kv):
                dve.wait_ge(h_exp, 2 * kv + 2)
                nc.vector.tensor_scalar(hid[:, 2, :], hid[:, 1, :], 1.0, None, ALU.add).then_inc(h_vec, 1)
                dve.wait_ge(h_vec, 3 * kv + 1)
                nc.vector.reciprocal(hid[:, 4, :], hid[:, 2, :]).then_inc(h_vec, 1)
                dve.wait_ge(h_vec, 3 * kv + 2)
                nc.vector.tensor_tensor(hid[:, 3, :], hid[:, 0, :], hid[:, 4, :], ALU.mult).then_inc(h_vec, 1)

            split_lo(nc, dve, s, PAIR_CMP + 2, 1)
            silu(0)
            nc.vector.reciprocal(z[:, 3, :], z[:, 3, :]).then_inc(zs, 1)
            split_lo(nc, dve, s, PAIR_CMP + 3, 0)
            dve.wait_ge(za, 4)
            dve.wait_ge(zs, 5)
            nc.vector.tensor_tensor(z[:, 4, :], z[:, 4, :], z[:, 1, :], ALU.subtract).then_inc(zs, 1)
            nc.vector.memset(z[:, 2, :], 1.0).then_inc(zs, 1)
            split_lo(nc, dve, s, PAIR_CMP + 3, 1)
            dve.wait_ge(k2s, 2)
            nc.vector.tensor_scalar(kst[:, 1:2], kst[:, 0:1], 1.0 / HD, EPS, ALU.mult, ALU.add).then_inc(k2v, 1)
            dve.wait_ge(zs, 7)
            nc.vector.tensor_tensor_scan(s.cum[:, :], z[:, 2, :], z[:, 4, :], 0.0, ALU.mult, ALU.add).then_inc(zs, 1)
            dve.wait_ge(k2s, 3)
            nc.vector.reciprocal(kst[:, 3:4], kst[:, 2:3]).then_inc(k2v, 1)
            dve.wait_ge(k2v, 2)
            nc.vector.tensor_scalar(kn[:, 1, :], kn[:, 0, :], kst[:, 3:4], None, ALU.mult).then_inc(k2v, 1)
            dve.wait_ge(zs, 8)
            nc.vector.tensor_scalar(s.auxR[:, :], s.cum[:, :], s.base[0:NZ, C_N1:C_N1 + 1], s.base[0:NZ, C_N2:C_N2 + 1],
                                    ALU.mult, ALU.add).then_inc(zs, 1)
            split_lo(nc, dve, s, PAIR_OUT, 0)
            silu(1)
            dve.wait_ge(gtr, 1)
            nc.vector.tensor_copy(s.gates[:, :, :], s.mb[0][:, 0:TM * NZ].rearrange("p (m n) -> p m n", m=TM)).then_inc(g_ready, 1)



ORDER = (0, 2, 1, 3)


def item_scores(nc, pe, s, a, I, at, qT, kT, aux, early):
    n = ORDER[at]
    w = (n + 1) * P
    if not early:
        pe.wait_ge(a.p_ready, I - 1)
    bank = s.gb[at % 2]
    nc.tensor.matmul(bank[:, n * P:w], s.ident_bf[:, :], s.causal_bf[:, :], start=True, stop=False, skip_group_check=True)
    if aux is not None:
        nc.tensor.matmul(bank[:, 0:w], aux[:, n * P:(n + 1) * P], s.auxR[:, 0:w], start=False, stop=False,
                         skip_group_check=True)
    nc.tensor.matmul(bank[:, 0:w], qT[:, n * P:(n + 1) * P], kT(w), start=False, stop=True,
                     skip_group_check=True).then_inc(a.s_done, 1)


def item_max(nc, dve, s, a, I, at):
    dve.wait_ge(a.s_done, I + 1)
    nc.vector.tensor_reduce(a.nmax[:, at:at + 1], s.gb[at % 2][:, 0:(ORDER[at] + 1) * P], AX.X, ALU.max,
                            negate=True).then_inc(a.max_ready, 1)


def item_exp(nc, act, s, a, I, at, early):
    w = (ORDER[at] + 1) * P
    act.wait_ge(a.max_ready, I + 1)
    if not early:
        act.wait_ge(a.pt_done, I - 3)
    nc.scalar.activation(a.p[:, at, 0:w], s.gb[at % 2][:, 0:w], ACT.Exp,
                         bias=a.nmax[:, at:at + 1], accum_out=a.rsum[:, at:at + 1]).then_inc(a.p_ready, 1)


def item_reciprocal(nc, dve, s, a, I, at):
    dve.wait_ge(a.p_ready, I + 1)
    nc.vector.tensor_scalar(a.rinv[:, 0, at:at + 1], a.rsum[:, at:at + 1], 1e-30, None, ALU.max).then_inc(a.r_ready, 1)
    dve.wait_ge(a.r_ready, 2 * I + 1)
    nc.vector.reciprocal(a.rinv[:, 1, at:at + 1], a.rinv[:, 0, at:at + 1]).then_inc(a.r_ready, 1)


def item_normalise(nc, dve, s, a, I, at, gate):
    dve.wait_ge(a.r_ready, 2 * I + 2)
    part = a.p[:, at, 0:(ORDER[at] + 1) * P]
    if gate is None:
        nc.vector.tensor_scalar(part, part, a.rinv[:, 1, at:at + 1], None, ALU.mult).then_inc(a.pn_ready, 1)
    else:
        nc.vector.tensor_scalar(part, part, a.rinv[:, 1, at:at + 1], gate(ORDER[at]), ALU.mult, ALU.mult).then_inc(a.pn_ready, 1)


def item_turn(nc, pe, s, a, I, at, early):
    pe.wait_ge(a.pn_ready, I + 1)
    if not early:
        pe.wait_ge(a.pt_ready, I - 1)
    for b in range(ORDER[at] + 1):
        mm = nc.tensor.transpose(s.gb[2 + at % 2][:, b * P:(b + 1) * P], a.p[:, at, b * P:(b + 1) * P], s.ident)
    mm.then_inc(a.pt_done, 1)


def item_copy(nc, act, s, a, I, at, early):
    w = (ORDER[at] + 1) * P
    act.wait_ge(a.pt_done, I + 1)
    if not early:
        act.wait_ge(a.pv_done, I - 1)
    nc.scalar.activation(a.pT[:, at % 2, 0:w], s.gb[2 + at % 2][:, 0:w], ACT.Copy).then_inc(a.pt_ready, 1)


def item_values(nc, pe, s, a, I, at, v, bank, start):
    pe.wait_ge(a.pt_ready, I + 1)
    n = ORDER[at]
    for b in range(n + 1):
        mm = nc.tensor.matmul(bank[:, n * P:(n + 1) * P], v[:, b, :], a.pT[:, at % 2, b * P:(b + 1) * P],
                              start=start and b == 0, stop=b == n, skip_group_check=True)
    mm.then_inc(a.pv_done, 1)


def attention_state(nc, s, sb, sem, tag):
    a = Names()
    a.p = s.w_raw[:, 1]
    a.pT = sb(tag + "pT", [P, 2, T])
    a.nmax, a.rsum, a.rinv = sb(tag + "nmax", [P, TM]), sb(tag + "rsum", [P, TM]), sb(tag + "rinv", [P, 3, TM])
    a.s_done, a.max_ready, a.p_ready = sem(tag + "scores_done"), sem(tag + "max_ready"), sem(tag + "p_ready")
    a.r_ready, a.pn_ready = sem(tag + "r_ready"), sem(tag + "pn_ready")
    a.pt_done, a.pt_ready, a.pv_done = sem(tag + "pT_done"), sem(tag + "pT_ready"), sem(tag + "pv_done")
    a.o_hi, a.o_lo = sem(tag + "o_hi"), sem(tag + "o_lo")
    return a


def sparse_state(ctx, nc, s):
    sb = lambda name, shape, dt=F32: ctx.enter_context(nc.sbuf_tensor(name, shape, dt))
    sem = s.sem
    q = Names()
    q.tabs = sb("nsa_tabs", [P, N_END])
    q.cos = q.tabs[:, N_COS:N_COS + 512].rearrange("p (m d) -> p m d", m=TM)
    q.sin = q.tabs[:, N_SIN:N_SIN + 512].rearrange("p (m d) -> p m d", m=TM)
    q.raw, q.gained_x, q.roped_x = (sb("nsa_" + name, [P, 2, TM, HD]) for name in ("raw", "gained_x", "roped_x"))
    q.ra, q.rb = sb("rope_a", [P, TM, HD]), sb("rope_b", [P, TM, HD])
    q.kT = sb("nsa_kT", [P, 2 * NG, T])
    q.tabs_in, q.q_in, q.k_in = sem("nsa_tabs_in"), [sem(f"nsa_q_in{i}") for i in range(2)], sem("nsa_k_in")
    q.gained, q.roped, q.r_a, q.r_b = sem("nsa_gained"), sem("nsa_roped"), sem("rope_a_done"), sem("rope_b_done")
    return q


def rope(nc, pool, q, t, e):
    x = q.gained_x
    pool.wait_ge(q.gained, t + 1)
    nc.gpsimd.tensor_tensor(q.ra[:, :, :], x[:, e], q.cos, ALU.mult).then_inc(q.r_a, 1)
    nc.gpsimd.tensor_tensor(q.rb[:, :, 0:64], x[:, e, :, 64:HD], q.sin[:, :, 0:64], ALU.mult).then_inc(q.r_b, 1)
    nc.gpsimd.tensor_tensor(q.rb[:, :, 64:HD], x[:, e, :, 0:64], q.sin[:, :, 64:HD], ALU.mult).then_inc(q.r_b, 1)
    pool.wait_ge(q.r_a, t + 1)
    pool.wait_ge(q.r_b, 2 * t + 2)
    nc.gpsimd.tensor_tensor(q.roped_x[:, e], q.ra[:, :, :], q.rb[:, :, :], ALU.add).then_inc(q.roped, 1)


NK = 2 * NG


def phase_fox(nc, A, s):
    with ExitStack() as ctx:
        sb = lambda name, shape, dt=F32: ctx.enter_context(nc.sbuf_tensor(name, shape, dt))
        sem = s.sem
        raw = sb("fox_raw", [P, 2, 3, TM, HD])
        qkT = sb("fox_qkT", [P, 2, 2, T])
        aux = sb("fox_aux", [NZ, 2, T])
        a = attention_state(nc, s, sb, sem, "fox_")
        landed, v_landed = [sem(f"fox_qk_landed{i}") for i in range(2)], [sem(f"fox_v_landed{i}") for i in range(2)]
        turned, turned_read, aux_ready = sem("fox_qk_turned"), sem("fox_qk_read"), sem("fox_aux_ready")
        q, key_turned, key_read = s.sparse, sem("nsa_key_turned"), s.key_read
        PAIRS = FOX // 2

        block = ctx.enter_context(nc.Block())

        @block.sync
        def _(sp):
            def load(j, e, first=False):
                for x in range(3):
                    if not first and x == 0:
                        sp.wait_ge(turned, 2 * (2 * j + e) - 2)
                    if not first and x == 2:
                        sp.wait_ge(a.pv_done, 4 * (2 * j + e) - 4)
                    src = s.proj[ds(2 * x + j // 2, 1), :, :, ds((j % 2) * 256 + e * HD, HD)]
                    sp.dma_start(raw[:, e, x], src.rearrange("o m p d -> p (o m) d")).then_inc(
                        (v_landed if x == 2 else landed)[e], 16)
            def load_key(j):
                sp.dma_start(q.raw[:, 1], s.proj[ds(9 + j // NG, 1), :, :, ds((j % NG) * HD, HD)].rearrange(
                    "o m p d -> p (o m) d")).then_inc(q.k_in, 16)
            load(0, 0, True)
            load_key(0)
            sp.dma_start(q.tabs[:, :], A.nsa_tabs).then_inc(q.tabs_in, 16)
            load(0, 1, True)
            sp.dma_start(q.raw[:, 0], s.proj[6, :, :, 0:HD].rearrange("m p d -> p m d")).then_inc(q.q_in[0], 16)
            with sp.Fori(1, PAIRS) as j:
                load(j, 0)
                sp.wait_ge(q.gained, j)
                load_key(j)
                load(j, 1)

        @block.gpsimd
        def _(pool):
            pool.wait_ge(q.tabs_in, 16)

            def gain(t, e, row):
                nc.gpsimd.tensor_tensor(q.gained_x[:, e], q.raw[:, e], s.gain_bc[:, ds(row, 1), :].broadcast_to([P, TM, HD]),
                                        ALU.mult).then_inc(q.gained, 1)

            pool.wait_ge(q.k_in, 16)
            gain(0, 1, 1)
            rope(nc, pool, q, 0, 1)
            with pool.Fori(1, NK) as t:
                pool.wait_ge(q.k_in, 16 * (t + 1))
                pool.wait_ge(q.roped, t)
                gain(t, 1, 1 + t // NG)
                pool.wait_ge(key_turned, t)
                rope(nc, pool, q, t, 1)
            pool.wait_ge(q.q_in[0], 16)
            pool.wait_ge(q.roped, NK)
            gain(NK, 0, 0)
            rope(nc, pool, q, NK, 0)

        def turn_qk(pe, j, e):
            h = 2 * j + e
            pe.wait_ge(landed[e], 32 * (j + 1))
            if not (isinstance(h, int) and h == 0):
                pe.wait_ge(turned_read, 2 * h)
            for x in range(2):
                for m in range(TM):
                    mm = nc.tensor.transpose(s.mb[2 + x][:, m * P:(m + 1) * P], raw[:, e, x, m, :], s.ident)
                mm.then_inc(turned, 1)

        @block.tensor
        def _(pe):
            def pair(j, first, last):
                for e in range(2):
                    h = 2 * j + e
                    start = first and e == 0
                    for n in range(TM):
                        I = 4 * h + n
                        if n == 0:
                            pe.wait_ge(turned_read, 2 * h + 2)
                            pe.wait_ge(aux_ready, h + 1)
                        item_scores(nc, pe, s, a, I, n, qkT[:, e, 0], lambda w: qkT[:, e, 1, 0:w], aux[:, e], start and n < 2)
                        if n >= 2 or not start:
                            item_turn(nc, pe, s, a, I - 2, (n - 2) % 4, start and n < 4)
                        if n == 3:
                            if not first:
                                pe.wait_ge(a.o_lo, h - 1)
                            pe.wait_ge(v_landed[e], 16 * (j + 1))
                            item_values(nc, pe, s, a, I - 3, 0, raw[:, e, 2], s.mb[e], True)
                        elif not start:
                            item_values(nc, pe, s, a, I - 3, n + 1, raw[:, 1 - e, 2], s.mb[1 - e], False)
                        if n == 1 and not (last and e == 1):
                            if e == 1:
                                pe.wait_ge(key_read, j + 1)
                            turn_qk(pe, j + e, 1 - e)
                        if n == 3 and e == 0:
                            pe.wait_ge(turned_read, 2 * h + 4)
                            pe.wait_ge(q.roped, j + 1)
                            for m in range(TM):
                                mm = nc.tensor.transpose(s.mb[3][:, m * P:(m + 1) * P], q.roped_x[:, 1, m, :], s.ident)
                            mm.then_inc(key_turned, 1)
            turn_qk(pe, 0, 0)
            pair(0, True, False)
            with pe.Fori(1, PAIRS - 1) as j:
                pair(j, False, False)
            pair(PAIRS - 1, False, True)
            END = 4 * FOX
            item_turn(nc, pe, s, a, END - 2, 2, False)
            item_values(nc, pe, s, a, END - 3, 1, raw[:, 1, 2], s.mb[1], False)
            item_turn(nc, pe, s, a, END - 1, 3, False)
            for n in (2, 3):
                item_values(nc, pe, s, a, END - 4 + n, n, raw[:, 1, 2], s.mb[1], False)

        @block.scalar
        def _(act):
            def read_qk(h, e):
                for x in range(2):
                    act.wait_ge(turned, 2 * h + x + 1)
                    if not isinstance(h, int) or h >= 2:
                        act.wait_ge(a.s_done, 4 * h - 4)
                    nc.scalar.activation(qkT[:, e, x], s.mb[2 + x][:, :], ACT.Copy,
                                         scale=s.fq_gain[:, :] if x == 0 else s.cols2[:, 17:18]).then_inc(turned_read, 1)

            def o_hi(h, e):
                act.wait_ge(a.pv_done, 4 * h + 4)
                nc.scalar.activation(s.act_hi[:, ds(h, 1), :].rearrange("p o t -> p (o t)"), s.mb[e][:, :],
                                     ACT.Copy).then_inc(a.o_hi, 1)

            def pair(j, first, last):
                for e in range(2):
                    h = 2 * j + e
                    start = first and e == 0
                    for n in range(TM):
                        item_exp(nc, act, s, a, 4 * h + n, n, start)
                        if n >= 2 or not start:
                            item_copy(nc, act, s, a, 4 * h + n - 2, (n - 2) % 4, start)
                        if n == 2 and not (last and e == 1):
                            read_qk(h + 1, 1 - e)
                        if n == 3 and not start:
                            o_hi(h - 1, 1 - e)
                        if n == 0 and e == 1:
                            act.wait_ge(key_turned, j + 1)
                            nc.scalar.activation(tile(q.kT, j), s.mb[3][:, :], ACT.Copy).then_inc(key_read, 1)
            read_qk(0, 0)
            pair(0, True, False)
            with act.Fori(1, PAIRS - 1) as j:
                pair(j, False, False)
            pair(PAIRS - 1, False, True)
            for n in (2, 3):
                item_copy(nc, act, s, a, 4 * FOX - 4 + n, n, False)
            o_hi(FOX - 1, 1)

        @block.vector
        def _(dve):
            def make_aux(h, e):
                if not isinstance(h, int) or h >= 2:
                    dve.wait_ge(a.s_done, 4 * h - 4)
                nc.vector.tensor_scalar(aux[:, e, :], s.cum[:, :], s.base[0:NZ, ds(C_M1 + h, 1)],
                                        s.base[0:NZ, ds(C_M2 + h, 1)], ALU.mult, ALU.add).then_inc(aux_ready, 1)

            def o_lo(h, e):
                dve.wait_ge(a.o_hi, h + 1)
                nc.vector.tensor_tensor(s.act_lo[:, ds(h, 1), :].rearrange("p o t -> p (o t)"), s.mb[e][:, :],
                                        s.act_hi[:, ds(h, 1), :].rearrange("p o t -> p (o t)").bitcast(F32),
                                        ALU.subtract).then_inc(a.o_lo, 1)

            def pair(j, first, last):
                for e in range(2):
                    h = 2 * j + e
                    start = first and e == 0
                    for n in range(TM):
                        I = 4 * h + n
                        item_max(nc, dve, s, a, I, n)
                        if n >= 1 or not start:
                            item_reciprocal(nc, dve, s, a, I - 1, (n - 1) % 4)
                            item_normalise(nc, dve, s, a, I - 1, (n - 1) % 4, None)
                        if n == 0 and not (first and e < 2) and not (isinstance(h, int) and h < 2):
                            o_lo(h - 2, e)
                        if n == 2:
                            if not (last and e == 1):
                                make_aux(h + 1, 1 - e)
            make_aux(0, 0)
            pair(0, True, False)
            with dve.Fori(1, PAIRS - 1) as j:
                pair(j, False, False)
            pair(PAIRS - 1, False, True)
            item_reciprocal(nc, dve, s, a, 4 * FOX - 1, 3)
            item_normalise(nc, dve, s, a, 4 * FOX - 1, 3, None)
            for e in range(2):
                o_lo(FOX - 2 + e, e)


def phase_nsa(nc, A, s):
    with ExitStack() as ctx:
        sb = lambda name, shape, dt=F32: ctx.enter_context(nc.sbuf_tensor(name, shape, dt))
        sem = s.sem
        q = s.sparse
        tabs, nq, qn, qr = q.tabs, q.raw, q.gained_x, q.roped_x
        kT = q.kT[:, :, :].rearrange("p (b g) t -> p b g t", g=NG)
        vv = sb("nsa_v", [P, 2, 2, TM, HD])
        qT = sb("nsa_qT", [P, 2, T])
        qrT = sb("nsa_qrT", [P, 2, T])
        pcw = sb("cmp_p", [P, 2, (TM + 1) * 64])
        pc = pcw[:, :, 0:TM * 64].rearrange("p e (m n) -> p e m n", m=TM)
        cst = sb("cmp_stats", [P, 4, TM])
        pcT = sb("cmp_pT", [64, 2, T])
        a = attention_state(nc, s, sb, sem, "nsa_")

        gained, roped, q_in = q.gained, q.roped, q.q_in
        v_in = [sem(f"nsa_v_in{i}") for i in range(2)]
        turned, turned_read = sem("nsa_turned"), sem("nsa_turned_read")
        c_s, c_v, c_e, c_t, c_tr, c_pv = (sem("cmp_scores"), sem("cmp_vec"), sem("cmp_exp"), sem("cmp_turned"),
                                          sem("cmp_turned_read"), sem("cmp_pv"))
        pad_zero = sem("cmp_pad_zero")
        PAIRS = NSA // 2
        C_V = 6

        block = ctx.enter_context(nc.Block())

        @block.sync
        def _(sp):
            def load_head(j, e, first=False):
                h = 2 * j + e
                if not first:
                    sp.wait_ge(gained, NK + h - 1)
                if not (first and e == 0):
                    sp.dma_start(nq[:, e], s.proj[ds(6 + j // 2, 1), :, :, ds((j % 2) * 256 + e * HD, HD)].rearrange(
                        "o m p d -> p (o m) d")).then_inc(q_in[e], 16)
                if not first:
                    sp.wait_ge(a.pv_done, 8 * h - 8)
                for br in range(2):
                    sp.dma_start(vv[:, e, br], s.proj[9 + br, :, :, ds((j // 2) * HD + 256, HD)].rearrange(
                        "m p d -> p m d")).then_inc(v_in[e], 16)
            for e in range(2):
                load_head(0, e, True)
            with sp.Fori(1, PAIRS) as j:
                for e in range(2):
                    load_head(j, e)

        @block.gpsimd
        def _(pool):
            nc.gpsimd.memset(pcw[:, :, TM * 64:], 0.0).then_inc(pad_zero, 1)

            def rope_head(h, e):
                pool.wait_ge(roped, NK + h)
                if not isinstance(h, int) or h >= 2:
                    pool.wait_ge(turned, 2 * h - 2)
                rope(nc, pool, q, NK + h, e)
            rope_head(1, 1)
            with pool.Fori(1, PAIRS) as j:
                for e in range(2):
                    rope_head(2 * j + e, e)

        def turn_plain(pe, h, e):
            pe.wait_ge(gained, NK + h + 1)
            if not isinstance(h, int) or h >= 1:
                pe.wait_ge(c_v, C_V * (h - 1) + 1)
            for m in range(TM):
                mm = nc.tensor.transpose(s.mb[2][:, m * P:(m + 1) * P], qn[:, e, m, :], s.ident)
            mm.then_inc(turned, 1)

        def turn_roped(pe, h, e):
            pe.wait_ge(roped, NK + h + 1)
            if not isinstance(h, int) or h >= 1:
                pe.wait_ge(c_tr, h)
            for m in range(TM):
                mm = nc.tensor.transpose(s.mb[3][:, m * P:(m + 1) * P], qr[:, e, m, :], s.ident)
            mm.then_inc(turned, 1)

        @block.tensor
        def _(pe):
            def cmp_scores(h, e):
                pe.wait_ge(turned_read, 2 * h + 1)
                for m in range(TM):
                    mm = nc.tensor.matmul(s.mb[2][:, m * 64:(m + 1) * 64], qT[:, e, m * P:(m + 1) * P], s.kcT[:, :],
                                          start=True, stop=True)
                mm.then_inc(c_s, 1)

            def cmp_turn(h, e):
                pe.wait_ge(c_v, C_V * h + 6)
                pe.wait_ge(turned_read, 2 * h + 2)
                for m in range(TM):
                    mm = nc.tensor.transpose(s.mb[3][:, m * P:(m + 1) * P], pcw[:, e, m * 64:m * 64 + P], s.ident)
                mm.then_inc(c_t, 1)

            def cmp_values(h, e, early):
                pe.wait_ge(c_tr, h + 1)
                if not early:
                    pe.wait_ge(a.o_lo, h - 1)
                nc.tensor.matmul(s.mb[e][:, :], s.vc[:, :], pcT[:, e, :], start=True, stop=False,
                                 skip_group_check=True).then_inc(c_pv, 1)

            def pair(j, first, last):
                for e in range(2):
                    h = 2 * j + e
                    start = first and e == 0
                    more = not (last and e == 1)
                    for i in range(8):
                        br, n = i // 4, i % 4
                        I = 8 * h + i
                        if i == 0:
                            pe.wait_ge(turned_read, 2 * h + 2)
                        item_scores(nc, pe, s, a, I, n, qrT[:, e], lambda w: kT[:, br, ds(j // 2, 1), 0:w].rearrange(
                            "p o t -> p (o t)"), None, start and i < 2)
                        if i >= 2 or not start:
                            item_turn(nc, pe, s, a, I - 2, (n - 2) % 4, start and i < 4)
                        if i == 0 and not start:
                            cmp_turn(h, e)
                        if i == 2:
                            cmp_values(h, e, first)
                        if i >= 3:
                            if i == 3:
                                pe.wait_ge(v_in[e], 32 * (j + 1))
                            item_values(nc, pe, s, a, I - 3, (n - 3) % 4, vv[:, e, (i - 3) // 4], s.mb[e], False)
                        elif not start:
                            item_values(nc, pe, s, a, I - 3, n + 1, vv[:, 1 - e, 1], s.mb[1 - e], False)
                        if more:
                            if i == 1:
                                turn_plain(pe, h + 1, 1 - e)
                            if i == 3:
                                cmp_scores(h + 1, 1 - e)
                            if i == 5:
                                turn_roped(pe, h + 1, 1 - e)
            pe.wait_ge(pad_zero, 1)
            turn_plain(pe, 0, 0)
            turn_roped(pe, 0, 0)
            cmp_scores(0, 0)
            cmp_turn(0, 0)
            pair(0, True, False)
            with pe.Fori(1, PAIRS - 1) as j:
                pair(j, False, False)
            pair(PAIRS - 1, False, True)
            END = 8 * NSA
            item_turn(nc, pe, s, a, END - 2, 2, False)
            item_values(nc, pe, s, a, END - 3, 1, vv[:, 1, 1], s.mb[1], False)
            item_turn(nc, pe, s, a, END - 1, 3, False)
            for n in (2, 3):
                item_values(nc, pe, s, a, END - 4 + n, n, vv[:, 1, 1], s.mb[1], False)

        @block.scalar
        def _(act):
            def read_plain(h, e):
                act.wait_ge(turned, 2 * h + 1)
                nc.scalar.activation(qT[:, e], s.mb[2][:, :], ACT.Copy).then_inc(turned_read, 1)

            def read_roped(h, e):
                act.wait_ge(turned, 2 * h + 2)
                nc.scalar.activation(qrT[:, e], s.mb[3][:, :], ACT.Copy).then_inc(turned_read, 1)

            def cmp_exp(h, e):
                act.wait_ge(c_v, C_V * h + 2)
                nc.scalar.activation(pc[:, e], pc[:, e], ACT.Exp).then_inc(c_e, 1)

            def cmp_read(h, e, early=False):
                act.wait_ge(c_t, h + 1)
                if not early:
                    act.wait_ge(c_pv, h - 1)
                nc.scalar.activation(pcT[:, e, :], s.mb[3][0:64, :], ACT.Copy).then_inc(c_tr, 1)

            def o_hi(h, e):
                act.wait_ge(a.pv_done, 8 * h + 8)
                nc.scalar.activation(s.act_hi[:, ds(FOX + h, 1), :].rearrange("p o t -> p (o t)"), s.mb[e][:, :],
                                     ACT.Copy).then_inc(a.o_hi, 1)

            def pair(j, first, last):
                for e in range(2):
                    h = 2 * j + e
                    start = first and e == 0
                    more = not (last and e == 1)
                    for i in range(8):
                        item_exp(nc, act, s, a, 8 * h + i, i % 4, start and i < 4)
                        if i >= 2 or not start:
                            item_copy(nc, act, s, a, 8 * h + i - 2, (i - 2) % 4, start and i < 4)
                        if i == 3:
                            if not start:
                                o_hi(h - 1, 1 - e)
                        if i == 0 and not start:
                            cmp_read(h, e, first)
                        if more:
                            if i == 1:
                                read_plain(h + 1, 1 - e)
                            if i == 4:
                                cmp_exp(h + 1, 1 - e)
                            if i == 5:
                                read_roped(h + 1, 1 - e)
            read_plain(0, 0)
            read_roped(0, 0)
            cmp_exp(0, 0)
            cmp_read(0, 0, True)
            pair(0, True, False)
            with act.Fori(1, PAIRS - 1) as j:
                pair(j, False, False)
            pair(PAIRS - 1, False, True)
            for n in (2, 3):
                item_copy(nc, act, s, a, 8 * NSA - 4 + n, n, False)
            o_hi(NSA - 1, 1)

        @block.vector
        def _(dve):
            def gain(h, e, uses):
                dve.wait_ge(q_in[e], 16 * uses)
                if not isinstance(h, int) or h >= 2:
                    dve.wait_ge(turned, 2 * h - 2)
                nc.vector.tensor_tensor(qn[:, e], nq[:, e], s.gain_bc[:, 0:1, :].broadcast_to([P, TM, HD]),
                                        ALU.mult).then_inc(gained, 1)

            def table(at, j):
                return tabs[:, ds(at + 256 * (j // 2), 256)].rearrange("p (m n) -> p m n", m=TM)

            def cmp_masked(h, e, j):
                dve.wait_ge(c_s, h + 1)
                nc.vector.tensor_tensor(pc[:, e], s.mb[2][:, 0:256].rearrange("p (m n) -> p m n", m=TM),
                                        table(N_NEG, j), ALU.add).then_inc(c_v, 1)
                dve.wait_ge(c_v, C_V * h + 1)
                nc.vector.tensor_reduce(cst[:, 0, :], pc[:, e], AX.X, ALU.max).then_inc(c_m, 1)

            def cmp_shifted(h, e):
                dve.wait_ge(c_m, h + 1)
                nc.vector.tensor_tensor(pc[:, e], pc[:, e], cst[:, 0, :].unsqueeze(2).broadcast_to([P, TM, 64]),
                                        ALU.subtract).then_inc(c_v, 1)

            def cmp_sum(h, e, j):
                dve.wait_ge(c_e, h + 1)
                nc.vector.tensor_tensor(pc[:, e], pc[:, e], table(N_MASK, j), ALU.mult).then_inc(c_v, 1)
                dve.wait_ge(c_v, C_V * h + 3)
                nc.vector.tensor_reduce(cst[:, 1, :], pc[:, e], AX.X, ALU.add).then_inc(c_v, 1)

            def cmp_factor(h):
                dve.wait_ge(c_v, C_V * h + 4)
                nc.vector.tensor_scalar(cst[:, 1, :], cst[:, 1, :], 1e-30, None, ALU.max).then_inc(c_r, 1)
                dve.wait_ge(c_r, 2 * h + 1)
                nc.vector.reciprocal(cst[:, 2, :], cst[:, 1, :]).then_inc(c_r, 1)
                dve.wait_ge(c_r, 2 * h + 2)
                nc.vector.tensor_tensor(cst[:, 3, :], cst[:, 2, :], s.gates[:, :, ds(FOX + 3 * h, 1)].rearrange(
                    "p m o -> p (m o)"), ALU.mult).then_inc(c_v, 1)

            def cmp_normalise(h, e):
                dve.wait_ge(c_v, C_V * h + 5)
                nc.vector.tensor_tensor(pc[:, e], pc[:, e], cst[:, 3, :].unsqueeze(2).broadcast_to([P, TM, 64]),
                                        ALU.mult).then_inc(c_v, 1)

            c_m, c_r = sem("cmp_max"), sem("cmp_r")

            def o_lo(h, e):
                dve.wait_ge(a.o_hi, h + 1)
                nc.vector.tensor_tensor(s.act_lo[:, ds(FOX + h, 1), :].rearrange("p o t -> p (o t)"), s.mb[e][:, :],
                                        s.act_hi[:, ds(FOX + h, 1), :].rearrange("p o t -> p (o t)").bitcast(F32),
                                        ALU.subtract).then_inc(a.o_lo, 1)

            def gate(h, br):
                return lambda n: s.gates[:, n, ds(FOX + 3 * h + 1 + br, 1)]

            def pair(j, first, last):
                for e in range(2):
                    h = 2 * j + e
                    start = first and e == 0
                    more = not (last and e == 1)
                    for i in range(8):
                        br, n = i // 4, i % 4
                        I = 8 * h + i
                        item_max(nc, dve, s, a, I, n)
                        if i >= 1 or not start:
                            item_reciprocal(nc, dve, s, a, I - 1, (n - 1) % 4)
                            item_normalise(nc, dve, s, a, I - 1, (n - 1) % 4,
                                           gate(h, (i - 1) // 4) if i else gate(h - 1, 1))
                        if i == 4 and not start:
                            o_lo(h - 1, 1 - e)
                        if more:
                            if i == 0:
                                gain(h + 1, 1 - e, j + e + 1)
                            if i == 3:
                                cmp_masked(h + 1, 1 - e, j + e)
                            if i == 4:
                                cmp_shifted(h + 1, 1 - e)
                            if i == 5:
                                cmp_sum(h + 1, 1 - e, j + e)
                            if i == 6:
                                cmp_factor(h + 1)
                            if i == 7:
                                cmp_normalise(h + 1, 1 - e)
            cmp_masked(0, 0, 0)
            cmp_shifted(0, 0)
            cmp_sum(0, 0, 0)
            cmp_factor(0)
            cmp_normalise(0, 0)
            pair(0, True, False)
            with dve.Fori(1, PAIRS - 1) as j:
                pair(j, False, False)
            pair(PAIRS - 1, False, True)
            item_reciprocal(nc, dve, s, a, 8 * NSA - 1, 3)
            item_normalise(nc, dve, s, a, 8 * NSA - 1, 3, gate(NSA - 1, 1))
            o_lo(NSA - 1, 1)



def phase_out(nc, A, s):
    with ExitStack() as ctx:
        gated = s.gated
        sem = s.sem
        square = ctx.enter_context(nc.sbuf_tensor("out_square", [P, 512], F32))
        x_in, added, squared = sem("x2_in"), sem("out_added"), sem("out_squared")

        block = ctx.enter_context(nc.Block())

        @block.sync
        def _(sp):
            for u in (1, 2):
                load_unit(sp, s, PAIR_OUT + u // 2, u % 2, w_out_unit(A, 0, u))
            for m in range(TM):
                sp.dma_start(s.x2[:, m, :], A.x[0, m * P:(m + 1) * P, :]).then_inc(x_in, 16)

            def loads(n, following):
                load_unit(sp, s, PAIR_OUT + 2 * n + 1, 1, w_out_unit(A, n, 3))
                for u in range(3):
                    load_unit(sp, s, PAIR_OUT + 2 * n + 2 + u // 2, u % 2, following(u))
            with sp.Fori(0, 3) as n:
                loads(n, lambda u: w_out_unit(A, n + 1, u))
            loads(3, lambda u: w_up_unit(A, 0, u))

        @block.tensor
        def _(pe):
            with pe.Fori(0, 4) as n:
                for u in range(4):
                    rows_unit(nc, pe, s, PAIR_OUT + 2 * n + u // 2, u % 2, s.act_hi, s.act_lo, 4 * u, u == 0, u == 3,
                              ROUND_OUT + n)

        @block.scalar
        def _(act):
            def body(n, early):
                for u in range(1, 5):
                    split_hi(nc, act, s, PAIR_OUT + 2 * n + u // 2, u % 2)
                for m in range(TM):
                    act.wait_ge(added, 4 * n + m + 1)
                    if not early or m:
                        act.wait_ge(squared, 4 * n + m)
                    nc.scalar.activation(square[:, :], s.x2[:, m, ds(n * 512, 512)], ACT.Square,
                                         accum_out=s.ssq2[:, m, ds(n, 1)]).then_inc(squared, 1)
            body(0, True)
            with act.Fori(1, 4) as n:
                body(n, False)

        @block.vector
        def _(dve):
            def body(n, first):
                for u in range(1, 5):
                    split_lo(nc, dve, s, PAIR_OUT + 2 * n + u // 2, u % 2)
                for m in range(TM):
                    await_bank(dve, s, ROUND_OUT + n, m, 2 * PAIR_OUT + 4 * n + 3)
                    if not first or m >= 2:
                        dve.wait_ge(added, 4 * n + m - 1)
                    nc.vector.tensor_tensor(gated[:, m % 2, :], s.gb[m][:, :], s.gate_bc[0][:, ds(n * 512, 512)],
                                            ALU.mult).then_inc(s.bank_free, 1)
            body(0, True)
            with dve.Fori(1, 4) as n:
                body(n, False)

        @block.gpsimd
        def _(pool):
            pool.wait_ge(x_in, 64)
            with pool.Fori(0, 4) as n:
                for m in range(TM):
                    pool.wait_ge(s.bank_free, 4 * (ROUND_OUT + n) + m + 1)
                    part = s.x2[:, m, ds(n * 512, 512)]
                    nc.gpsimd.tensor_tensor(part, part, gated[:, m % 2, :], ALU.add).then_inc(added, 1)



def phase_norm2(nc, A, s):
    with ExitStack() as ctx:
        sb = lambda name, shape, dt=F32: ctx.enter_context(nc.sbuf_tensor(name, shape, dt))
        sem = s.sem
        xn = sb("xn2", [P, TM, D])
        st = sb("stats2", [P, 4, TM])
        ms_ready, rms_ready, rstd_ready = sem("ms2"), sem("rms2"), sem("rstd2")
        xn_vector, xn_scalar = sem("xn2_vector"), sem("xn2_scalar")
        tmp = s.gate_bc[0][:, :].rearrange("p (e t) -> p e t", e=4)
        q = modulate_state(sem, "h2_", s.mb, tmp, s.mod[:, 2, :], s.mod[:, 3, :])

        block = ctx.enter_context(nc.Block())

        @block.sync
        def _(sp):
            load_unit(sp, s, PAIR_FF + 1, 1, w_up_unit(A, 0, 3))
            for u in range(3):
                load_unit(sp, s, PAIR_FF + 2 + u // 2, u % 2, w_up_unit(A, 1, u))

        @block.scalar
        def _(act):
            act.wait_ge(ms_ready, 2)
            nc.scalar.activation(st[:, 2, :], st[:, 1, :], ACT.Sqrt).then_inc(rms_ready, 1)
            act.wait_ge(rstd_ready, 1)

            def normalise(g):
                for m in (2, 3):
                    nc.scalar.activation(xn[:, m, g * 512:(g + 1) * 512], s.x2[:, m, g * 512:(g + 1) * 512], ACT.Copy,
                                         scale=st[:, 3, m:m + 1]).then_inc(xn_scalar, 1)
            normalise(0)
            for g in range(4):
                if g < 3:
                    normalise(g + 1)
                modulate_scalar(nc, act, s, g, q)
                split_hi(nc, act, s, PAIR_FF + (g + 1) // 2, (g + 1) % 2)

        @block.tensor
        def _(pe):
            def turn(g):
                pe.wait_ge(xn_vector, 2 * g + 2)
                pe.wait_ge(xn_scalar, 2 * g + 2)
                modulate_tensor(nc, pe, s, xn, g, q)
            turn(0)
            for g in range(4):
                if g < 3:
                    turn(g + 1)
                pe.wait_ge(q.lo, 4 * g + 4)
                cols_unit(nc, pe, s, PAIR_FF + g // 2, g % 2, 4 * g, g == 0, g == 3, ROUND_FF)

        @block.vector
        def _(dve):
            nc.vector.tensor_reduce(st[:, 0, :], s.ssq2[:, :, :], AX.X, ALU.add).then_inc(ms_ready, 1)
            dve.wait_ge(ms_ready, 1)
            nc.vector.tensor_scalar(st[:, 1, :], st[:, 0, :], 1.0 / D, EPS, ALU.mult, ALU.add).then_inc(ms_ready, 1)
            dve.wait_ge(rms_ready, 1)
            nc.vector.reciprocal(st[:, 3, :], st[:, 2, :]).then_inc(rstd_ready, 1)
            dve.wait_ge(rstd_ready, 1)

            def normalise(g):
                for m in (0, 1):
                    nc.vector.tensor_scalar(xn[:, m, g * 512:(g + 1) * 512], s.x2[:, m, g * 512:(g + 1) * 512],
                                            st[:, 3, m:m + 1], None, ALU.mult).then_inc(xn_vector, 1)
            normalise(0)
            for g in range(4):
                if g < 3:
                    normalise(g + 1)
                modulate_vector(nc, dve, s, g, q)
                split_lo(nc, dve, s, PAIR_FF + (g + 1) // 2, (g + 1) % 2)



def phase_mlp(nc, A, s):
    with ExitStack() as ctx:
        sb = lambda name, shape, dt=F32: ctx.enter_context(nc.sbuf_tensor(name, shape, dt))
        sem = s.sem
        u_hi, u_lo = sb("u_hi", [P, 8, T], F32R), sb("u_lo", [P, 8, T], F32R)
        spare = s.gate_bc[0][:, :].rearrange("p (a e t) -> p a e t", a=2, e=2)
        relu, squ = spare[:, 0], spare[:, 1]
        gated = s.gated
        sq_n, hi_n, lo_n, added = sem("relu_sq_n"), sem("u_hi_n"), sem("u_lo_n"), sem("mlp_added")
        out_stored = sem("out_stored")

        block = ctx.enter_context(nc.Block())

        @block.sync
        def _(sp):
            def down_loads(c, n):
                for u in range(2):
                    load_unit(sp, s, PAIR_FF + 8 * c + 4 + n, u, w_down_unit(A, c, n, u))

            def up_loads(c, b, units):
                for u in units:
                    load_unit(sp, s, PAIR_FF + 8 * c + 2 * b + u // 2, u % 2, w_up_unit(A, 2 * c + b, u))
            up_loads(0, 1, (3,))
            with sp.Fori(0, CHUNKS - 1) as c:
                with sp.Fori(0, 4) as n:
                    down_loads(c, n)
                with sp.Fori(0, 2) as b:
                    up_loads(c + 1, b, range(4))
            with sp.Fori(0, 4) as n:
                down_loads(CHUNKS - 1, n)
            with sp.Fori(0, 4) as n:
                for m in range(TM):
                    sp.wait_ge(added, 16 * (CHUNKS - 1) + 4 * n + m + 1)
                    sp.dma_start(A.out[0, m * P:(m + 1) * P, ds(n * 512, 512)], s.x2[:, m, ds(n * 512, 512)]).then_inc(
                        out_stored, 16)
            sp.wait_ge(out_stored, 256)

        @block.tensor
        def _(pe):
            def up(c, b):
                for u in range(4):
                    cols_unit(nc, pe, s, PAIR_FF + 8 * c + 2 * b + u // 2, u % 2, 4 * u, u == 0, u == 3,
                              ROUND_FF + 6 * c + b)

            def down(c):
                with pe.Fori(0, 4) as n:
                    for u in range(2):
                        pe.wait_ge(lo_n, 8 * c + 4 * u + 4)
                        rows_unit(nc, pe, s, PAIR_FF + 8 * c + 4 + n, u, u_hi, u_lo, 4 * u, u == 0, u == 1,
                                  ROUND_FF + 6 * c + 2 + n)
            up(0, 1)
            down(0)
            with pe.Fori(1, CHUNKS) as c:
                with pe.Fori(0, 2) as b:
                    up(c, b)
                down(c)

        @block.scalar
        def _(act):
            def hi(t, b, m):
                act.wait_ge(sq_n, t + 1)
                nc.scalar.activation(tile(u_hi, 4 * b + m), squ[:, m % 2, :], ACT.Copy).then_inc(hi_n, 1)

            def up(c, b, first=False):
                for m in range(4):
                    t = 8 * c + 4 * b + m
                    await_bank(act, s, ROUND_FF + 6 * c + b, m, 2 * PAIR_FF + 16 * c + 4 * b + 3)
                    if not first or m >= 2:
                        act.wait_ge(sq_n, t - 1)
                    nc.scalar.activation(relu[:, m % 2, :], s.gb[m][:, :], ACT.Relu).then_inc(s.bank_free, 1)
                    if m >= 1:
                        hi(t - 1, b, m - 1)
                hi(8 * c + 4 * b + 3, b, 3)

            def splits(pair, units):
                for u in units:
                    split_hi(nc, act, s, pair + u // 2, u % 2)

            up(0, 0, True)
            splits(PAIR_FF + 2, range(1, 5))
            up(0, 1)
            with act.Fori(0, 4) as n:
                splits(PAIR_FF + 4 + n, (1, 2))
            with act.Fori(1, CHUNKS - 1) as c:
                with act.Fori(0, 2) as b:
                    splits(PAIR_FF + 8 * c + 2 * b, range(1, 5))
                    up(c, b)
                with act.Fori(0, 4) as n:
                    splits(PAIR_FF + 8 * c + 4 + n, (1, 2))
            with act.Fori(0, 2) as b:
                splits(PAIR_FF + 8 * (CHUNKS - 1) + 2 * b, range(1, 5))
                up(CHUNKS - 1, b)
            with act.Fori(0, 3) as n:
                splits(PAIR_FF + 8 * (CHUNKS - 1) + 4 + n, (1, 2))
            splits(PAIR_FF + 8 * (CHUNKS - 1) + 7, (1,))

        @block.vector
        def _(dve):
            def lo(t, b, m):
                dve.wait_ge(hi_n, t + 1)
                nc.vector.tensor_tensor(tile(u_lo, 4 * b + m), squ[:, m % 2, :], tile(u_hi, 4 * b + m).bitcast(F32),
                                        ALU.subtract).then_inc(lo_n, 1)

            def up(c, b, first=False):
                for m in range(4):
                    t = 8 * c + 4 * b + m
                    dve.wait_ge(s.bank_free, 4 * (ROUND_FF + 6 * c + b) + m + 1)
                    if not first or m >= 2:
                        dve.wait_ge(lo_n, t - 1)
                    nc.vector.tensor_tensor(squ[:, m % 2, :], relu[:, m % 2, :], relu[:, m % 2, :], ALU.mult).then_inc(sq_n, 1)
                    if m >= 1:
                        lo(t - 1, b, m - 1)
                lo(8 * c + 4 * b + 3, b, 3)

            def splits(pair, units):
                for u in units:
                    split_lo(nc, dve, s, pair + u // 2, u % 2)

            def gate(c, n, first=False):
                for m in range(TM):
                    e = 16 * c + 4 * n + m
                    await_bank(dve, s, ROUND_FF + 6 * c + 2 + n, m, 2 * PAIR_FF + 16 * c + 8 + 2 * n + 1)
                    if not first or m >= 2:
                        dve.wait_ge(added, e - 1)
                    nc.vector.tensor_tensor(gated[:, m % 2, :], s.gb[m][:, :], s.gate_bc[1][:, ds(n * 512, 512)],
                                            ALU.mult).then_inc(s.bank_free, 1)

            def down(c, n):
                splits(PAIR_FF + 8 * c + 4 + n, (1, 2))
                gate(c, n)

            up(0, 0, True)
            splits(PAIR_FF + 2, range(1, 5))
            up(0, 1)
            splits(PAIR_FF + 4, (1, 2))
            gate(0, 0, True)
            with dve.Fori(1, 4) as n:
                down(0, n)
            with dve.Fori(1, CHUNKS - 1) as c:
                with dve.Fori(0, 2) as b:
                    splits(PAIR_FF + 8 * c + 2 * b, range(1, 5))
                    up(c, b)
                with dve.Fori(0, 4) as n:
                    down(c, n)
            with dve.Fori(0, 2) as b:
                splits(PAIR_FF + 8 * (CHUNKS - 1) + 2 * b, range(1, 5))
                up(CHUNKS - 1, b)
            with dve.Fori(0, 3) as n:
                down(CHUNKS - 1, n)
            splits(PAIR_FF + 8 * (CHUNKS - 1) + 7, (1,))
            gate(CHUNKS - 1, 3)

        @block.gpsimd
        def _(pool):
            with pool.Fori(0, CHUNKS) as c:
                with pool.Fori(0, 4) as n:
                    for m in range(TM):
                        pool.wait_ge(s.bank_free, 4 * (ROUND_FF + 6 * c + 2 + n) + m + 1)
                        part = s.x2[:, m, ds(n * 512, 512)]
                        nc.gpsimd.tensor_tensor(part, part, gated[:, m % 2, :], ALU.add).then_inc(added, 1)


def build(nc, A):
    with ExitStack() as ctx:
        sb = lambda name, shape, dt=F32: ctx.enter_context(nc.sbuf_tensor(name, shape, dt))
        sem = lambda name: ctx.enter_context(nc.semaphore(name))
        s = Names()
        s.sem = sem
        s.act_hi, s.act_lo = sb("act_hi", [P, KT, T], F32R), sb("act_lo", [P, KT, T], F32R)
        s.w_raw = sb("w_raw", [P, 2, 4, 512])
        s.w_hi, s.w_lo = sb("w_hi", [P, 2, 4, 512], F32R), sb("w_lo", [P, 2, 4, 512], F32R)
        s.base = sb("base_consts", [P, C_END])
        s.ident = s.base[:, C_ID:C_ID + P]
        s.ones = sb("ones", [P, P])
        s.ident_bf, s.causal_bf = sb("ident_bf", [P, P], mybir.dt.bfloat16), sb("causal_bf", [P, P], mybir.dt.bfloat16)
        s.cols1, s.cols2 = sb("cols1", [P, P]), sb("cols2", [P, P])
        s.c_col = sb("c_col", [P, 4, KT])
        s.mod = sb("mod", [P, 6, KT])
        s.fq_gain = sb("fq_gain", [P, 1])
        s.gain_bc = sb("gain_bc", [P, 3, HD])
        s.cum, s.auxR = sb("cum", [NZ, T]), sb("auxR", [NZ, T])
        s.gates = sb("gates", [P, TM, NZ])
        s.kcT, s.vc = sb("kcT", [P, 64]), sb("vc", [64, HD])
        s.gb = [ctx.enter_context(nc.psum_tensor(f"gemm_bank{m}", [P, 512], F32)) for m in range(4)]
        s.mb = [ctx.enter_context(nc.psum_tensor(f"misc_bank{m}", [P, 512], F32)) for m in range(4)]
        s.w_landed = [sem(f"w_landed{i}") for i in range(2)]
        s.w_hi_ready, s.w_lo_ready, s.unit_used = sem("w_hi_ready"), sem("w_lo_ready"), sem("unit_used")
        s.bank_done, s.bank_free = sem("bank_done"), sem("bank_free")
        s.wz, s.wz_in = sb("narrow_columns", [P, 2 * 512]), sem("wz_in")
        s.gated = s.wz[:, :].rearrange("p (e n) -> p e n", e=2)
        s.ssq2 = sb("ssq2", [P, TM, 4])
        s.proj_stored = [sem(f"proj_stored{m}") for m in range(TM)]
        s.gates_ready, s.cmp_ready = sem("gates_ready"), sem("cmp_ready")
        s.proj = nc.dram_tensor("proj", [NB_IN, TM, P, 512], F32).ap()

        phase_start(nc, A, s)
        with nc.sbuf_tensor("gate2_bc", [P, D], F32) as gate2:
            with nc.sbuf_tensor("gate1_bc", [P, D], F32) as gate1:
                s.gate_bc = [gate1, gate2]
                phase_project(nc, A, s)
                phase_compress(nc, A, s)
                with ExitStack() as sparse:
                    s.sparse, s.key_read = sparse_state(sparse, nc, s), sem("nsa_key_read")
                    phase_fox(nc, A, s)
                    phase_nsa(nc, A, s)
                with nc.sbuf_tensor("x2", [P, TM, D], F32) as x2:
                    s.x2 = x2
                    phase_out(nc, A, s)
                    phase_norm2(nc, A, s)
                    phase_mlp(nc, A, s)


INPUTS = ["x", "c", "w_ada", "b_ada", "norm1_g", "w_in", "b_forget", "fox_q_norm", "fox_k_norm", "nsa_q_norm",
          "cmp_k_norm", "slc_k_norm", "win_k_norm", "cmp_pe_k", "cmp_w1_k", "cmp_w2_k", "cmp_pe_v", "cmp_w1_v",
          "cmp_w2_v", "w_out", "norm2_g", "w_up", "w_down"]


def kernel(**inputs):
    import concourse.bacc as _bacc
    from concourse.bass_utils import run_bass_kernel_spmd as _run

    nc = _bacc.Bacc("TRN2", target_bir_lowering=False, num_devices=1)
    base, nsa_tabs = host_constants()
    arrays = {name: np.ascontiguousarray(inputs[name]) for name in INPUTS}
    arrays["base"], arrays["nsa_tabs"] = base, nsa_tabs
    fields = {name: nc.dram_tensor("in_" + name, a.shape, mybir.dt.from_np(a.dtype), kind="ExternalInput").ap()
              for name, a in arrays.items()}
    fields["out"] = nc.dram_tensor("out", (1, T, D), F32, kind="ExternalOutput").ap()
    A = namedtuple("Arrays", fields)(**fields)
    build(nc, A)
    r = _run(nc, [{"in_" + name: a for name, a in arrays.items()}], core_ids=[0])
    return r.results[0]["out"]
```

```python
from collections import namedtuple
from contextlib import ExitStack

import numpy as np

import concourse.bass as bass
from concourse import mybir

F32 = mybir.dt.float32
F32R = mybir.dt.float32r
ALU = mybir.AluOpType
ACT = mybir.ActivationFunctionType
AX = mybir.AxisListType
ds = bass.ds


class Names:
    pass

P = 128
T = 512
TM = T // P
D = 2048
KT = D // P
HD = 128
FOX = 8
NSA = 8
NG = 2
FF = 4 * D
CMP_LEN, CMP_STRIDE = 32, 16
NCMP = (T - CMP_LEN) // CMP_STRIDE + 1
CW = 32
CMP_HID = 2 * HD
NB_IN = 11
FOX_COLS = 3 * FOX * HD
FZ = FOX_COLS
GZ = FZ + FOX + 5 * 512
NZ = 40
ND = 3 * NZ
ZW = KT * NZ + P
XW = CMP_LEN * 64 + 64
EPS = 1e-6
SCALE = HD ** -0.5
NEG = -1e30

C_ID, C_CAUSAL, C_FLAG, C_NFLAG, C_M1, C_M2, C_N1, C_N2, C_END = 0, 128, 256, 300, 344, 352, 360, 361, 362
N_MASK, N_NEG, N_COS, N_SIN, N_END = 0, 512, 1024, 1536, 2048

PAIR_CMP = 2 * NB_IN
PAIR_OUT = PAIR_CMP + 4
PAIR_FF = PAIR_OUT + 8
CHUNKS = 8
PAIR_END = PAIR_FF + 8 * CHUNKS
ROUND_OUT = NB_IN
ROUND_FF = ROUND_OUT + 4


def host_constants():
    p = np.arange(P)[:, None]
    base = np.zeros((P, C_END), np.float32)
    base[:, C_ID:C_ID + P] = np.eye(P)
    base[:, C_CAUSAL:C_CAUSAL + P] = np.where(np.arange(P)[None, :] <= p, 0.0, NEG)
    flag = np.zeros((NB_IN, 4), np.float32)
    flag[[0, 1, 2, 3, 6, 7]] = 1.0
    flag[9:11, 0:2] = 1.0
    base[:, C_FLAG:C_FLAG + 44] = flag.reshape(1, 44)
    base[:, C_NFLAG:C_NFLAG + 44] = 1.0 - flag.reshape(1, 44)
    h = np.arange(FOX)[None, :]
    row = np.where(p < ND, p % NZ, -1)
    base[:, C_M1:C_M1 + FOX] = row == h
    base[:, C_M2:C_M2 + FOX] = -1.0 * (row == 32 + h)
    base[:, C_N1] = row[:, 0] >= 32
    base[:, C_N2] = (row[:, 0] >= 0) & (row[:, 0] < FOX)

    nsa = np.zeros((P, N_END), np.float32)
    m = np.arange(TM)[None, :, None]
    n = np.arange(NG * CW)[None, None, :]
    t = m * P + p[:, :, None]
    for g in range(NG):
        see = (n // CW == g) & (n % CW < NCMP) & ((n % CW) * CMP_STRIDE + CMP_LEN - 1 <= t)
        nsa[:, N_MASK + g * 256:N_MASK + (g + 1) * 256] = see.reshape(P, 256)
        nsa[:, N_NEG + g * 256:N_NEG + (g + 1) * 256] = np.where(see, 0.0, NEG).reshape(P, 256)
    half = HD // 2
    inv = np.float32(10000.0) ** (-np.arange(half, dtype=np.float32) / np.float32(half))
    ang = (np.arange(T, dtype=np.float32)[:, None] * inv[None, :]).astype(np.float32)
    cos, sin = np.cos(ang), np.sin(ang)
    cos2 = np.concatenate([cos, cos], 1).reshape(TM, P, HD).transpose(1, 0, 2)
    sin2 = np.concatenate([-sin, sin], 1).reshape(TM, P, HD).transpose(1, 0, 2)
    nsa[:, N_COS:N_COS + 512] = cos2.reshape(P, 512)
    nsa[:, N_SIN:N_SIN + 512] = sin2.reshape(P, 512)
    return base, nsa



def load_unit(sp, s, pair, slot, src, first=False):
    if not first:
        sp.wait_ge(s.w_lo_ready, 2 * pair + slot - 1)
    sp.dma_start(s.w_raw[:, slot], src).then_inc(s.w_landed[slot], 16)


def split_hi(nc, act, s, pair, slot, first=False):
    act.wait_ge(s.w_landed[slot], 16 * (pair + 1))
    if not first:
        act.wait_ge(s.unit_used, 2 * pair + slot - 1)
    nc.scalar.activation(s.w_hi[:, slot], s.w_raw[:, slot], ACT.Copy).then_inc(s.w_hi_ready, 1)


def split_lo(nc, dve, s, pair, slot):
    dve.wait_ge(s.w_hi_ready, 2 * pair + slot + 1)
    nc.vector.tensor_tensor(s.w_lo[:, slot], s.w_raw[:, slot], s.w_hi[:, slot].bitcast(F32),
                            ALU.subtract).then_inc(s.w_lo_ready, 1)


def split_lo_gpsimd(nc, pool, s, pair, slot):
    pool.wait_ge(s.w_hi_ready, 2 * pair + slot + 1)
    nc.gpsimd.tensor_tensor(s.w_lo[:, slot], s.w_raw[:, slot], s.w_hi[:, slot].bitcast(F32),
                            ALU.subtract).then_inc(s.w_lo_ready, 1)


def await_bank(eng, s, product_round, m, last_unit):
    if m < 3:
        eng.wait_ge(s.bank_done, 3 * product_round + m + 1)
    else:
        eng.wait_ge(s.unit_used, last_unit + 1)


def three_products(nc, out, a_hi, a_lo, b_hi, b_lo, start, stop):
    nc.tensor.matmul(out, a_hi, b_hi, start=start, stop=False)
    nc.tensor.matmul(out, a_hi, b_lo, start=False, stop=False)
    return nc.tensor.matmul(out, a_lo, b_hi, start=False, stop=stop)


def rows_unit(nc, pe, s, pair, slot, lhs_hi, lhs_lo, k0, first, last, round_):
    pe.wait_ge(s.w_lo_ready, 2 * pair + slot + 1)
    for m in range(TM):
        if first and not (isinstance(round_, int) and round_ == 0):
            pe.wait_ge(s.bank_free, 4 * round_ + m - 3)
        for kk in range(4):
            tok = slice(m * P, (m + 1) * P)
            mm = three_products(nc, s.gb[m][:, :], lhs_hi[:, k0 + kk, tok], lhs_lo[:, k0 + kk, tok],
                                s.w_hi[:, slot, kk, :], s.w_lo[:, slot, kk, :],
                                first and kk == 0, last and kk == 3)
        if last and m < 3:
            mm.then_inc(s.bank_done, 1)
    mm.then_inc(s.unit_used, 1)


def cols_unit(nc, pe, s, pair, slot, k0, first, last, round_):
    pe.wait_ge(s.w_lo_ready, 2 * pair + slot + 1)
    for m in range(4):
        if first and not (isinstance(round_, int) and round_ == 0):
            pe.wait_ge(s.bank_free, 4 * round_ + m - 3)
        for kk in range(4):
            col = slice(m * P, (m + 1) * P)
            mm = three_products(nc, s.gb[m][:, :], s.w_hi[:, slot, kk, col], s.w_lo[:, slot, kk, col],
                                s.act_hi[:, k0 + kk, :], s.act_lo[:, k0 + kk, :],
                                first and kk == 0, last and kk == 3)
        if last and m < 3:
            mm.then_inc(s.bank_done, 1)
    mm.then_inc(s.unit_used, 1)



def modulate_tensor(nc, pe, s, xn, g, q):
    for k in range(4 * g, 4 * g + 4):
        if k >= len(q.banks):
            pe.wait_ge((q.a_done, q.b_done)[k % 2], (k - len(q.banks)) // 2 + 1)
        for m in range(TM):
            mm = nc.tensor.transpose(q.banks[k % len(q.banks)][:, m * P:(m + 1) * P], xn[:, m, k * P:(k + 1) * P], s.ident)
        mm.then_inc(q.turned, 1)


def tile(t, k):
    return t[:, ds(k, 1), :].rearrange("p o t -> p (o t)")


def modulate_scalar(nc, act, s, g, q):
    for e in range(0, 4, 2):
        act.wait_ge(q.turned, 4 * g + e + 1)
        if e == 0 and q.mod_ready is not None:
            act.wait_ge(q.mod_ready, g + 1)
        if not isinstance(g, int) or g > 0:
            act.wait_ge(q.lo, 4 * g + e - 3)
        nc.scalar.activation(q.tmp[:, e, :], q.banks[e % len(q.banks)][:, :], ACT.Identity, scale=q.a[:, ds(4 * g + e, 1)],
                             bias=q.b[:, ds(4 * g + e, 1)]).then_inc(q.a_done, 1)
        act.wait_ge(q.a_done, 2 * g + e // 2 + 1)
        nc.scalar.activation(tile(s.act_hi, 4 * g + e), q.tmp[:, e, :], ACT.Copy).then_inc(q.hi, 1)
        act.wait_ge(q.b_done, 2 * g + e // 2 + 1)
        nc.scalar.activation(tile(s.act_hi, 4 * g + e + 1), q.tmp[:, e + 1, :], ACT.Copy).then_inc(q.hi, 1)


def modulate_vector(nc, dve, s, g, q):
    for e in range(0, 4, 2):
        dve.wait_ge(q.turned, 4 * g + e + 2)
        nc.vector.tensor_scalar(q.tmp[:, e + 1, :], q.banks[(e + 1) % len(q.banks)][:, :], q.a[:, ds(4 * g + e + 1, 1)],
                                q.b[:, ds(4 * g + e + 1, 1)], ALU.mult, ALU.add).then_inc(q.b_done, 1)
        for o in (e, e + 1):
            dve.wait_ge(q.hi, 4 * g + o + 1)
            nc.vector.tensor_tensor(tile(s.act_lo, 4 * g + o), q.tmp[:, o, :], tile(s.act_hi, 4 * g + o).bitcast(F32),
                                    ALU.subtract).then_inc(q.lo, 1)


def modulate_state(sem, tag, banks, tmp, a, b):
    q = Names()
    q.banks, q.tmp, q.a, q.b = banks, tmp, a, b
    q.turned, q.a_done, q.b_done = sem(tag + "turned"), sem(tag + "even_done"), sem(tag + "odd_done")
    q.hi, q.lo, q.mod_ready = sem(tag + "hi"), sem(tag + "lo"), None
    return q


def w_in_unit(A, block, u):
    w = A.w_in.rearrange("l (k p) n -> p (l k) n", p=P)
    return w[:, 4 * u:4 * u + 4, ds(block, 512)]


def w_cmp_unit(w1, u):
    return w1.rearrange("l (k p) n -> p (l k) n", p=P)[:, 8 * u:8 * u + 8, :].rearrange(
        "p (a b) n -> p a b n", b=2)


def w_out_unit(A, n, u):
    return A.w_out.rearrange("l (k p) n -> p (l k) n", p=P)[:, 4 * u:4 * u + 4, ds(n * 512, 512)]


def w_up_unit(A, block, u):
    return A.w_up.rearrange("l (k p) n -> p (l k) n", p=P)[:, 4 * u:4 * u + 4, ds(block * 512, 512)]


def w_down_unit(A, chunk, n, u):
    w = A.w_down.rearrange("l (k p) n -> p (l k) n", p=P)
    return w[:, ds(chunk * 8 + 4 * u, 4), ds(n * 512, 512)]



def phase_start(nc, A, s):
    with ExitStack() as ctx:
        sb = lambda name, shape, dt=F32: ctx.enter_context(nc.sbuf_tensor(name, shape, dt))
        sem = s.sem
        SLOTS, STEPS = 4, 8
        xn = sb("xn", [P, TM, D])
        ada_raw = sb("ada1_raw", [P, SLOTS, 2, 2, 512])
        acc = sb("ada1_acc", [P, 2, 2, 512])
        tmp = sb("mod1_tmp", [P, 4, T])
        rows = s.wz[:, 0:2 * P].rearrange("p (e c) -> p e c", e=2)
        ssq = sb("ssq1", [P, 16])

        consts_in, rows_in = sem("consts_in"), sem("rows_in")
        gains_in = sem("gains_in")
        x_in = [sem(f"x_in{m}") for m in range(TM)]
        ada_in = [sem(f"ada1_in{i}") for i in range(SLOTS)]
        ada_used, rows_zero = sem("ada1_used"), sem("rows_zero")
        cols_done, cols_read, c_exp, c_ready = sem("cols_done"), sem("cols_read"), sem("c_exp"), sem("c_ready")
        sq_done, ms_ready, rms_ready, rstd_ready = sem("sq1"), sem("ms1"), sem("rms1"), sem("rstd1")
        xn_ready, mod_sums, mod_part = sem("xn1_ready"), sem("mod1_sums"), sem("mod1_part")
        ones_set, scaled = sem("ones_set"), sem("gain_scaled")
        q = modulate_state(sem, "h1_", s.mb[0:2], tmp, s.mod[:, 0, :], s.mod[:, 1, :])
        q.mod_ready = sem("h1_mod_ready")
        ada = A.w_ada.rearrange("l (k p) (s n) -> p (l k) s n", p=P, n=D)

        block = ctx.enter_context(nc.Block())

        @block.sync
        def _(sp):
            sp.dma_start(s.base[:, :], A.base).then_inc(consts_in, 16)
            sp.dma_start(rows[0:96, 0, :], A.b_ada.rearrange("l (r c) -> (l r) c", c=P)).then_inc(rows_in, 16)
            sp.dma_start(rows[96:112, 0, :], A.norm1_g.rearrange("l (r c) -> (l r) c", c=P)).then_inc(rows_in, 16)
            sp.dma_start(rows[112:128, 0, :], A.norm2_g.rearrange("l (r c) -> (l r) c", c=P)).then_inc(rows_in, 16)
            sp.wait_ge(rows_zero, 1)
            sp.dma_start(rows[0:16, 1, :], A.c.rearrange("l (r c) -> (l r) c", c=P)).then_inc(rows_in, 16)
            for r, v in enumerate((A.fox_q_norm, A.fox_k_norm, A.nsa_q_norm, A.cmp_k_norm)):
                sp.dma_start(rows[16 + r:17 + r, 1, :], v).then_inc(rows_in, 16)
            sp.dma_start(rows[22:54, 1, :], A.cmp_pe_k.rearrange("l r c -> (l r) c")).then_inc(rows_in, 16)
            sp.dma_start(rows[54:86, 1, :], A.cmp_pe_v.rearrange("l r c -> (l r) c")).then_inc(rows_in, 16)

            def load_ada(g, k, used):
                if used is not None:
                    sp.wait_ge(ada_used, used)
                for r in range(2):
                    sp.dma_start(ada_raw[:, k % SLOTS, r], ada[:, 2 * k + r, 0:2, ds(g * 512, 512)]).then_inc(
                        ada_in[k % SLOTS], 16)

            for k in range(SLOTS):
                load_ada(0, k, None)
            for m in range(TM):
                sp.dma_start(xn[:, m, :], A.x[0, m * P:(m + 1) * P, :]).then_inc(x_in[m], 16)
            for r, v in enumerate((A.nsa_q_norm, A.slc_k_norm, A.win_k_norm)):
                sp.dma_start(s.gain_bc[:, r, :], v[0, :].partition_broadcast(P)).then_inc(gains_in, 16)
            for k in range(SLOTS, STEPS):
                load_ada(0, k, 2 * (k - SLOTS + 1))
            for u in range(2):
                load_unit(sp, s, 0, u, w_in_unit(A, 0, u), first=True)
            for g in range(1, 4):
                for k in range(STEPS):
                    load_ada(g, k, 2 * (STEPS * g + k - SLOTS + 1))
                    if k == 6:
                        load_unit(sp, s, (g + 1) // 2, (g + 1) % 2, w_in_unit(A, 0, g + 1) if g < 3 else w_in_unit(A, 512, 0))
            for u in (1, 2):
                load_unit(sp, s, 2 + u // 2, u % 2, w_in_unit(A, 512, u))

        @block.gpsimd
        def _(pool):
            nc.gpsimd.memset(rows[:, 1, :], 0.0).then_inc(rows_zero, 1)
            nc.gpsimd.memset(s.ones[:, :], 1.0).then_inc(ones_set, 1)
            nc.gpsimd.memset(s.wz[:, KT * NZ:KT * NZ + P], 0.0).then_inc(ones_set, 1)
            for u in range(5):
                split_lo_gpsimd(nc, pool, s, u // 2, u % 2)

        @block.scalar
        def _(act):
            act.wait_ge(cols_done, 1)
            nc.scalar.activation(s.cols1[:, :], s.mb[0][:, 0:P], ACT.Copy).then_inc(cols_read, 1)
            nc.scalar.activation(s.cols2[:, :], s.mb[0][:, P:2 * P], ACT.Copy).then_inc(cols_read, 1)
            act.wait_ge(cols_read, 2)
            nc.scalar.activation(s.c_col[:, 0, :], s.cols2[:, 0:KT], ACT.Exp, scale=-1.0).then_inc(c_exp, 1)
            junk = tmp[:, :, :].rearrange("p e t -> p (e t)")
            for m in range(TM):
                act.wait_ge(x_in[m], 16)
                nc.scalar.activation(junk, xn[:, m, :], ACT.Square, accum_out=ssq[:, m:m + 1]).then_inc(sq_done, 1)
                act.wait_ge(sq_done, m + 1)
            act.wait_ge(ms_ready, 1)
            nc.scalar.activation(ssq[:, 8:12], ssq[:, 4:8], ACT.Sqrt).then_inc(rms_ready, 1)
            act.wait_ge(rstd_ready, 1)
            for m in range(TM):
                nc.scalar.activation(xn[:, m, :], xn[:, m, :], ACT.Copy, scale=ssq[:, 12 + m:13 + m]).then_inc(xn_ready, 1)
            split_hi(nc, act, s, 0, 0, first=True)
            for g in range(4):
                if g:
                    split_hi(nc, act, s, g // 2, g % 2, first=g == 1)
                modulate_scalar(nc, act, s, g, q)
            split_hi(nc, act, s, 2, 0)

        @block.tensor
        def _(pe):
            pe.wait_ge(consts_in, 16)
            pe.wait_ge(rows_in, 16 * 10)
            nc.tensor.transpose(s.mb[0][:, 0:P], rows[:, 0, :], s.ident)
            nc.tensor.transpose(s.mb[0][:, P:2 * P], rows[:, 1, :], s.ident).then_inc(cols_done, 1)
            pe.wait_ge(xn_ready, TM)
            pe.wait_ge(ones_set, 2)
            for g in range(4):
                pe.wait_ge(ada_used, 2 * STEPS * (g + 1))
                if g:
                    pe.wait_ge(q.mod_ready, g)
                for sct in range(2):
                    for k in range(4):
                        mm = nc.tensor.matmul(s.mb[2][:, sct * 4 + k:sct * 4 + k + 1],
                                              acc[:, g % 2, sct, k * P:(k + 1) * P], s.ones[:, 0:1], start=True, stop=True)
                mm.then_inc(mod_sums, 1)
                modulate_tensor(nc, pe, s, xn, g, q)
                pe.wait_ge(q.lo, 4 * g + 4)
                rows_unit(nc, pe, s, g // 2, g % 2, s.act_hi, s.act_lo, 4 * g, g == 0, g == 3, 0)

        @block.vector
        def _(dve):
            dve.wait_ge(c_exp, 1)
            nc.vector.tensor_scalar(s.c_col[:, 1, :], s.c_col[:, 0, :], 1.0, None, ALU.add).then_inc(c_ready, 1)
            dve.wait_ge(c_ready, 1)
            nc.vector.reciprocal(s.c_col[:, 2, :], s.c_col[:, 1, :]).then_inc(c_ready, 1)
            dve.wait_ge(c_ready, 2)
            nc.vector.tensor_tensor(s.c_col[:, 3, :], s.c_col[:, 2, :], s.cols2[:, 0:KT], ALU.mult).then_inc(c_ready, 1)
            nc.vector.tensor_copy(s.ident_bf[:, :], s.ident).then_inc(scaled, 1)
            nc.vector.tensor_copy(s.causal_bf[:, :], s.base[:, C_CAUSAL:C_CAUSAL + P]).then_inc(scaled, 1)
            nc.vector.tensor_scalar(s.fq_gain[:, :], s.cols2[:, 16:17], SCALE, None, ALU.mult).then_inc(scaled, 1)
            dve.wait_ge(c_ready, 3)

            def steps(g, ks):
                for k in ks:
                    dve.wait_ge(ada_in[k % SLOTS], 32 * (2 * g + k // SLOTS + 1))
                    for r in range(2):
                        part, c = acc[:, g % 2], s.c_col[:, 3, 2 * k + r:2 * k + r + 1]
                        if k + r == 0:
                            nc.vector.tensor_scalar(part, ada_raw[:, 0, 0], c, None, ALU.mult).then_inc(ada_used, 1)
                        else:
                            dve.wait_ge(ada_used, 2 * (STEPS * g + k) + r)
                            nc.vector.scalar_tensor_tensor(out=part, in0=ada_raw[:, k % SLOTS, r], scalar=c, in1=part,
                                                           op0=ALU.mult, op1=ALU.add).then_inc(ada_used, 1)

            steps(0, range(3))
            dve.wait_ge(sq_done, TM)
            nc.vector.tensor_scalar(ssq[:, 4:8], ssq[:, 0:4], 1.0 / D, EPS, ALU.mult, ALU.add).then_inc(ms_ready, 1)
            steps(0, range(3, 4))
            dve.wait_ge(rms_ready, 1)
            nc.vector.reciprocal(ssq[:, 12:16], ssq[:, 8:12]).then_inc(rstd_ready, 1)
            steps(0, range(4, STEPS))
            dve.wait_ge(gains_in, 48)
            nc.vector.tensor_scalar(s.gain_bc[:, 0, :], s.gain_bc[:, 0, :], SCALE, None, ALU.mult).then_inc(scaled, 1)
            for g in range(4):
                if g < 3:
                    steps(g + 1, range(2))
                dve.wait_ge(mod_sums, g + 1)
                c = slice(4 * g, 4 * g + 4)
                nc.vector.tensor_tensor(s.mod[:, 1, c], s.mb[2][:, 0:4], s.cols1[:, c], ALU.add).then_inc(mod_part, 1)
                nc.vector.tensor_tensor(s.mod[:, 4, c], s.mb[2][:, 4:8], s.cols1[:, KT + 4 * g:KT + 4 * g + 4],
                                        ALU.add).then_inc(mod_part, 1)
                dve.wait_ge(mod_part, 2 * g + 2)
                nc.vector.scalar_tensor_tensor(out=s.mod[:, 0, c], in0=s.mod[:, 4, c], scalar=1.0,
                                               in1=s.cols1[:, 96 + 4 * g:100 + 4 * g], op0=ALU.add,
                                               op1=ALU.mult).then_inc(q.mod_ready, 1)
                if g < 3:
                    steps(g + 1, range(2, 3))
                dve.wait_ge(q.mod_ready, g + 1)
                modulate_vector(nc, dve, s, g, q)
                if g < 3:
                    steps(g + 1, range(3, STEPS))
            dve.wait_ge(scaled, 4)


def windows(nc, dve, s, kv):
    xv = s.xb[:, 0:CMP_LEN * 64].rearrange("p (l g n) -> p l g n", g=NG, n=CW)
    for g in range(NG):
        src = s.kcvT[:, 2 * kv + g, :].rearrange("p (n b) -> p b n", b=CMP_STRIDE)
        for a in range(2):
            pe_l = s.cols2[:, 22 + 32 * kv + 16 * a:22 + 32 * kv + 16 * a + 16]
            nc.vector.tensor_tensor(xv[:, 16 * a:16 * a + 16, g, 0:NCMP], src[:, :, a:a + NCMP],
                                    pe_l.unsqueeze(2).broadcast_to([P, 16, NCMP]), ALU.add).then_inc(s.x_ready, 1)


def window_columns(piece):
    return slice(0, XW) if piece is None else slice(piece * 512, (piece + 1) * 512 if piece < 3 else XW)


def windows_hi(nc, act, s, kv, piece=None):
    c = window_columns(piece)
    act.wait_ge(s.x_ready, 4 * kv + 4)
    nc.scalar.activation(s.xb_hi[:, c], s.xb[:, c], ACT.Copy).then_inc(s.xh, 1)


def windows_lo(nc, dve, s, kv, piece=None):
    c = window_columns(piece)
    dve.wait_ge(s.xh, 1 if kv == 0 else piece + 2)
    nc.vector.tensor_tensor(s.xb_lo[:, c], s.xb[:, c], s.xb_hi[:, c].bitcast(F32), ALU.subtract).then_inc(s.xl, 1)



def phase_project(nc, A, s):
    with ExitStack() as ctx:
        sem = s.sem
        ada_raw = s.ada_raw
        acc, stage = s.ada_acc, s.stage
        sq = s.mb[2:4]
        st = s.proj_stats

        ada_in = [sem(f"ada2_in{i}") for i in range(2)]
        ada_used, acc_zero, bias_in = sem("ada2_used"), sem("acc2_zero"), sem("gate_bias_in")
        squared, summed = sem("proj_squared"), sem("proj_summed")
        ms, rms, rstd, normed = sem("proj_ms"), sem("proj_rms"), sem("proj_rstd"), sem("proj_normed")
        stored = s.proj_stored
        wz_hi, wz_lo, wzh, wzl = s.wz_hi, s.wz_lo, sem("wz_hi_ready"), sem("wz_lo_ready")
        kcv_in, zeroed = sem("kcv_in"), sem("xb_zeroed")
        sum_ready, sum_read, col_done = sem("section_sum"), sem("section_sum_read"), sem("section_columns")
        PER = 8
        ADA_BLOCKS = 4 * KT // PER
        NADA = 4 * KT
        SUMS_BLOCK = ADA_BLOCKS + 1
        SUMS_ORDER = (0, 3, 1, 2)
        ada = A.w_ada.rearrange("l (k p) n -> p (l k) n", p=P)

        block = ctx.enter_context(nc.Block())

        @block.sync
        def _(sp):
            for g, sct in enumerate((2, 5)):
                sp.dma_start(s.gate_bc[g][:, :], A.b_ada[0, sct * D:(sct + 1) * D].partition_broadcast(P)).then_inc(bias_in, 16)

            wz = s.wz[:, 0:KT * NZ].rearrange("p (k n) -> p k n", n=NZ)
            src = A.w_in.rearrange("l (k p) n -> p (l k) n", p=P)

            def loads(i, steps=False, first=False, last=None):
                for u in range(4):
                    for e in ((2 * u, 2 * u + 1) if steps else ()):
                        j = PER * (i - 1) + e
                        if e >= 2 or not first:
                            sp.wait_ge(ada_used, j - 1)
                        sp.dma_start(ada_raw[:, e % 2, :], ada[:, ds(j % KT, 1), ds((2 + j // KT) * D, D)].rearrange(
                            "p o n -> p (o n)")).then_inc(ada_in[e % 2], 16)
                    if u == 0:
                        load_unit(sp, s, 2 * i + 1, 1, w_in_unit(A, column(i), 3))
                    elif last is None:
                        load_unit(sp, s, 2 * i + 2 + (u - 1) // 2, (u - 1) % 2, w_in_unit(A, column(i + 1), u - 1))
                    else:
                        load_unit(sp, s, 2 * i + 2 + (u - 1) // 2, (u - 1) % 2, last(u - 1))

            def column(i):
                return i * 512 + (i // 6) * FOX

            loads(1, True, first=True)
            sp.dma_start(wz[:, :, 0:FOX], src[:, :, FZ:FZ + FOX]).then_inc(s.wz_in, 16)
            sp.dma_start(wz[:, :, FOX:32], src[:, :, GZ:GZ + 24]).then_inc(s.wz_in, 16)
            sp.dma_start(wz[:, :, 32:NZ], src[:, :, FZ:FZ + FOX]).then_inc(s.wz_in, 16)
            with sp.Fori(2, ADA_BLOCKS + 1) as i:
                loads(i, True)
            loads(NB_IN - 2)
            sp.wait_ge(col_done, 1)
            for m in range(TM):
                sp.wait_ge(stored[m], 16 * 9)
                sp.dma_start(s.kcv[:, m, :], s.proj[8, m]).then_inc(kcv_in, 16)
            loads(NB_IN - 1, last=lambda u: w_cmp_unit(A.cmp_w1_k, u))

        @block.scalar
        def _(act):
            def evacuate(i, first=False):
                for m in range(TM):
                    await_bank(act, s, i, m, 4 * i + 3)
                    if not first:
                        act.wait_ge(stored[m], 16 * i)
                    nc.scalar.activation(stage[:, m, :], s.gb[m][:, :], ACT.Copy).then_inc(s.bank_free, 1)
                    act.wait_ge(s.bank_free, 4 * (i) + m + 1)
                    if not first or m >= 2:
                        act.wait_ge(summed, 4 * i + m - 1)
                    nc.scalar.activation(sq[m % 2][:, :], stage[:, m, :], ACT.Square).then_inc(squared, 1)
                act.wait_ge(ms, i + 1)
                nc.scalar.activation(st[:, 2, :], st[:, 1, :], ACT.Sqrt).then_inc(rms, 1)

            def splits(i, units=range(1, 5)):
                for u in units:
                    split_hi(nc, act, s, 2 * i + u // 2, u % 2)

            evacuate(0, True)
            splits(1)
            evacuate(1)
            act.wait_ge(s.wz_in, 48)
            nc.scalar.activation(wz_hi[:, :], s.wz[:, 0:ZW], ACT.Copy).then_inc(wzh, 1)
            with act.Fori(2, NB_IN - 1) as i:
                splits(i)
                evacuate(i)
            splits(NB_IN - 1, (1, 2))
            act.wait_ge(col_done, 2)
            for e in range(4):
                act.wait_ge(s.keys_turned, e + 1)
                nc.scalar.activation(s.kcvT[:, e, :], s.mb[e % 2][:, :], ACT.Copy).then_inc(s.keys_read, 1)
            splits(NB_IN - 1, (3, 4))
            windows_hi(nc, act, s, 0)
            evacuate(NB_IN - 1)
            split_hi(nc, act, s, PAIR_CMP, 1)

        @block.tensor
        def _(pe):
            def units(i, us):
                for u in us:
                    rows_unit(nc, pe, s, 2 * i + u // 2, u % 2, s.act_hi, s.act_lo, 4 * u, u == 0, u == 3, i)

            with pe.Fori(1, SUMS_BLOCK) as i:
                units(i, range(4))
            units(SUMS_BLOCK, range(2))
            pe.wait_ge(ada_used, NADA)
            for e, sct in enumerate(SUMS_ORDER):
                for n in range(4):
                    if e or n >= 2:
                        pe.wait_ge(sum_read, 4 * e + n - 1)
                    nc.tensor.matmul(s.mb[n % 2][:, :], s.ones[:, :], acc[:, sct, n * 512:(n + 1) * 512],
                                     start=True, stop=True).then_inc(sum_ready, 1)
            units(SUMS_BLOCK, range(2, 4))
            units(SUMS_BLOCK + 1, range(2))
            pe.wait_ge(kcv_in, 64)
            pe.wait_ge(sum_read, 16)
            for e in range(4):
                if e >= 2:
                    pe.wait_ge(s.keys_read, e - 1)
                for m in range(TM):
                    mm = nc.tensor.transpose(s.mb[e % 2][:, m * P:(m + 1) * P], s.kcv[:, m, e * HD:(e + 1) * HD], s.ident)
                mm.then_inc(s.keys_turned, 1)
            units(SUMS_BLOCK + 1, range(2, 4))
            pe.wait_ge(wzl, 1)
            pe.wait_ge(s.keys_read, 3)
            for k in range(KT):
                c = slice(k * NZ, k * NZ + P)
                mm = three_products(nc, s.mb[0][:, :], wz_hi[:, c], wz_lo[:, c], s.act_hi[:, k, :], s.act_lo[:, k, :],
                                    k == 0, k == KT - 1)
            mm.then_inc(s.z_sums, 1)

        @block.vector
        def _(dve):
            def step(j, slot, uses, first):
                dve.wait_ge(ada_in[slot], 16 * uses)
                if not first:
                    dve.wait_ge(ada_used, j)
                sct = acc[:, ds(j // KT, 1), :].rearrange("p o n -> p (o n)")
                nc.vector.scalar_tensor_tensor(out=sct, in0=ada_raw[:, slot, :], scalar=s.c_col[:, 3, ds(j % KT, 1)],
                                               in1=sct, op0=ALU.mult, op1=ALU.add).then_inc(ada_used, 1)

            def work(i, steps, first=False, units=range(1, 5)):
                for u in units:
                    split_lo(nc, dve, s, 2 * i + u // 2, u % 2)
                    for e in ((2 * u - 2, 2 * u - 1) if steps else ()):
                        step(PER * (i - 1) + e, e % 2, (PER * (i - 1) + e) // 2 + 1, first and e == 0)

            def statistics(i):
                for m in range(TM):
                    dve.wait_ge(squared, 4 * i + m + 1)
                    nc.vector.tensor_reduce(st[:, 0, 4 * m:4 * m + 4],
                                            sq[m % 2][:, :].rearrange("p (h d) -> p h d", h=4),
                                            AX.X, ALU.add).then_inc(summed, 1)
                dve.wait_ge(summed, 4 * i + 4)
                nc.vector.tensor_scalar(st[:, 1, :], st[:, 0, :], 1.0 / HD, EPS, ALU.mult, ALU.add).then_inc(ms, 1)
                dve.wait_ge(rms, i + 1)
                nc.vector.reciprocal(st[:, 3, :], st[:, 2, :]).then_inc(rstd, 1)
                dve.wait_ge(rstd, 3 * i + 1)
                r = st[:, 3, :].rearrange("p (m h) -> p m h", m=TM)
                flag = s.base[:, ds(C_FLAG + 4 * i, 4)].unsqueeze(1).broadcast_to([P, TM, 4])
                nflag = s.base[:, ds(C_NFLAG + 4 * i, 4)].unsqueeze(1).broadcast_to([P, TM, 4])
                nc.vector.tensor_tensor(r, r, flag, ALU.mult).then_inc(rstd, 1)
                dve.wait_ge(rstd, 3 * i + 2)
                nc.vector.tensor_tensor(r, r, nflag, ALU.add).then_inc(rstd, 1)
                dve.wait_ge(rstd, 3 * i + 3)
                for m in range(TM):
                    v = stage[:, m, :].rearrange("p (h d) -> p h d", h=4)
                    nc.vector.tensor_tensor(v, v, st[:, 3, 4 * m:4 * m + 4].unsqueeze(2).broadcast_to([P, 4, HD]),
                                            ALU.mult).then_inc(normed, 1)

            statistics(0)
            dve.wait_ge(acc_zero, 1)
            work(1, True, True)
            statistics(1)
            dve.wait_ge(wzh, 1)
            nc.vector.tensor_tensor(wz_lo[:, :], s.wz[:, 0:ZW], wz_hi[:, :].bitcast(F32), ALU.subtract).then_inc(wzl, 1)
            with dve.Fori(2, ADA_BLOCKS + 1) as i:
                work(i, True)
                statistics(i)
            work(SUMS_BLOCK, False, units=(1, 2))
            dve.wait_ge(bias_in, 32)
            for e, sct in enumerate(SUMS_ORDER):
                for n in range(4):
                    dve.wait_ge(sum_ready, 4 * e + n + 1)
                    part = slice(n * 512, (n + 1) * 512)
                    if e < 2:
                        nc.vector.tensor_tensor(s.gate_bc[e][:, part], s.mb[n % 2][:, :], s.gate_bc[e][:, part],
                                                ALU.add).then_inc(sum_read, 1)
                    else:
                        nc.vector.tensor_tensor(ada_raw[:, e % 2, part].rearrange("p (k c) -> p k c", k=4),
                                                s.mb[n % 2][:, :].rearrange("p (k c) -> p k c", k=4),
                                                s.ident.unsqueeze(1).broadcast_to([P, 4, P]), ALU.mult).then_inc(sum_read, 1)
            work(SUMS_BLOCK, False, units=(3, 4))
            dve.wait_ge(sum_read, 16)
            for e in range(2):
                nc.vector.tensor_reduce(s.mod[:, 4 + e, :], ada_raw[:, e, :].rearrange("p (k c) -> p k c", k=KT), AX.X,
                                        ALU.add).then_inc(col_done, 1)
            statistics(SUMS_BLOCK)
            work(SUMS_BLOCK + 1, False, units=(1, 2))
            dve.wait_ge(zeroed, 1)
            dve.wait_ge(s.keys_read, 2)
            windows(nc, dve, s, 0)
            work(SUMS_BLOCK + 1, False, units=(3, 4))
            windows_lo(nc, dve, s, 0)
            dve.wait_ge(col_done, 2)
            nc.vector.tensor_tensor(s.mod[:, 3, :], s.mod[:, 4, :], s.cols1[:, 3 * KT:4 * KT], ALU.add).then_inc(col_done, 1)
            nc.vector.tensor_tensor(s.mod[:, 5, :], s.mod[:, 5, :], s.cols1[:, 4 * KT:5 * KT], ALU.add).then_inc(col_done, 1)
            dve.wait_ge(col_done, 4)
            nc.vector.scalar_tensor_tensor(out=s.mod[:, 2, :], in0=s.mod[:, 5, :], scalar=1.0,
                                           in1=s.cols1[:, 112:128], op0=ALU.add, op1=ALU.mult).then_inc(col_done, 1)
            statistics(SUMS_BLOCK + 1)
            split_lo(nc, dve, s, PAIR_CMP, 1)

        @block.gpsimd
        def _(pool):
            nc.gpsimd.memset(acc[:, :, :], 0.0).then_inc(acc_zero, 1)

            def store(i):
                for m in range(TM):
                    pool.wait_ge(normed, 4 * i + m + 1)
                    pool.dma_start(s.proj[ds(i, 1), m].rearrange("o p n -> (o p) n"), stage[:, m, :]).then_inc(stored[m], 16)
            with pool.Fori(0, NB_IN - 1) as i:
                store(i)
            pool.wait_ge(sum_ready, 16)
            nc.gpsimd.memset(s.xb[:, :], 0.0).then_inc(zeroed, 1)
            store(NB_IN - 1)
            for m in range(TM):
                pool.wait_ge(stored[m], 16 * NB_IN)



def phase_compress(nc, A, s):
    with ExitStack() as ctx:
        sb = lambda name, shape, dt=F32: ctx.enter_context(nc.sbuf_tensor(name, shape, dt))
        sem = s.sem
        zb = sb("z_bias", [NZ, 1])
        kcv, xb_hi, xb_lo = s.kcv, s.xb_hi, s.xb_lo
        z = sb("z", [NZ, 5, T])
        w2 = kcv[:, 2, :].rearrange("p (v c n) -> p v c n", v=2, c=2)
        free = s.stage[:, :, :].rearrange("p a b -> p (a b)")
        hid = free[0:64, 0:5 * CMP_HID].rearrange("p (a n) -> p a n", a=5)
        parts = free[0:NZ, 5 * CMP_HID:].bitcast(mybir.dt.bfloat16).rearrange("p (a t) -> p a t", a=3)
        hidT = kcv[:, 1, 0:P].rearrange("p (c n) -> p c n", c=2)
        kn = kcv[0:64, 0, 0:2 * HD].rearrange("p (e d) -> p e d", e=2)
        kst = sb("cmp_kst", [64, 4])

        zb_in, w2_in = sem("zb_in"), sem("w2_in")
        zeroed = sem("z_bias_zero")
        z_sums = s.z_sums
        zs, za, gtr, g_ready = sem("z_vector"), sem("z_scalar"), sem("gates_turned"), sem("gates_ready")
        xl = s.xl
        h_exp, h_vec, h_tr, h_trr = sem("hid_exp"), sem("hid_vec"), sem("hid_turned"), sem("hid_turned_read")
        k2, k2s, k2v, k2t, k2r = sem("cmp_out"), sem("cmp_out_sq"), sem("cmp_out_vec"), sem("cmp_out_turned"), sem("cmp_ready")

        block = ctx.enter_context(nc.Block())

        @block.sync
        def _(sp):
            sp.wait_ge(zeroed, 2)
            sp.dma_start(zb[0:FOX, :], A.b_forget.rearrange("l h -> h l")).then_inc(zb_in, 16)
            sp.dma_start(zb[32:NZ, :], A.b_forget.rearrange("l h -> h l")).then_inc(zb_in, 16)
            for kv, w in enumerate((A.cmp_w2_k, A.cmp_w2_v)):
                sp.dma_start(w2[:, kv], w.rearrange("l (k p) n -> p (l k) n", p=P)).then_inc(w2_in, 16)
            load_unit(sp, s, PAIR_CMP + 1, 1, w_cmp_unit(A.cmp_w1_k, 3))
            for u in range(4):
                load_unit(sp, s, PAIR_CMP + 2 + u // 2, u % 2, w_cmp_unit(A.cmp_w1_v, u))
            load_unit(sp, s, PAIR_OUT, 0, w_out_unit(A, 0, 0))
            sp.wait_ge(zs, 13)
            for part in range(3):
                sp.dma_start(s.decay[part * NZ:(part + 1) * NZ, :], parts[:, part, :]).then_inc(s.decay_in, 16)
            sp.wait_ge(s.decay_in, 48)

        @block.gpsimd
        def _(pool):
            nc.gpsimd.memset(zb[:, :], 0.0).then_inc(zeroed, 1)
            nc.gpsimd.memset(kst[:, :], 0.0).then_inc(zeroed, 1)

        @block.tensor
        def _(pe):
            def hidden_unit(kv, u):
                pair, slot = PAIR_CMP + 2 * kv + u // 2, u % 2
                pe.wait_ge(s.w_lo_ready, 2 * pair + slot + 1)
                if kv == 1:
                    pe.wait_ge(xl, min(u + 3, 5))
                wh = s.w_hi[:, slot].rearrange("p a (b n) -> p (a b) n", b=2)
                wl = s.w_lo[:, slot].rearrange("p a (b n) -> p (a b) n", b=2)
                for e in range(8):
                    l = 8 * u + e
                    c = slice(l * 64, l * 64 + P)
                    mm = three_products(nc, s.mb[2 + kv][:, 0:256], xb_hi[:, c], xb_lo[:, c],
                                        wh[:, e, :], wl[:, e, :], l == 0, l == CMP_LEN - 1)
                mm.then_inc(s.unit_used, 1)

            def turn_hidden(kv):
                pe.wait_ge(h_vec, 3 * kv + 3)
                for c in range(2):
                    mm = nc.tensor.transpose(s.mb[1][:, c * 64:(c + 1) * 64], hid[:, 3, c * P:(c + 1) * P], s.ident[0:64, 0:64])
                mm.then_inc(h_tr, 1)

            def second_layer(kv):
                pe.wait_ge(h_trr, kv + 1)
                pe.wait_ge(w2_in, 32)
                for c in range(2):
                    mm = nc.tensor.matmul(s.gb[kv][0:64, 0:HD], hidT[:, c, :], w2[:, kv, c, :], start=c == 0, stop=c == 1)
                mm.then_inc(k2, 1)

            pe.wait_ge(xl, 1)
            for u in range(4):
                hidden_unit(0, u)
            hidden_unit(1, 0)
            hidden_unit(1, 1)
            turn_hidden(0)
            hidden_unit(1, 2)
            second_layer(0)
            hidden_unit(1, 3)
            pe.wait_ge(k2v, 3)
            nc.tensor.transpose(s.gb[2][:, 0:64], kn[:, 1, :], s.ident[0:64, 0:64]).then_inc(k2t, 1)
            pe.wait_ge(zs, 5)
            for m in range(TM):
                mm = nc.tensor.transpose(s.mb[0][:, m * NZ:(m + 1) * NZ], z[:, 3, m * P:(m + 1) * P], s.ident[0:NZ, 0:NZ])
            mm.then_inc(gtr, 1)
            turn_hidden(1)
            second_layer(1)

        @block.scalar
        def _(act):
            def value_windows(piece):
                act.wait_ge(s.unit_used, 2 * PAIR_CMP + piece + 1)
                windows_hi(nc, act, s, 1, piece)

            for u in (2, 3):
                split_hi(nc, act, s, PAIR_CMP + 1, u % 2)
                value_windows(u - 2)
            act.wait_ge(zs, 1)
            nc.scalar.activation(z[:, 1, :], z[:, 0, :], ACT.Abs).then_inc(za, 1)
            act.wait_ge(za, 1)
            nc.scalar.activation(z[:, 2, :], z[:, 1, :], ACT.Exp, scale=-1.0).then_inc(za, 1)
            nc.scalar.activation(z[:, 3, :], z[:, 0, :], ACT.Exp, scale=-1.0).then_inc(za, 1)
            for u in (2, 3):
                split_hi(nc, act, s, PAIR_CMP + 2, u % 2)
                value_windows(u)

            def hidden(kv):
                act.wait_ge(s.unit_used, 2 * PAIR_CMP + 4 * kv + 4)
                nc.scalar.activation(hid[:, 0, :], s.mb[2 + kv][0:64, 0:256], ACT.Copy).then_inc(h_exp, 1)
                act.wait_ge(h_exp, 2 * kv + 1)
                nc.scalar.activation(hid[:, 1, :], hid[:, 0, :], ACT.Exp, scale=-1.0).then_inc(h_exp, 1)

            def read_hidden(kv):
                act.wait_ge(h_tr, kv + 1)
                nc.scalar.activation(hidT[:, :, :], s.mb[1][:, 0:P].rearrange("p (c n) -> p c n", c=2), ACT.Copy).then_inc(h_trr, 1)

            hidden(0)
            act.wait_ge(zs, 2)
            nc.scalar.activation(z[:, 1, :], z[:, 2, :], ACT.Ln).then_inc(za, 1)
            split_hi(nc, act, s, PAIR_CMP + 3, 0)
            read_hidden(0)
            split_hi(nc, act, s, PAIR_CMP + 3, 1)
            act.wait_ge(k2, 1)
            nc.scalar.activation(kn[:, 0, :], s.gb[0][0:64, 0:HD], ACT.Copy).then_inc(k2s, 1)
            act.wait_ge(k2s, 1)
            nc.scalar.activation(hid[:, 1, 0:HD], kn[:, 0, :], ACT.Square, accum_out=kst[:, 0:1]).then_inc(k2s, 1)
            act.wait_ge(k2v, 1)
            nc.scalar.activation(kst[:, 2:3], kst[:, 1:2], ACT.Sqrt).then_inc(k2s, 1)
            hidden(1)
            act.wait_ge(k2t, 1)
            nc.scalar.activation(s.kcT[:, :], s.gb[2][:, 0:64], ACT.Copy, scale=s.cols2[:, 19:20]).then_inc(k2r, 1)
            read_hidden(1)
            act.wait_ge(k2, 2)
            nc.scalar.activation(s.vc[:, :], s.gb[1][0:64, 0:HD], ACT.Copy).then_inc(k2r, 1)

        @block.vector
        def _(dve):
            windows(nc, dve, s, 1)
            dve.wait_ge(z_sums, 1)
            dve.wait_ge(zb_in, 32)
            nc.vector.tensor_scalar(z[:, 0, :], s.mb[0][0:NZ, :], zb[:, :], None, ALU.add).then_inc(zs, 1)
            for u in (2, 3):
                split_lo(nc, dve, s, PAIR_CMP + 1, u % 2)
                windows_lo(nc, dve, s, 1, u - 2)
            dve.wait_ge(za, 3)
            nc.vector.tensor_scalar(z[:, 2, :], z[:, 2, :], 1.0, None, ALU.add).then_inc(zs, 1)
            nc.vector.tensor_scalar(z[:, 3, :], z[:, 3, :], 1.0, None, ALU.add).then_inc(zs, 1)
            dve.wait_ge(zs, 3)
            nc.vector.tensor_scalar(z[:, 4, :], z[:, 0, :], 0.0, None, ALU.min).then_inc(zs, 1)
            for u in (2, 3):
                split_lo(nc, dve, s, PAIR_CMP + 2, u % 2)
                windows_lo(nc, dve, s, 1, u)

            def silu(kv):
                dve.wait_ge(h_exp, 2 * kv + 2)
                nc.vector.tensor_scalar(hid[:, 2, :], hid[:, 1, :], 1.0, None, ALU.add).then_inc(h_vec, 1)
                dve.wait_ge(h_vec, 3 * kv + 1)
                nc.vector.reciprocal(hid[:, 4, :], hid[:, 2, :]).then_inc(h_vec, 1)
                dve.wait_ge(h_vec, 3 * kv + 2)
                nc.vector.tensor_tensor(hid[:, 3, :], hid[:, 0, :], hid[:, 4, :], ALU.mult).then_inc(h_vec, 1)

            silu(0)
            split_lo(nc, dve, s, PAIR_CMP + 3, 0)
            split_lo(nc, dve, s, PAIR_CMP + 3, 1)
            nc.vector.reciprocal(z[:, 3, :], z[:, 3, :]).then_inc(zs, 1)
            dve.wait_ge(za, 4)
            dve.wait_ge(zs, 5)
            nc.vector.tensor_tensor(z[:, 4, :], z[:, 4, :], z[:, 1, :], ALU.subtract).then_inc(zs, 1)
            nc.vector.memset(z[:, 2, :], 1.0).then_inc(zs, 1)
            dve.wait_ge(k2s, 2)
            nc.vector.tensor_scalar(kst[:, 1:2], kst[:, 0:1], 1.0 / HD, EPS, ALU.mult, ALU.add).then_inc(k2v, 1)
            dve.wait_ge(zs, 7)
            nc.vector.tensor_tensor_scan(z[:, 0, :], z[:, 2, :], z[:, 4, :], 0.0, ALU.mult, ALU.add).then_inc(zs, 1)
            dve.wait_ge(k2s, 3)
            nc.vector.reciprocal(kst[:, 3:4], kst[:, 2:3]).then_inc(k2v, 1)
            dve.wait_ge(k2v, 2)
            nc.vector.tensor_scalar(kn[:, 1, :], kn[:, 0, :], kst[:, 3:4], None, ALU.mult).then_inc(k2v, 1)
            left = (z[:, 0, :], z[:, 1, :])
            for part in range(3):
                dve.wait_ge(zs, 8 + 2 * part)
                nc.vector.tensor_copy(parts[:, part, :], left[part % 2]).then_inc(zs, 1)
                if part < 2:
                    dve.wait_ge(zs, 9 + 2 * part)
                    nc.vector.tensor_tensor(left[1 - part % 2], left[part % 2], parts[:, part, :], ALU.subtract).then_inc(zs, 1)
            silu(1)
            dve.wait_ge(gtr, 1)
            nc.vector.tensor_copy(s.gates[:, :, :], s.mb[0][:, 0:TM * NZ].rearrange("p (m n) -> p m n", m=TM)).then_inc(g_ready, 1)



ORDER = (0, 3, 1, 2)


def early(I, count):
    return isinstance(I, int) and I < count


def item_scores(nc, pe, s, a, I, at, qT, kT, aux):
    n = ORDER[at]
    w = (n + 1) * P
    if not early(I, 2):
        pe.wait_ge(a.p_ready, I - 1)
    bank = s.gb[at % 2]
    nc.tensor.matmul(bank[:, n * P:w], s.ident_bf[:, :], s.causal_bf[:, :], start=True, stop=False, skip_group_check=True)
    if aux is not None:
        nc.tensor.matmul(bank[:, 0:w], aux[:, n * P:(n + 1) * P], s.auxR[:, 0:w], start=False, stop=False,
                         skip_group_check=True)
    nc.tensor.matmul(bank[:, 0:w], qT[:, n * P:(n + 1) * P], kT(w), start=False, stop=True,
                     skip_group_check=True).then_inc(a.s_done, 1)


def item_max(nc, dve, s, a, I, at):
    dve.wait_ge(a.s_done, I + 1)
    nc.vector.tensor_reduce(a.nmax[:, at:at + 1], s.gb[at % 2][:, 0:(ORDER[at] + 1) * P], AX.X, ALU.max,
                            negate=True).then_inc(a.max_ready, 1)


def item_exp(nc, act, s, a, I, at):
    w = (ORDER[at] + 1) * P
    act.wait_ge(a.max_ready, I + 1)
    if not early(I, 4):
        act.wait_ge(a.pt_done, I - 3)
    nc.scalar.activation(a.p[:, at, 0:w], s.gb[at % 2][:, 0:w], ACT.Exp,
                         bias=a.nmax[:, at:at + 1], accum_out=a.rsum[:, at:at + 1]).then_inc(a.p_ready, 1)


def item_reciprocal(nc, dve, s, a, I, at):
    dve.wait_ge(a.p_ready, I + 1)
    nc.vector.tensor_scalar(a.rinv[:, 0, at:at + 1], a.rsum[:, at:at + 1], 1e-30, None, ALU.max).then_inc(a.r_ready, 1)
    dve.wait_ge(a.r_ready, 2 * I + 1)
    nc.vector.reciprocal(a.rinv[:, 1, at:at + 1], a.rinv[:, 0, at:at + 1]).then_inc(a.r_ready, 1)


def item_normalise(nc, dve, s, a, I, at, gate):
    dve.wait_ge(a.r_ready, 2 * I + 2)
    part = a.p[:, at, 0:(ORDER[at] + 1) * P]
    if gate is None:
        nc.vector.tensor_scalar(part, part, a.rinv[:, 1, at:at + 1], None, ALU.mult).then_inc(a.pn_ready, 1)
    else:
        nc.vector.tensor_scalar(part, part, a.rinv[:, 1, at:at + 1], gate(ORDER[at]), ALU.mult, ALU.mult).then_inc(a.pn_ready, 1)


def item_turn(nc, pe, s, a, I, at):
    pe.wait_ge(a.pn_ready, I + 1)
    if not early(I, 2):
        pe.wait_ge(a.pt_ready, I - 1)
    for b in range(ORDER[at] + 1):
        mm = nc.tensor.transpose(s.gb[2 + at % 2][:, b * P:(b + 1) * P], a.p[:, at, b * P:(b + 1) * P], s.ident)
    mm.then_inc(a.pt_done, 1)


def item_copy(nc, act, s, a, I, at):
    w = (ORDER[at] + 1) * P
    act.wait_ge(a.pt_done, I + 1)
    if not early(I, 2):
        act.wait_ge(a.pv_done, I - 1)
    nc.scalar.activation(a.pT[:, at % 2, 0:w], s.gb[2 + at % 2][:, 0:w], ACT.Copy).then_inc(a.pt_ready, 1)


def item_values(nc, pe, s, a, I, at, v, bank, start):
    pe.wait_ge(a.pt_ready, I + 1)
    n = ORDER[at]
    for b in range(n + 1):
        mm = nc.tensor.matmul(bank[:, n * P:(n + 1) * P], v[:, b, :], a.pT[:, at % 2, b * P:(b + 1) * P],
                              start=start and b == 0, stop=b == n, skip_group_check=True)
    mm.then_inc(a.pv_done, 1)


def attention_state(nc, s, sb, sem, tag):
    a = Names()
    a.p = s.w_raw[:, 1]
    a.pT = sb(tag + "pT", [P, 2, T])
    a.nmax, a.rsum, a.rinv = sb(tag + "nmax", [P, TM]), sb(tag + "rsum", [P, TM]), sb(tag + "rinv", [P, 3, TM])
    a.s_done, a.max_ready, a.p_ready = sem(tag + "scores_done"), sem(tag + "max_ready"), sem(tag + "p_ready")
    a.r_ready, a.pn_ready = sem(tag + "r_ready"), sem(tag + "pn_ready")
    a.pt_done, a.pt_ready, a.pv_done = sem(tag + "pT_done"), sem(tag + "pT_ready"), sem(tag + "pv_done")
    a.o_hi, a.o_lo = sem(tag + "o_hi"), sem(tag + "o_lo")
    return a


def sparse_state(ctx, nc, s):
    sb = lambda name, shape, dt=F32: ctx.enter_context(nc.sbuf_tensor(name, shape, dt))
    sem = s.sem
    q = Names()
    q.tabs = sb("nsa_tabs", [P, N_END])
    q.cos = q.tabs[:, N_COS:N_COS + 512].rearrange("p (m d) -> p m d", m=TM)
    q.sin = q.tabs[:, N_SIN:N_SIN + 512].rearrange("p (m d) -> p m d", m=TM)
    q.raw, q.gained_x, q.roped_x = (sb("nsa_" + name, [P, 2, TM, HD]) for name in ("raw", "gained_x", "roped_x"))
    q.ra, q.rb = sb("rope_a", [P, TM, HD]), sb("rope_b", [P, TM, HD])
    q.kT = sb("nsa_kT", [P, 2 * NG, T])
    q.tabs_in, q.q_in, q.k_in = sem("nsa_tabs_in"), [sem(f"nsa_q_in{i}") for i in range(2)], sem("nsa_k_in")
    q.gained, q.roped, q.r_a, q.r_b = sem("nsa_gained"), sem("nsa_roped"), sem("rope_a_done"), sem("rope_b_done")
    return q


def rope(nc, pool, q, t, e):
    x = q.gained_x
    pool.wait_ge(q.gained, t + 1)
    nc.gpsimd.tensor_tensor(q.ra[:, :, :], x[:, e], q.cos, ALU.mult).then_inc(q.r_a, 1)
    nc.gpsimd.tensor_tensor(q.rb[:, :, 0:64], x[:, e, :, 64:HD], q.sin[:, :, 0:64], ALU.mult).then_inc(q.r_b, 1)
    nc.gpsimd.tensor_tensor(q.rb[:, :, 64:HD], x[:, e, :, 0:64], q.sin[:, :, 64:HD], ALU.mult).then_inc(q.r_b, 1)
    pool.wait_ge(q.r_a, t + 1)
    pool.wait_ge(q.r_b, 2 * t + 2)
    nc.gpsimd.tensor_tensor(q.roped_x[:, e], q.ra[:, :, :], q.rb[:, :, :], ALU.add).then_inc(q.roped, 1)


NK = 2 * NG


def phase_fox(nc, A, s):
    with ExitStack() as ctx:
        sb = lambda name, shape, dt=F32: ctx.enter_context(nc.sbuf_tensor(name, shape, dt))
        sem = s.sem
        raw = sb("fox_raw", [P, 2, 3, TM, HD])
        qkT = sb("fox_qkT", [P, 2, 2, T])
        aux = sb("fox_aux", [ND, 2, T], mybir.dt.bfloat16)
        a = attention_state(nc, s, sb, sem, "fox_")
        landed, v_landed = [sem(f"fox_qk_landed{i}") for i in range(2)], [sem(f"fox_v_landed{i}") for i in range(2)]
        turned, turned_read, aux_ready = sem("fox_qk_turned"), sem("fox_qk_read"), sem("fox_aux_ready")
        auxR_ready = sem("auxR_ready")
        q, key_turned, key_read = s.sparse, sem("nsa_key_turned"), s.key_read
        PAIRS = FOX // 2

        block = ctx.enter_context(nc.Block())

        @block.sync
        def _(sp):
            def load(x, j, e):
                src = s.proj[ds(2 * x + j // 2, 1), :, :, ds((j % 2) * 256 + e * HD, HD)]
                sp.dma_start(raw[:, e, x], src.rearrange("o m p d -> p (o m) d")).then_inc(
                    (v_landed if x == 2 else landed)[e], 16)

            def load_qk(j, e, first=False):
                if not first:
                    sp.wait_ge(turned, 2 * (2 * j + e) - 2)
                for x in range(2):
                    load(x, j, e)

            def load_v(j, e, first=False):
                if not first:
                    sp.wait_ge(a.pv_done, 4 * (2 * j + e) - 4)
                load(2, j, e)

            def load_key(j):
                sp.dma_start(q.raw[:, 1], s.proj[ds(9 + j // NG, 1), :, :, ds((j % NG) * HD, HD)].rearrange(
                    "o m p d -> p (o m) d")).then_inc(q.k_in, 16)

            def pair(j, first=False):
                load_qk(j, 0)
                load_v(j - 1, 1, first)
                sp.wait_ge(q.gained, j)
                load_key(j)
                load_qk(j, 1)
                load_v(j, 0)
            load_qk(0, 0, True)
            load_key(0)
            sp.dma_start(q.tabs[:, :], A.nsa_tabs).then_inc(q.tabs_in, 16)
            load_qk(0, 1, True)
            load_v(0, 0, True)
            sp.dma_start(q.raw[:, 0], s.proj[6, :, :, 0:HD].rearrange("m p d -> p m d")).then_inc(q.q_in[0], 16)
            pair(1, True)
            with sp.Fori(2, PAIRS) as j:
                pair(j)
            load_v(PAIRS - 1, 1)

        @block.gpsimd
        def _(pool):
            pool.wait_ge(q.tabs_in, 16)

            def gain(t, e, row):
                nc.gpsimd.tensor_tensor(q.gained_x[:, e], q.raw[:, e], s.gain_bc[:, ds(row, 1), :].broadcast_to([P, TM, HD]),
                                        ALU.mult).then_inc(q.gained, 1)

            pool.wait_ge(q.k_in, 16)
            gain(0, 1, 1)
            rope(nc, pool, q, 0, 1)
            with pool.Fori(1, NK) as t:
                pool.wait_ge(q.k_in, 16 * (t + 1))
                pool.wait_ge(q.roped, t)
                gain(t, 1, 1 + t // NG)
                pool.wait_ge(key_turned, t)
                rope(nc, pool, q, t, 1)
            pool.wait_ge(q.q_in[0], 16)
            pool.wait_ge(q.roped, NK)
            gain(NK, 0, 0)
            rope(nc, pool, q, NK, 0)

        def turn_qk(pe, j, e):
            h = 2 * j + e
            pe.wait_ge(landed[e], 32 * (j + 1))
            if not (isinstance(h, int) and h == 0):
                pe.wait_ge(turned_read, 2 * h)
            for x in range(2):
                for m in range(TM):
                    mm = nc.tensor.transpose(s.mb[2 + x][:, m * P:(m + 1) * P], raw[:, e, x, m, :], s.ident)
                mm.then_inc(turned, 1)

        @block.tensor
        def _(pe):
            def values(j, e, n, first):
                h = 2 * j + e
                if n == 0:
                    if not first:
                        pe.wait_ge(a.o_lo, h - 1)
                    pe.wait_ge(v_landed[e], 16 * (j + 1))
                item_values(nc, pe, s, a, 4 * h + n, n, raw[:, e, 2], s.mb[e], n == 0)

            def pair(j, first, last):
                for e in range(2):
                    h = 2 * j + e
                    start = first and e == 0
                    for n in range(TM):
                        I = 4 * h + n
                        if n == 0:
                            pe.wait_ge(turned_read, 2 * h + 2)
                            pe.wait_ge(aux_ready, h + 1)
                        item_scores(nc, pe, s, a, I, n, qkT[:, e, 0], lambda w: qkT[:, e, 1, 0:w], aux[:, e])
                        if n == 3 or not start:
                            item_turn(nc, pe, s, a, I - 3, (n + 1) % 4)
                        if not start:
                            values(j if e else j - 1, 1 - e, n, early(h, 3))
                        if n == 1 and not (last and e == 1):
                            if e == 1:
                                pe.wait_ge(key_read, j + 1)
                            turn_qk(pe, j + e, 1 - e)
                        if n == 3 and e == 0:
                            pe.wait_ge(turned_read, 2 * h + 3)
                            pe.wait_ge(q.roped, j + 1)
                            for m in range(TM):
                                mm = nc.tensor.transpose(s.mb[2][:, m * P:(m + 1) * P], q.roped_x[:, 1, m, :], s.ident)
                            mm.then_inc(key_turned, 1)
            turn_qk(pe, 0, 0)
            pe.wait_ge(auxR_ready, 1)
            pair(0, True, False)
            pair(1, False, False)
            with pe.Fori(2, PAIRS - 1) as j:
                pair(j, False, False)
            pair(PAIRS - 1, False, True)
            END = 4 * FOX
            for n in range(TM):
                if n < 3:
                    item_turn(nc, pe, s, a, END - 3 + n, n + 1)
                values(PAIRS - 1, 1, n, False)

        @block.scalar
        def _(act):
            def read_qk(x, h, e):
                act.wait_ge(turned, 2 * h + x + 1)
                if not isinstance(h, int) or h >= 2:
                    act.wait_ge(a.s_done, 4 * h - 4)
                nc.scalar.activation(qkT[:, e, x], s.mb[2 + x][:, :], ACT.Copy,
                                     scale=s.fq_gain[:, :] if x == 0 else s.cols2[:, 17:18]).then_inc(turned_read, 1)

            def o_hi(h, e):
                act.wait_ge(a.pv_done, 4 * h + 4)
                nc.scalar.activation(s.act_hi[:, ds(h, 1), :].rearrange("p o t -> p (o t)"), s.mb[e][:, :],
                                     ACT.Copy).then_inc(a.o_hi, 1)

            def pair(j, first, last):
                for e in range(2):
                    h = 2 * j + e
                    start = first and e == 0
                    for n in range(TM):
                        item_exp(nc, act, s, a, 4 * h + n, n)
                        if n == 3 or not start:
                            item_copy(nc, act, s, a, 4 * h + n - 3, (n + 1) % 4)
                        if n == 1 and not (last and e == 1):
                            for x in range(2):
                                read_qk(x, h + 1, 1 - e)
                        if n == 0 and not first:
                            o_hi(h - 2, e)
                        if n == 0 and e == 1:
                            act.wait_ge(key_turned, j + 1)
                            nc.scalar.activation(tile(q.kT, j), s.mb[2][:, :], ACT.Copy).then_inc(key_read, 1)
            split_hi(nc, act, s, PAIR_OUT, 0)
            for x in range(2):
                read_qk(x, 0, 0)
            pair(0, True, False)
            with act.Fori(1, PAIRS - 1) as j:
                pair(j, False, False)
            pair(PAIRS - 1, False, True)
            for n in (1, 2, 3):
                item_copy(nc, act, s, a, 4 * FOX - 4 + n, n)
            for e in range(2):
                o_hi(FOX - 2 + e, e)

        @block.vector
        def _(dve):
            def make_aux(h, e):
                if not isinstance(h, int) or h >= 2:
                    dve.wait_ge(a.s_done, 4 * h - 4)
                nc.vector.tensor_scalar(aux[:, e, :], s.decay[:, :], s.base[0:ND, ds(C_M1 + h, 1)],
                                        s.base[0:ND, ds(C_M2 + h, 1)], ALU.mult, ALU.add).then_inc(aux_ready, 1)

            def o_lo(h, e):
                dve.wait_ge(a.o_hi, h + 1)
                nc.vector.tensor_tensor(s.act_lo[:, ds(h, 1), :].rearrange("p o t -> p (o t)"), s.mb[e][:, :],
                                        s.act_hi[:, ds(h, 1), :].rearrange("p o t -> p (o t)").bitcast(F32),
                                        ALU.subtract).then_inc(a.o_lo, 1)

            def pair(j, first, last):
                for e in range(2):
                    h = 2 * j + e
                    start = first and e == 0
                    for n in range(TM):
                        I = 4 * h + n
                        item_max(nc, dve, s, a, I, n)
                        if n >= 1 or not start:
                            item_reciprocal(nc, dve, s, a, I - 1, (n - 1) % 4)
                            item_normalise(nc, dve, s, a, I - 1, (n - 1) % 4, None)
                        if n == 1 and not first:
                            o_lo(h - 2, e)
                        if n == 2:
                            if not (last and e == 1):
                                make_aux(h + 1, 1 - e)
            dve.wait_ge(s.decay_in, 48)
            nc.vector.tensor_scalar(s.auxR[:, :], s.decay[:, :], s.base[0:ND, C_N1:C_N1 + 1], s.base[0:ND, C_N2:C_N2 + 1],
                                    ALU.mult, ALU.add).then_inc(auxR_ready, 1)
            make_aux(0, 0)
            split_lo(nc, dve, s, PAIR_OUT, 0)
            pair(0, True, False)
            with dve.Fori(1, PAIRS - 1) as j:
                pair(j, False, False)
            pair(PAIRS - 1, False, True)
            item_reciprocal(nc, dve, s, a, 4 * FOX - 1, 3)
            item_normalise(nc, dve, s, a, 4 * FOX - 1, 3, None)
            for e in range(2):
                o_lo(FOX - 2 + e, e)


def phase_nsa(nc, A, s):
    with ExitStack() as ctx:
        sb = lambda name, shape, dt=F32: ctx.enter_context(nc.sbuf_tensor(name, shape, dt))
        sem = s.sem
        q = s.sparse
        tabs, nq, qn, qr = q.tabs, q.raw, q.gained_x, q.roped_x
        kT = q.kT[:, :, :].rearrange("p (b g) t -> p b g t", g=NG)
        vv = sb("nsa_v", [P, 2, 2, TM, HD])
        qT = sb("nsa_qT", [P, 2, T])
        qrT = sb("nsa_qrT", [P, 2, T])
        pcw = sb("cmp_p", [P, 2, (TM + 1) * 64])
        pc = pcw[:, :, 0:TM * 64].rearrange("p e (m n) -> p e m n", m=TM)
        cst = sb("cmp_stats", [P, 4, TM])
        pcT = sb("cmp_pT", [64, 2, T])
        a = attention_state(nc, s, sb, sem, "nsa_")

        gained, roped, q_in = q.gained, q.roped, q.q_in
        v_in = [sem(f"nsa_v_in{i}") for i in range(2)]
        turned, turned_read = sem("nsa_turned"), sem("nsa_turned_read")
        c_s, c_v, c_e, c_t, c_tr, c_pv = (sem("cmp_scores"), sem("cmp_vec"), sem("cmp_exp"), sem("cmp_turned"),
                                          sem("cmp_turned_read"), sem("cmp_pv"))
        pad_zero = sem("cmp_pad_zero")
        PAIRS = NSA // 2
        C_V = 6
        c_m, c_r = sem("cmp_max"), sem("cmp_r")

        block = ctx.enter_context(nc.Block())

        @block.sync
        def _(sp):
            def load_head(j, e, first=False):
                h = 2 * j + e
                if not first:
                    sp.wait_ge(gained, NK + h - 1)
                if not (first and e == 0):
                    sp.dma_start(nq[:, e], s.proj[ds(6 + j // 2, 1), :, :, ds((j % 2) * 256 + e * HD, HD)].rearrange(
                        "o m p d -> p (o m) d")).then_inc(q_in[e], 16)
                if not first:
                    sp.wait_ge(a.pv_done, 8 * h - 8)
                for br in range(2):
                    sp.dma_start(vv[:, e, br], s.proj[9 + br, :, :, ds((j // 2) * HD + 256, HD)].rearrange(
                        "m p d -> p m d")).then_inc(v_in[e], 16)
            for e in range(2):
                load_head(0, e, True)
            with sp.Fori(1, PAIRS) as j:
                for e in range(2):
                    load_head(j, e)

        def table(at, j):
            return tabs[:, ds(at + 256 * (j // 2), 256)].rearrange("p (m n) -> p m n", m=TM)

        @block.gpsimd
        def _(pool):
            nc.gpsimd.memset(pcw[:, :, TM * 64:], 0.0).then_inc(pad_zero, 1)

            def prepare(h, e, uses):
                pool.wait_ge(q_in[e], 16 * uses)
                if not isinstance(h, int) or h >= 2:
                    pool.wait_ge(turned, 2 * h - 2)
                pool.wait_ge(roped, NK + h)
                nc.gpsimd.tensor_tensor(qn[:, e], nq[:, e], s.gain_bc[:, 0:1, :].broadcast_to([P, TM, HD]),
                                        ALU.mult).then_inc(gained, 1)
                rope(nc, pool, q, NK + h, e)

            def cmp_softmax(h, e):
                pool.wait_ge(c_m, h + 1)
                nc.gpsimd.tensor_tensor(pc[:, e], pc[:, e], cst[:, 0, :].unsqueeze(2).broadcast_to([P, TM, 64]),
                                        ALU.subtract).then_inc(c_v, 1)
                pool.wait_ge(c_v, C_V * h + 5)
                nc.gpsimd.tensor_tensor(pc[:, e], pc[:, e], cst[:, 3, :].unsqueeze(2).broadcast_to([P, TM, 64]),
                                        ALU.mult).then_inc(c_v, 1)
            cmp_softmax(0, 0)
            prepare(1, 1, 1)
            cmp_softmax(1, 1)
            with pool.Fori(1, PAIRS) as j:
                for e in range(2):
                    prepare(2 * j + e, e, j + 1)
                    cmp_softmax(2 * j + e, e)

        def turn_plain(pe, h, e):
            pe.wait_ge(gained, NK + h + 1)
            if not isinstance(h, int) or h >= 1:
                pe.wait_ge(c_v, C_V * (h - 1) + 1)
            for m in range(TM):
                mm = nc.tensor.transpose(s.mb[2][:, m * P:(m + 1) * P], qn[:, e, m, :], s.ident)
            mm.then_inc(turned, 1)

        def turn_roped(pe, h, e):
            pe.wait_ge(roped, NK + h + 1)
            if not isinstance(h, int) or h >= 1:
                pe.wait_ge(c_tr, h)
            for m in range(TM):
                mm = nc.tensor.transpose(s.mb[3][:, m * P:(m + 1) * P], qr[:, e, m, :], s.ident)
            mm.then_inc(turned, 1)

        @block.tensor
        def _(pe):
            def cmp_scores(h, e):
                pe.wait_ge(turned_read, 2 * h + 1)
                for m in range(TM):
                    mm = nc.tensor.matmul(s.mb[2][:, m * 64:(m + 1) * 64], qT[:, e, m * P:(m + 1) * P], s.kcT[:, :],
                                          start=True, stop=True)
                mm.then_inc(c_s, 1)

            def cmp_turn(h, e):
                pe.wait_ge(c_v, C_V * h + 6)
                pe.wait_ge(turned_read, 2 * h + 2)
                for m in range(TM):
                    mm = nc.tensor.transpose(s.mb[3][:, m * P:(m + 1) * P], pcw[:, e, m * 64:m * 64 + P], s.ident)
                mm.then_inc(c_t, 1)

            def cmp_values(h, e, first):
                pe.wait_ge(c_tr, h + 1)
                if not first:
                    pe.wait_ge(a.o_lo, h - 1)
                nc.tensor.matmul(s.mb[e][:, :], s.vc[:, :], pcT[:, e, :], start=True, stop=False,
                                 skip_group_check=True).then_inc(c_pv, 1)

            def pair(j, first, last):
                for e in range(2):
                    h = 2 * j + e
                    start = first and e == 0
                    more = not (last and e == 1)
                    for i in range(8):
                        br, n = i // 4, i % 4
                        I = 8 * h + i
                        if i == 0:
                            pe.wait_ge(turned_read, 2 * h + 2)
                        item_scores(nc, pe, s, a, I, n, qrT[:, e], lambda w: kT[:, br, ds(j // 2, 1), 0:w].rearrange(
                            "p o t -> p (o t)"), None)
                        if i >= 3 or not start:
                            item_turn(nc, pe, s, a, I - 3, (n + 1) % 4)
                        if i == 0 and not start:
                            cmp_turn(h, e)
                        if i == 3:
                            cmp_values(h, e, first)
                        if i >= 4:
                            if i == 4:
                                pe.wait_ge(v_in[e], 32 * (j + 1))
                            item_values(nc, pe, s, a, I - 4, n, vv[:, e, 0], s.mb[e], False)
                        elif not start:
                            item_values(nc, pe, s, a, I - 4, n, vv[:, 1 - e, 1], s.mb[1 - e], False)
                        if more:
                            if i == 1:
                                turn_plain(pe, h + 1, 1 - e)
                            if i == 3:
                                cmp_scores(h + 1, 1 - e)
                            if i == 5:
                                turn_roped(pe, h + 1, 1 - e)
            pe.wait_ge(pad_zero, 1)
            turn_plain(pe, 0, 0)
            turn_roped(pe, 0, 0)
            cmp_scores(0, 0)
            cmp_turn(0, 0)
            pair(0, True, False)
            with pe.Fori(1, PAIRS - 1) as j:
                pair(j, False, False)
            pair(PAIRS - 1, False, True)
            END = 8 * NSA
            for n in range(TM):
                if n < 3:
                    item_turn(nc, pe, s, a, END - 3 + n, n + 1)
                item_values(nc, pe, s, a, END - 4 + n, n, vv[:, 1, 1], s.mb[1], False)

        @block.scalar
        def _(act):
            def read_plain(h, e):
                act.wait_ge(turned, 2 * h + 1)
                nc.scalar.activation(qT[:, e], s.mb[2][:, :], ACT.Copy).then_inc(turned_read, 1)

            def read_roped(h, e):
                act.wait_ge(turned, 2 * h + 2)
                nc.scalar.activation(qrT[:, e], s.mb[3][:, :], ACT.Copy).then_inc(turned_read, 1)

            def cmp_exp(h, e):
                act.wait_ge(c_v, C_V * h + 2)
                nc.scalar.activation(pc[:, e], pc[:, e], ACT.Exp).then_inc(c_e, 1)

            def cmp_read(h, e, first):
                act.wait_ge(c_t, h + 1)
                if not first:
                    act.wait_ge(c_pv, h - 1)
                nc.scalar.activation(pcT[:, e, :], s.mb[3][0:64, :], ACT.Copy).then_inc(c_tr, 1)

            def o_hi(h, e):
                act.wait_ge(a.pv_done, 8 * h + 8)
                nc.scalar.activation(s.act_hi[:, ds(FOX + h, 1), :].rearrange("p o t -> p (o t)"), s.mb[e][:, :],
                                     ACT.Copy).then_inc(a.o_hi, 1)

            def pair(j, first, last):
                for e in range(2):
                    h = 2 * j + e
                    start = first and e == 0
                    more = not (last and e == 1)
                    for i in range(8):
                        item_exp(nc, act, s, a, 8 * h + i, i % 4)
                        if i >= 3 or not start:
                            item_copy(nc, act, s, a, 8 * h + i - 3, (i + 1) % 4)
                        if i == 4 and not start:
                            o_hi(h - 1, 1 - e)
                        if i == 0 and not start:
                            cmp_read(h, e, first)
                        if more:
                            if i == 1:
                                read_plain(h + 1, 1 - e)
                            if i == 4:
                                cmp_exp(h + 1, 1 - e)
                            if i == 5:
                                read_roped(h + 1, 1 - e)
            read_plain(0, 0)
            read_roped(0, 0)
            cmp_exp(0, 0)
            cmp_read(0, 0, True)
            pair(0, True, False)
            with act.Fori(1, PAIRS - 1) as j:
                pair(j, False, False)
            pair(PAIRS - 1, False, True)
            for n in (1, 2, 3):
                item_copy(nc, act, s, a, 8 * NSA - 4 + n, n)
            o_hi(NSA - 1, 1)

        @block.vector
        def _(dve):
            def cmp_masked(h, e, j):
                dve.wait_ge(c_s, h + 1)
                nc.vector.tensor_tensor(pc[:, e], s.mb[2][:, 0:256].rearrange("p (m n) -> p m n", m=TM),
                                        table(N_NEG, j), ALU.add).then_inc(c_v, 1)
                dve.wait_ge(c_v, C_V * h + 1)
                nc.vector.tensor_reduce(cst[:, 0, :], pc[:, e], AX.X, ALU.max).then_inc(c_m, 1)

            def cmp_sum(h, e, j):
                dve.wait_ge(c_e, h + 1)
                nc.vector.tensor_tensor(pc[:, e], pc[:, e], table(N_MASK, j), ALU.mult).then_inc(c_v, 1)
                dve.wait_ge(c_v, C_V * h + 3)
                nc.vector.tensor_reduce(cst[:, 1, :], pc[:, e], AX.X, ALU.add).then_inc(c_v, 1)

            def cmp_factor(h):
                dve.wait_ge(c_v, C_V * h + 4)
                nc.vector.tensor_scalar(cst[:, 1, :], cst[:, 1, :], 1e-30, None, ALU.max).then_inc(c_r, 1)
                dve.wait_ge(c_r, 2 * h + 1)
                nc.vector.reciprocal(cst[:, 2, :], cst[:, 1, :]).then_inc(c_r, 1)
                dve.wait_ge(c_r, 2 * h + 2)
                nc.vector.tensor_tensor(cst[:, 3, :], cst[:, 2, :], s.gates[:, :, ds(FOX + 3 * h, 1)].rearrange(
                    "p m o -> p (m o)"), ALU.mult).then_inc(c_v, 1)

            def o_lo(h, e):
                dve.wait_ge(a.o_hi, h + 1)
                nc.vector.tensor_tensor(s.act_lo[:, ds(FOX + h, 1), :].rearrange("p o t -> p (o t)"), s.mb[e][:, :],
                                        s.act_hi[:, ds(FOX + h, 1), :].rearrange("p o t -> p (o t)").bitcast(F32),
                                        ALU.subtract).then_inc(a.o_lo, 1)

            def gate(h, br):
                return lambda n: s.gates[:, n, ds(FOX + 3 * h + 1 + br, 1)]

            def pair(j, first, last):
                for e in range(2):
                    h = 2 * j + e
                    start = first and e == 0
                    more = not (last and e == 1)
                    for i in range(8):
                        br, n = i // 4, i % 4
                        I = 8 * h + i
                        item_max(nc, dve, s, a, I, n)
                        if i >= 1 or not start:
                            item_reciprocal(nc, dve, s, a, I - 1, (n - 1) % 4)
                            item_normalise(nc, dve, s, a, I - 1, (n - 1) % 4,
                                           gate(h, (i - 1) // 4) if i else gate(h - 1, 1))
                        if i == 5 and not start:
                            o_lo(h - 1, 1 - e)
                        if more:
                            if i == 3:
                                cmp_masked(h + 1, 1 - e, j + e)
                            if i == 5:
                                cmp_sum(h + 1, 1 - e, j + e)
                            if i == 6:
                                cmp_factor(h + 1)
            cmp_masked(0, 0, 0)
            cmp_sum(0, 0, 0)
            cmp_factor(0)
            pair(0, True, False)
            with dve.Fori(1, PAIRS - 1) as j:
                pair(j, False, False)
            pair(PAIRS - 1, False, True)
            item_reciprocal(nc, dve, s, a, 8 * NSA - 1, 3)
            item_normalise(nc, dve, s, a, 8 * NSA - 1, 3, gate(NSA - 1, 1))
            o_lo(NSA - 1, 1)



def phase_out(nc, A, s):
    with ExitStack() as ctx:
        gated = s.gated
        sem = s.sem
        square = ctx.enter_context(nc.sbuf_tensor("out_square", [P, 512], F32))
        x_in, added, squared = sem("x2_in"), sem("out_added"), sem("out_squared")

        block = ctx.enter_context(nc.Block())

        @block.sync
        def _(sp):
            for u in (1, 2):
                load_unit(sp, s, PAIR_OUT + u // 2, u % 2, w_out_unit(A, 0, u))
            for m in range(TM):
                sp.dma_start(s.x2[:, m, :], A.x[0, m * P:(m + 1) * P, :]).then_inc(x_in, 16)

            def loads(n, following):
                load_unit(sp, s, PAIR_OUT + 2 * n + 1, 1, w_out_unit(A, n, 3))
                for u in range(3):
                    load_unit(sp, s, PAIR_OUT + 2 * n + 2 + u // 2, u % 2, following(u))
            with sp.Fori(0, 3) as n:
                loads(n, lambda u: w_out_unit(A, n + 1, u))
            loads(3, lambda u: w_up_unit(A, 0, u))

        @block.tensor
        def _(pe):
            with pe.Fori(0, 4) as n:
                for u in range(4):
                    rows_unit(nc, pe, s, PAIR_OUT + 2 * n + u // 2, u % 2, s.act_hi, s.act_lo, 4 * u, u == 0, u == 3,
                              ROUND_OUT + n)

        @block.scalar
        def _(act):
            def body(n, first):
                for u in range(1, 5):
                    split_hi(nc, act, s, PAIR_OUT + 2 * n + u // 2, u % 2)
                for m in range(TM):
                    act.wait_ge(added, 4 * n + m + 1)
                    if not first or m:
                        act.wait_ge(squared, 4 * n + m)
                    nc.scalar.activation(square[:, :], s.x2[:, m, ds(n * 512, 512)], ACT.Square,
                                         accum_out=s.ssq2[:, m, ds(n, 1)]).then_inc(squared, 1)
            body(0, True)
            with act.Fori(1, 4) as n:
                body(n, False)

        @block.vector
        def _(dve):
            def body(n, first):
                for u in range(1, 5):
                    split_lo(nc, dve, s, PAIR_OUT + 2 * n + u // 2, u % 2)
                for m in range(TM):
                    await_bank(dve, s, ROUND_OUT + n, m, 2 * PAIR_OUT + 4 * n + 3)
                    if not first or m >= 2:
                        dve.wait_ge(added, 4 * n + m - 1)
                    nc.vector.tensor_tensor(gated[:, m % 2, :], s.gb[m][:, :], s.gate_bc[0][:, ds(n * 512, 512)],
                                            ALU.mult).then_inc(s.bank_free, 1)
            body(0, True)
            with dve.Fori(1, 4) as n:
                body(n, False)

        @block.gpsimd
        def _(pool):
            pool.wait_ge(x_in, 64)
            with pool.Fori(0, 4) as n:
                for m in range(TM):
                    pool.wait_ge(s.bank_free, 4 * (ROUND_OUT + n) + m + 1)
                    part = s.x2[:, m, ds(n * 512, 512)]
                    nc.gpsimd.tensor_tensor(part, part, gated[:, m % 2, :], ALU.add).then_inc(added, 1)



def phase_norm2(nc, A, s):
    with ExitStack() as ctx:
        sb = lambda name, shape, dt=F32: ctx.enter_context(nc.sbuf_tensor(name, shape, dt))
        sem = s.sem
        xn = sb("xn2", [P, TM, D])
        st = sb("stats2", [P, 4, TM])
        ms_ready, rms_ready, rstd_ready = sem("ms2"), sem("rms2"), sem("rstd2")
        xn_vector, xn_scalar = sem("xn2_vector"), sem("xn2_scalar")
        tmp = s.gate_bc[0][:, :].rearrange("p (e t) -> p e t", e=4)
        q = modulate_state(sem, "h2_", s.mb, tmp, s.mod[:, 2, :], s.mod[:, 3, :])

        block = ctx.enter_context(nc.Block())

        @block.sync
        def _(sp):
            load_unit(sp, s, PAIR_FF + 1, 1, w_up_unit(A, 0, 3))
            for u in range(3):
                load_unit(sp, s, PAIR_FF + 2 + u // 2, u % 2, w_up_unit(A, 1, u))

        @block.scalar
        def _(act):
            act.wait_ge(ms_ready, 2)
            nc.scalar.activation(st[:, 2, :], st[:, 1, :], ACT.Sqrt).then_inc(rms_ready, 1)
            act.wait_ge(rstd_ready, 1)

            def normalise(g):
                for m in (2, 3):
                    nc.scalar.activation(xn[:, m, g * 512:(g + 1) * 512], s.x2[:, m, g * 512:(g + 1) * 512], ACT.Copy,
                                         scale=st[:, 3, m:m + 1]).then_inc(xn_scalar, 1)
            normalise(0)
            for g in range(4):
                if g < 3:
                    normalise(g + 1)
                modulate_scalar(nc, act, s, g, q)
                split_hi(nc, act, s, PAIR_FF + (g + 1) // 2, (g + 1) % 2)

        @block.tensor
        def _(pe):
            def turn(g):
                pe.wait_ge(xn_vector, 2 * g + 2)
                pe.wait_ge(xn_scalar, 2 * g + 2)
                modulate_tensor(nc, pe, s, xn, g, q)
            turn(0)
            for g in range(4):
                if g < 3:
                    turn(g + 1)
                pe.wait_ge(q.lo, 4 * g + 4)
                cols_unit(nc, pe, s, PAIR_FF + g // 2, g % 2, 4 * g, g == 0, g == 3, ROUND_FF)

        @block.vector
        def _(dve):
            nc.vector.tensor_reduce(st[:, 0, :], s.ssq2[:, :, :], AX.X, ALU.add).then_inc(ms_ready, 1)
            dve.wait_ge(ms_ready, 1)
            nc.vector.tensor_scalar(st[:, 1, :], st[:, 0, :], 1.0 / D, EPS, ALU.mult, ALU.add).then_inc(ms_ready, 1)
            dve.wait_ge(rms_ready, 1)
            nc.vector.reciprocal(st[:, 3, :], st[:, 2, :]).then_inc(rstd_ready, 1)
            dve.wait_ge(rstd_ready, 1)

            def normalise(g):
                for m in (0, 1):
                    nc.vector.tensor_scalar(xn[:, m, g * 512:(g + 1) * 512], s.x2[:, m, g * 512:(g + 1) * 512],
                                            st[:, 3, m:m + 1], None, ALU.mult).then_inc(xn_vector, 1)
            normalise(0)
            for g in range(4):
                if g < 3:
                    normalise(g + 1)
                modulate_vector(nc, dve, s, g, q)
                split_lo(nc, dve, s, PAIR_FF + (g + 1) // 2, (g + 1) % 2)



def phase_mlp(nc, A, s):
    with ExitStack() as ctx:
        sb = lambda name, shape, dt=F32: ctx.enter_context(nc.sbuf_tensor(name, shape, dt))
        sem = s.sem
        u_hi, u_lo = sb("u_hi", [P, 8, T], F32R), sb("u_lo", [P, 8, T], F32R)
        spare = s.gate_bc[0][:, :].rearrange("p (a e t) -> p a e t", a=2, e=2)
        relu, squ = spare[:, 0], spare[:, 1]
        gated = s.gated
        sq_n, hi_n, lo_n, added = sem("relu_sq_n"), sem("u_hi_n"), sem("u_lo_n"), sem("mlp_added")
        out_stored = sem("out_stored")

        block = ctx.enter_context(nc.Block())

        @block.sync
        def _(sp):
            def down_loads(c, n):
                for u in range(2):
                    load_unit(sp, s, PAIR_FF + 8 * c + 4 + n, u, w_down_unit(A, c, n, u))

            def up_loads(c, b, units):
                for u in units:
                    load_unit(sp, s, PAIR_FF + 8 * c + 2 * b + u // 2, u % 2, w_up_unit(A, 2 * c + b, u))
            up_loads(0, 1, (3,))
            with sp.Fori(0, CHUNKS - 1) as c:
                with sp.Fori(0, 4) as n:
                    down_loads(c, n)
                with sp.Fori(0, 2) as b:
                    up_loads(c + 1, b, range(4))
            with sp.Fori(0, 4) as n:
                down_loads(CHUNKS - 1, n)
            with sp.Fori(0, 4) as n:
                for m in range(TM):
                    sp.wait_ge(added, 16 * (CHUNKS - 1) + 4 * n + m + 1)
                    sp.dma_start(A.out[0, m * P:(m + 1) * P, ds(n * 512, 512)], s.x2[:, m, ds(n * 512, 512)]).then_inc(
                        out_stored, 16)
            sp.wait_ge(out_stored, 256)

        @block.tensor
        def _(pe):
            def up(c, b):
                for u in range(4):
                    cols_unit(nc, pe, s, PAIR_FF + 8 * c + 2 * b + u // 2, u % 2, 4 * u, u == 0, u == 3,
                              ROUND_FF + 6 * c + b)

            def down(c):
                with pe.Fori(0, 4) as n:
                    for u in range(2):
                        pe.wait_ge(lo_n, 8 * c + 4 * u + 4)
                        rows_unit(nc, pe, s, PAIR_FF + 8 * c + 4 + n, u, u_hi, u_lo, 4 * u, u == 0, u == 1,
                                  ROUND_FF + 6 * c + 2 + n)
            up(0, 1)
            down(0)
            with pe.Fori(1, CHUNKS) as c:
                with pe.Fori(0, 2) as b:
                    up(c, b)
                down(c)

        @block.scalar
        def _(act):
            def hi(t, b, m):
                act.wait_ge(sq_n, t + 1)
                nc.scalar.activation(tile(u_hi, 4 * b + m), squ[:, m % 2, :], ACT.Copy).then_inc(hi_n, 1)

            def up(c, b, first=False):
                for m in range(4):
                    t = 8 * c + 4 * b + m
                    await_bank(act, s, ROUND_FF + 6 * c + b, m, 2 * PAIR_FF + 16 * c + 4 * b + 3)
                    if not first or m >= 2:
                        act.wait_ge(sq_n, t - 1)
                    nc.scalar.activation(relu[:, m % 2, :], s.gb[m][:, :], ACT.Relu).then_inc(s.bank_free, 1)
                    if m >= 1:
                        hi(t - 1, b, m - 1)
                hi(8 * c + 4 * b + 3, b, 3)

            def splits(pair, units):
                for u in units:
                    split_hi(nc, act, s, pair + u // 2, u % 2)

            up(0, 0, True)
            splits(PAIR_FF + 2, range(1, 5))
            up(0, 1)
            with act.Fori(0, 4) as n:
                splits(PAIR_FF + 4 + n, (1, 2))
            with act.Fori(1, CHUNKS - 1) as c:
                with act.Fori(0, 2) as b:
                    splits(PAIR_FF + 8 * c + 2 * b, range(1, 5))
                    up(c, b)
                with act.Fori(0, 4) as n:
                    splits(PAIR_FF + 8 * c + 4 + n, (1, 2))
            with act.Fori(0, 2) as b:
                splits(PAIR_FF + 8 * (CHUNKS - 1) + 2 * b, range(1, 5))
                up(CHUNKS - 1, b)
            with act.Fori(0, 3) as n:
                splits(PAIR_FF + 8 * (CHUNKS - 1) + 4 + n, (1, 2))
            splits(PAIR_FF + 8 * (CHUNKS - 1) + 7, (1,))

        @block.vector
        def _(dve):
            def lo(t, b, m):
                dve.wait_ge(hi_n, t + 1)
                nc.vector.tensor_tensor(tile(u_lo, 4 * b + m), squ[:, m % 2, :], tile(u_hi, 4 * b + m).bitcast(F32),
                                        ALU.subtract).then_inc(lo_n, 1)

            def up(c, b, first=False):
                for m in range(4):
                    t = 8 * c + 4 * b + m
                    dve.wait_ge(s.bank_free, 4 * (ROUND_FF + 6 * c + b) + m + 1)
                    if not first or m >= 2:
                        dve.wait_ge(lo_n, t - 1)
                    nc.vector.tensor_tensor(squ[:, m % 2, :], relu[:, m % 2, :], relu[:, m % 2, :], ALU.mult).then_inc(sq_n, 1)
                    if m >= 1:
                        lo(t - 1, b, m - 1)
                lo(8 * c + 4 * b + 3, b, 3)

            def splits(pair, units):
                for u in units:
                    split_lo(nc, dve, s, pair + u // 2, u % 2)

            def gate(c, n, first=False):
                for m in range(TM):
                    e = 16 * c + 4 * n + m
                    await_bank(dve, s, ROUND_FF + 6 * c + 2 + n, m, 2 * PAIR_FF + 16 * c + 8 + 2 * n + 1)
                    if not first or m >= 2:
                        dve.wait_ge(added, e - 1)
                    nc.vector.tensor_tensor(gated[:, m % 2, :], s.gb[m][:, :], s.gate_bc[1][:, ds(n * 512, 512)],
                                            ALU.mult).then_inc(s.bank_free, 1)

            def down(c, n):
                splits(PAIR_FF + 8 * c + 4 + n, (1, 2))
                gate(c, n)

            up(0, 0, True)
            splits(PAIR_FF + 2, range(1, 5))
            up(0, 1)
            splits(PAIR_FF + 4, (1, 2))
            gate(0, 0, True)
            with dve.Fori(1, 4) as n:
                down(0, n)
            with dve.Fori(1, CHUNKS - 1) as c:
                with dve.Fori(0, 2) as b:
                    splits(PAIR_FF + 8 * c + 2 * b, range(1, 5))
                    up(c, b)
                with dve.Fori(0, 4) as n:
                    down(c, n)
            with dve.Fori(0, 2) as b:
                splits(PAIR_FF + 8 * (CHUNKS - 1) + 2 * b, range(1, 5))
                up(CHUNKS - 1, b)
            with dve.Fori(0, 3) as n:
                down(CHUNKS - 1, n)
            splits(PAIR_FF + 8 * (CHUNKS - 1) + 7, (1,))
            gate(CHUNKS - 1, 3)

        @block.gpsimd
        def _(pool):
            with pool.Fori(0, CHUNKS) as c:
                with pool.Fori(0, 4) as n:
                    for m in range(TM):
                        pool.wait_ge(s.bank_free, 4 * (ROUND_FF + 6 * c + 2 + n) + m + 1)
                        part = s.x2[:, m, ds(n * 512, 512)]
                        nc.gpsimd.tensor_tensor(part, part, gated[:, m % 2, :], ALU.add).then_inc(added, 1)


def build(nc, A):
    with ExitStack() as ctx:
        sb = lambda name, shape, dt=F32: ctx.enter_context(nc.sbuf_tensor(name, shape, dt))
        sem = lambda name: ctx.enter_context(nc.semaphore(name))
        s = Names()
        s.sem = sem
        s.act_hi, s.act_lo = sb("act_hi", [P, KT, T], F32R), sb("act_lo", [P, KT, T], F32R)
        s.w_raw = sb("w_raw", [P, 2, 4, 512])
        s.w_hi, s.w_lo = sb("w_hi", [P, 2, 4, 512], F32R), sb("w_lo", [P, 2, 4, 512], F32R)
        s.base = sb("base_consts", [P, C_END])
        s.ident = s.base[:, C_ID:C_ID + P]
        s.ones = sb("ones", [P, P])
        s.ident_bf, s.causal_bf = sb("ident_bf", [P, P], mybir.dt.bfloat16), sb("causal_bf", [P, P], mybir.dt.bfloat16)
        s.cols1, s.cols2 = sb("cols1", [P, P]), sb("cols2", [P, P])
        s.c_col = sb("c_col", [P, 4, KT])
        s.mod = sb("mod", [P, 6, KT])
        s.fq_gain = sb("fq_gain", [P, 1])
        s.gain_bc = sb("gain_bc", [P, 3, HD])
        s.decay, s.auxR = (sb(name, [ND, T], mybir.dt.bfloat16) for name in ("decay", "auxR"))
        s.decay_in = sem("decay_in")
        s.gates = sb("gates", [P, TM, NZ])
        s.kcT, s.vc = sb("kcT", [P, 64]), sb("vc", [64, HD])
        s.gb = [ctx.enter_context(nc.psum_tensor(f"gemm_bank{m}", [P, 512], F32)) for m in range(4)]
        s.mb = [ctx.enter_context(nc.psum_tensor(f"misc_bank{m}", [P, 512], F32)) for m in range(4)]
        s.w_landed = [sem(f"w_landed{i}") for i in range(2)]
        s.w_hi_ready, s.w_lo_ready, s.unit_used = sem("w_hi_ready"), sem("w_lo_ready"), sem("unit_used")
        s.bank_done, s.bank_free = sem("bank_done"), sem("bank_free")
        s.wz, s.wz_in = sb("narrow_columns", [P, 2 * 512]), sem("wz_in")
        s.gated = s.wz[:, :].rearrange("p (e n) -> p e n", e=2)
        s.ssq2 = sb("ssq2", [P, TM, 4])
        s.proj_stored = [sem(f"proj_stored{m}") for m in range(TM)]
        s.proj = nc.dram_tensor("proj", [NB_IN, TM, P, 512], F32).ap()

        phase_start(nc, A, s)
        with nc.sbuf_tensor("gate2_bc", [P, D], F32) as gate2:
            with nc.sbuf_tensor("gate1_bc", [P, D], F32) as gate1:
                s.gate_bc = [gate1, gate2]
                with ExitStack() as narrow:
                    s.wz_hi, s.wz_lo = (narrow.enter_context(nc.sbuf_tensor(name, [P, ZW], F32R)) for name in ("wz_hi", "wz_lo"))
                    s.ada_raw = narrow.enter_context(nc.sbuf_tensor("ada2_raw", [P, 2, D], F32))
                    s.proj_stats = narrow.enter_context(nc.sbuf_tensor("proj_stats", [P, 4, 16], F32))
                    s.stage = narrow.enter_context(nc.sbuf_tensor("proj_stage", [P, TM, 512], F32))
                    with nc.sbuf_tensor("ada2_acc", [P, 4, D], F32) as acc:
                        s.ada_acc = acc
                    s.xb = narrow.enter_context(nc.sbuf_tensor("xb", [P, XW], F32))
                    s.xb_hi, s.xb_lo = (narrow.enter_context(nc.sbuf_tensor(name, [P, XW], F32R)) for name in ("xb_hi", "xb_lo"))
                    s.kcv = s.ada_raw[:, 0, :].rearrange("p (m n) -> p m n", m=TM)
                    s.kcvT = s.ada_raw[:, 1, :].rearrange("p (e t) -> p e t", e=4)
                    s.z_sums, s.keys_turned, s.keys_read = sem("z_sums"), sem("kcv_turned"), sem("kcv_read")
                    s.x_ready, s.xh, s.xl = sem("xb_ready"), sem("xb_hi_ready"), sem("xb_lo_ready")
                    phase_project(nc, A, s)
                    phase_compress(nc, A, s)
                with ExitStack() as sparse:
                    s.sparse, s.key_read = sparse_state(sparse, nc, s), sem("nsa_key_read")
                    phase_fox(nc, A, s)
                    phase_nsa(nc, A, s)
                with nc.sbuf_tensor("x2", [P, TM, D], F32) as x2:
                    s.x2 = x2
                    phase_out(nc, A, s)
                    phase_norm2(nc, A, s)
                    phase_mlp(nc, A, s)


INPUTS = ["x", "c", "w_ada", "b_ada", "norm1_g", "w_in", "b_forget", "fox_q_norm", "fox_k_norm", "nsa_q_norm",
          "cmp_k_norm", "slc_k_norm", "win_k_norm", "cmp_pe_k", "cmp_w1_k", "cmp_w2_k", "cmp_pe_v", "cmp_w1_v",
          "cmp_w2_v", "w_out", "norm2_g", "w_up", "w_down"]


def kernel(**inputs):
    import concourse.bacc as _bacc
    from concourse.bass_utils import run_bass_kernel_spmd as _run

    nc = _bacc.Bacc("TRN2", target_bir_lowering=False, num_devices=1)
    base, nsa_tabs = host_constants()
    arrays = {name: np.ascontiguousarray(inputs[name]) for name in INPUTS}
    arrays["base"], arrays["nsa_tabs"] = base, nsa_tabs
    fields = {name: nc.dram_tensor("in_" + name, a.shape, mybir.dt.from_np(a.dtype), kind="ExternalInput").ap()
              for name, a in arrays.items()}
    fields["out"] = nc.dram_tensor("out", (1, T, D), F32, kind="ExternalOutput").ap()
    A = namedtuple("Arrays", fields)(**fields)
    build(nc, A)
    r = _run(nc, [{"in_" + name: a for name, a in arrays.items()}], core_ids=[0])
    return r.results[0]["out"]
```
